# Optimizing a Trainium2 kernel written in Bass

```python
import jax, jax.numpy as jnp
from jax import lax
import numpy as np
import math

D_MODEL = 1024
BATCH = 1
SEQ = 512
DEPTH = 1

MEM_LEN = 256
HEAD_DIM = 64
POOL_WINDOWS = (2, 4, 8, 16)
POOL_GROUPS = len(POOL_WINDOWS)
POOL_WIDTH = D_MODEL // 4
POOL_CH = POOL_WIDTH // POOL_GROUPS
SB_WIDTH = D_MODEL // 2
SB_HEADS = SB_WIDTH // HEAD_DIM
MEM_HEADS = 4
MEM_WIDTH = D_MODEL // 4
MEM_HEAD_DIM = MEM_WIDTH // MEM_HEADS
MIX_WIDTH = POOL_WIDTH + SB_WIDTH + MEM_WIDTH
IN_SPLITS = (POOL_WIDTH, POOL_WIDTH, SB_WIDTH, SB_WIDTH, SB_WIDTH, SB_WIDTH, MEM_WIDTH, MEM_WIDTH)
IN_WIDTH = sum(IN_SPLITS)
Q_BLOCK = 128
EPS = 1e-6


def rmsnorm(x, g):
    xf = x.astype(jnp.float32)
    y = xf * lax.rsqrt(jnp.mean(xf * xf, axis=-1, keepdims=True) + EPS)
    return (y * g.astype(jnp.float32)).astype(x.dtype)

def pool_mixer(u, pool_w, pool_scale):
    B, S, _ = u.shape
    uf = u.astype(jnp.float32).reshape(B, S, POOL_GROUPS, POOL_CH)
    csum = jnp.concatenate([jnp.zeros_like(uf[:, :1]), jnp.cumsum(uf, axis=1)], axis=1)
    t = jnp.arange(S)
    means = []
    for g, w in enumerate(POOL_WINDOWS):
        lo = jnp.maximum(t + 1 - w, 0)
        win_sum = csum[:, 1:, g] - csum[:, lo, g]
        count = (t + 1 - lo).astype(jnp.float32)
        means.append(win_sum / count[None, :, None])
    pooled = (jnp.stack(means, axis=2) - uf).astype(u.dtype)
    y = jnp.einsum('bsgc,gcd->bsgd', pooled, pool_w)
    return y.reshape(B, S, POOL_WIDTH) * pool_scale

def stick_breaking_attention(q, k, v):
    B, S, H, Dh = q.shape
    scale = Dh ** -0.5
    outs = []
    for i in range(S // Q_BLOCK):
        q0 = i * Q_BLOCK
        kv_len = q0 + Q_BLOCK
        qb = q[:, q0:kv_len]
        kb = k[:, :kv_len]
        vb = v[:, :kv_len]
        z = jnp.einsum('bqhd,bkhd->bhqk', qb, kb).astype(jnp.float32) * scale
        t_idx = q0 + jnp.arange(Q_BLOCK)
        s_idx = jnp.arange(kv_len)
        mask = s_idx[None, :] < t_idx[:, None]
        log_beta = jax.nn.log_sigmoid(z)
        log_1m_beta = jnp.where(mask, jax.nn.log_sigmoid(-z), 0.0)
        cum = jnp.cumsum(log_1m_beta, axis=-1)
        log_a = log_beta + cum[..., -1:] - cum
        a = jnp.where(mask, jnp.exp(log_a), 0.0)
        outs.append(jnp.einsum('bhqk,bkhd->bqhd', a.astype(v.dtype), vb))
    return jnp.concatenate(outs, axis=1)

def memory_attention(q, mem_k, mem_v, q_norm_g, k_norm_g):
    q = rmsnorm(q, q_norm_g)
    mem_k = rmsnorm(mem_k, k_norm_g)
    s = jnp.einsum('bqhd,bmhd->bhqm', q, mem_k).astype(jnp.float32) * (q.shape[-1] ** -0.5)
    p = jax.nn.softmax(s, axis=-1)
    return jnp.einsum('bhqm,bmhd->bqhd', p.astype(mem_v.dtype), mem_v)

def first_inputs(seed: int = 0) -> dict:
    key = jax.random.key(seed)
    ks = jax.random.split(key, 12)
    f32 = jnp.float32
    x = jax.random.normal(ks[0], (BATCH, SEQ, D_MODEL), f32)
    mem = jax.random.normal(ks[1], (BATCH, MEM_LEN, D_MODEL), f32)
    norm_g = 1.0 + 0.02 * jax.random.normal(ks[2], (DEPTH, D_MODEL), f32)
    w_in = jax.random.normal(ks[3], (DEPTH, D_MODEL, IN_WIDTH), f32) * D_MODEL ** -0.5
    pool_w = jax.random.normal(ks[4], (DEPTH, POOL_GROUPS, POOL_CH, POOL_CH), f32) * POOL_CH ** -0.5
    pool_scale = 1.0 + 0.1 * jax.random.normal(ks[5], (DEPTH, POOL_WIDTH), f32)
    mem_norm_g = 1.0 + 0.02 * jax.random.normal(ks[6], (DEPTH, D_MODEL), f32)
    w_mem_kv = jax.random.normal(ks[7], (DEPTH, D_MODEL, 2 * MEM_WIDTH), f32) * D_MODEL ** -0.5
    q_norm_g = 1.0 + 0.02 * jax.random.normal(ks[8], (DEPTH, MEM_HEAD_DIM), f32)
    k_norm_g = 1.0 + 0.02 * jax.random.normal(ks[9], (DEPTH, MEM_HEAD_DIM), f32)
    w_out = jax.random.normal(ks[10], (DEPTH, MIX_WIDTH, D_MODEL), f32) * MIX_WIDTH ** -0.5
    return {"x": x, "mem": mem, "norm_g": norm_g, "w_in": w_in, "pool_w": pool_w,
            "pool_scale": pool_scale, "mem_norm_g": mem_norm_g, "w_mem_kv": w_mem_kv,
            "q_norm_g": q_norm_g, "k_norm_g": k_norm_g, "w_out": w_out}

def first_block(x, mem, norm_g, w_in, pool_w, pool_scale, mem_norm_g, w_mem_kv, q_norm_g, k_norm_g, w_out):
    B, S, _ = x.shape
    M = mem.shape[1]
    split_points = list(np.cumsum(IN_SPLITS)[:-1])
    for l in range(DEPTH):
        h = rmsnorm(x, norm_g[l])
        proj = jnp.einsum('bsd,de->bse', h, w_in[l])
        (pool_v, pool_gate, sb_q, sb_k, sb_v, sb_gate,
         mem_q, mem_gate) = jnp.split(proj, split_points, axis=-1)

        y_pool = pool_mixer(pool_v, pool_w[l], pool_scale[l]) * jax.nn.silu(pool_gate)

        heads = lambda t: t.reshape(B, S, SB_HEADS, HEAD_DIM)
        y_sb = stick_breaking_attention(heads(sb_q), heads(sb_k), heads(sb_v)).reshape(B, S, SB_WIDTH)
        y_sb = y_sb * jax.nn.silu(sb_gate)

        mkv = jnp.einsum('bmd,de->bme', rmsnorm(mem, mem_norm_g[l]), w_mem_kv[l])
        mem_k, mem_v = jnp.split(mkv, 2, axis=-1)
        mem_k = mem_k.reshape(B, M, MEM_HEADS, MEM_HEAD_DIM)
        mem_v = mem_v.reshape(B, M, MEM_HEADS, MEM_HEAD_DIM)
        y_mem = memory_attention(mem_q.reshape(B, S, MEM_HEADS, MEM_HEAD_DIM), mem_k, mem_v,
                                 q_norm_g[l], k_norm_g[l]).reshape(B, S, MEM_WIDTH)
        y_mem = y_mem * jax.nn.silu(mem_gate)

        mixed = jnp.concatenate([y_pool, y_sb, y_mem], axis=-1)
        x = x + jnp.einsum('bse,ed->bsd', mixed, w_out[l])
    return x


DEPTH_2 = 2

GRID_W = 64
CHUNK = 128
MIX_WIDTH_2 = D_MODEL
RET_HEADS = 8
RET_DH = (MIX_WIDTH_2 // 2) // RET_HEADS
RET_WIDTH = RET_HEADS * RET_DH
ROPE_BASE = 10000.0
NA_HEADS = 8
NA_DH = (MIX_WIDTH_2 // 2) // NA_HEADS
NA_WIDTH = NA_HEADS * NA_DH
NA_WIN_R = 8
NA_WIN_C = 16
NA_QBLK = 16
AB_IN_DIM = 4 * RET_WIDTH + 3 * NA_WIDTH
SSD_INNER = 2 * D_MODEL
SSD_HEADDIM = 64
SSD_HEADS = SSD_INNER // SSD_HEADDIM
SSD_GROUPS = 4
SSD_HPG = SSD_HEADS // SSD_GROUPS
SSD_STATE = 128
SSD_CONV = 5
SSD_XBC = SSD_INNER + 2 * SSD_GROUPS * SSD_STATE
SSD_IN_DIM = SSD_INNER + SSD_XBC + 2 * SSD_HEADS
FFN_DIM = 2816
FFN_CONV = 3
N_EVEN = (DEPTH_2 + 1) // 2
N_ODD = DEPTH_2 // 2


def rms_norm(x, g):
    xf = x.astype(jnp.float32)
    y = xf * lax.rsqrt(jnp.mean(xf * xf, axis=-1, keepdims=True) + EPS)
    return (y * g.astype(jnp.float32)).astype(x.dtype)

def depthwise_conv_centered(x, w, b):
    width, ch = w.shape
    pad = width // 2
    y = lax.conv_general_dilated(x, w[:, None, :].astype(x.dtype), window_strides=(1,),
                                 padding=[(pad, pad)], dimension_numbers=('NWC', 'WIO', 'NWC'),
                                 feature_group_count=ch)
    return y + b.astype(x.dtype)

def rotary(x, pos):
    half = x.shape[-1] // 2
    inv = 1.0 / (ROPE_BASE ** (jnp.arange(half, dtype=jnp.float32) / half))
    ang = pos.astype(jnp.float32)[:, None] * inv[None, :]
    cos = jnp.cos(ang)[None, :, None, :]
    sin = jnp.sin(ang)[None, :, None, :]
    xf = x.astype(jnp.float32)
    x1, x2 = xf[..., :half], xf[..., half:]
    return jnp.concatenate([x1 * cos - x2 * sin, x1 * sin + x2 * cos], axis=-1).astype(x.dtype)

def chunked_scan(q, k, v, log_a, include_diag):
    f32 = jnp.float32
    bsz, s, g, n = q.shape
    hg, p = v.shape[3], v.shape[4]
    n_chunks = s // CHUNK

    def to_chunks(t):
        return jnp.moveaxis(t.astype(f32).reshape(bsz, n_chunks, CHUNK, *t.shape[2:]), 1, 0)

    qc, kc, vc, ac = to_chunks(q), to_chunks(k), to_chunks(v), to_chunks(log_a)
    idx = jnp.arange(CHUNK)
    mask = (idx[:, None] >= idx[None, :]) if include_diag else (idx[:, None] > idx[None, :])

    def step(h, inp):
        qq, kk, vv, aa = inp
        cs = jnp.cumsum(aa, axis=1)
        seg = cs[:, :, None] - cs[:, None, :]
        decay = jnp.exp(jnp.where(mask[None, :, :, None, None], seg, -jnp.inf))
        qk = jnp.einsum('bjgn,blgn->bjlg', qq, kk)
        y_intra = jnp.einsum('bjlgh,blghp->bjghp', qk[..., None] * decay, vv)
        y_inter = jnp.einsum('bjgn,bghnp->bjghp', qq, h) * jnp.exp(cs)[..., None]
        tail = jnp.exp(cs[:, -1:] - cs)
        h_new = h * jnp.exp(cs[:, -1])[..., None, None] + jnp.einsum('blgn,blghp->bghnp', kk, vv * tail[..., None])
        return h_new, y_intra + y_inter

    h0 = jnp.zeros((bsz, g, hg, n, p), f32)
    _, ys = lax.scan(step, h0, (qc, kc, vc, ac))
    return jnp.moveaxis(ys, 0, 1).reshape(bsz, s, g, hg, p)

def bidir_scan(q, k, v_f, v_b, a_f, a_b):
    y_f = chunked_scan(q, k, v_f, a_f, True)
    flip = lambda t: jnp.flip(t, axis=1)
    y_b = flip(chunked_scan(flip(q), flip(k), flip(v_b), flip(a_b), False))
    return y_f + y_b

def neighborhood_attention(q, k, v, rpb):
    f32 = jnp.float32
    bsz, s, h, dh = q.shape
    rows = s // GRID_W
    win_r = min(NA_WIN_R, rows)
    n_cb = GRID_W // NA_QBLK
    span = NA_QBLK + NA_WIN_C
    qb_all = (q.astype(f32) * dh ** -0.5).reshape(bsz, rows, n_cb, NA_QBLK, h, dh)
    qb_all = jnp.moveaxis(qb_all, 2, 0)
    k = k.reshape(bsz, rows, GRID_W, h, dh)
    v = v.reshape(bsz, rows, GRID_W, h, dh)
    r = jnp.arange(rows)
    key_rows = jnp.clip(r - win_r // 2, 0, rows - win_r)[:, None] + jnp.arange(win_r)[None, :]
    dr = key_rows - r[:, None] + (NA_WIN_R - 1)
    c0s = jnp.arange(n_cb) * NA_QBLK

    def block(args):
        qb, c0 = args
        qcols = c0 + jnp.arange(NA_QBLK)
        kcols = jnp.clip(c0 - NA_WIN_C // 2, 0, GRID_W - span) + jnp.arange(span)
        cstart = jnp.clip(qcols - NA_WIN_C // 2, 0, GRID_W - NA_WIN_C)
        valid = (kcols[None, :] >= cstart[:, None]) & (kcols[None, :] < cstart[:, None] + NA_WIN_C)
        dc = jnp.clip(kcols[None, :] - qcols[:, None], -(NA_WIN_C - 1), NA_WIN_C - 1) + (NA_WIN_C - 1)
        kb = k[:, key_rows[:, :, None], kcols[None, None, :]].astype(f32)
        vb = v[:, key_rows[:, :, None], kcols[None, None, :]].astype(f32)
        bias = rpb[:, dr[:, None, :, None], dc[None, :, None, :]].astype(f32)
        sc = jnp.einsum('brqhd,brwchd->bhrqwc', qb, kb) + bias[None]
        sc = jnp.where(valid[:, None, :], sc, -jnp.inf)
        pr = jax.nn.softmax(sc.reshape(*sc.shape[:4], -1), axis=-1).reshape(sc.shape)
        return jnp.einsum('bhrqwc,brwchd->brqhd', pr, vb)

    out = lax.map(block, (qb_all, c0s))
    return jnp.moveaxis(out, 0, 2).reshape(bsz, s, h * dh)

def retention_na_mixer(hn, w_in, ret_decay_logit, ret_gn_g, na_rpb, w_out):
    f32 = jnp.float32
    bsz, s, _ = hn.shape
    proj = hn @ w_in
    R, N = RET_WIDTH, NA_WIDTH
    rq, rk, rv, rg, nq, nk, nv = jnp.split(proj, [R, 2 * R, 3 * R, 4 * R, 4 * R + N, 4 * R + 2 * N], axis=-1)
    pos = jnp.arange(s)
    rshape = (bsz, s, RET_HEADS, RET_DH)
    rq = rotary(rq.reshape(rshape), pos)
    rk = rotary(rk.reshape(rshape), pos) * (RET_DH ** -0.5)
    rv = rv.reshape(bsz, s, RET_HEADS, 1, RET_DH)
    log_gamma = -jax.nn.softplus(-ret_decay_logit.astype(f32))
    a_f = jnp.broadcast_to(log_gamma[0][None, None, :, None], (bsz, s, RET_HEADS, 1))
    a_b = jnp.broadcast_to(log_gamma[1][None, None, :, None], (bsz, s, RET_HEADS, 1))
    y = bidir_scan(rq, rk, rv, rv, a_f, a_b).reshape(rshape)
    mu = jnp.mean(y, axis=-1, keepdims=True)
    var = jnp.mean(jnp.square(y - mu), axis=-1, keepdims=True)
    y = ((y - mu) * lax.rsqrt(var + EPS)).reshape(bsz, s, RET_WIDTH) * ret_gn_g.astype(f32)
    ret_out = (jax.nn.silu(rg.astype(f32)) * y).astype(hn.dtype)
    nshape = (bsz, s, NA_HEADS, NA_DH)
    na_out = neighborhood_attention(nq.reshape(nshape), nk.reshape(nshape), nv.reshape(nshape), na_rpb).astype(hn.dtype)
    return jnp.concatenate([ret_out, na_out], axis=-1) @ w_out

def ssd_mixer(hn, w_in, conv_w, conv_b, dt_bias, a_log, d_skip, norm_g, w_out):
    f32 = jnp.float32
    bsz, s, _ = hn.shape
    proj = hn @ w_in
    z, xbc, dt_raw = jnp.split(proj, [SSD_INNER, SSD_INNER + SSD_XBC], axis=-1)
    xbc = jax.nn.silu(depthwise_conv_centered(xbc, conv_w, conv_b))
    xs, bm, cm = jnp.split(xbc, [SSD_INNER, SSD_INNER + SSD_GROUPS * SSD_STATE], axis=-1)
    dt = jax.nn.softplus(dt_raw.astype(f32).reshape(bsz, s, 2, SSD_HEADS) + dt_bias.astype(f32))
    A = -jnp.exp(a_log.astype(f32))
    log_a = dt * A
    grp = (bsz, s, SSD_GROUPS, SSD_HPG)
    xh = xs.astype(f32).reshape(bsz, s, SSD_GROUPS, SSD_HPG, SSD_HEADDIM)
    v_f = xh * dt[:, :, 0].reshape(grp)[..., None]
    v_b = xh * dt[:, :, 1].reshape(grp)[..., None]
    qc = cm.reshape(bsz, s, SSD_GROUPS, SSD_STATE)
    kb = bm.reshape(bsz, s, SSD_GROUPS, SSD_STATE)
    y = bidir_scan(qc, kb, v_f, v_b, log_a[:, :, 0].reshape(grp), log_a[:, :, 1].reshape(grp))
    y = y + xh * d_skip.astype(f32).reshape(SSD_GROUPS, SSD_HPG)[..., None]
    y = y.reshape(bsz, s, SSD_INNER) * jax.nn.silu(z.astype(f32))
    yg = y.reshape(bsz, s, SSD_GROUPS, SSD_INNER // SSD_GROUPS)
    yg = yg * lax.rsqrt(jnp.mean(yg * yg, axis=-1, keepdims=True) + EPS)
    y = yg.reshape(bsz, s, SSD_INNER) * norm_g.astype(f32)
    return y.astype(hn.dtype) @ w_out

def conv_geglu_ffn(hn, w_up, conv_w, conv_b, w_down):
    u = depthwise_conv_centered(hn @ w_up, conv_w, conv_b)
    gate, val = jnp.split(u, 2, axis=-1)
    return (jax.nn.gelu(gate, approximate=True) * val) @ w_down

def second_inputs(seed: int = 0) -> dict:
    key = jax.random.key(seed)
    ks = jax.random.split(key, 24)
    f32 = jnp.float32

    def nrm(k, shape, scale):
        return jax.random.normal(k, shape, f32) * scale

    def gain(k, shape):
        return 1.0 + 0.05 * jax.random.normal(k, shape, f32)

    x = nrm(ks[0], (BATCH, SEQ, D_MODEL), 1.0)
    norm_mix_pre = gain(ks[1], (DEPTH_2, D_MODEL))
    norm_mix_post = gain(ks[2], (DEPTH_2, D_MODEL))
    norm_ffn_pre = gain(ks[3], (DEPTH_2, D_MODEL))
    norm_ffn_post = gain(ks[4], (DEPTH_2, D_MODEL))
    ab_w_in = nrm(ks[5], (N_EVEN, D_MODEL, AB_IN_DIM), D_MODEL ** -0.5)
    gamma0 = 1.0 - 2.0 ** (-5.0 - jnp.arange(RET_HEADS, dtype=f32))
    ab_ret_decay_logit = (jnp.log(gamma0) - jnp.log1p(-gamma0))[None, None, :] + nrm(ks[6], (N_EVEN, 2, RET_HEADS), 0.05)
    ab_ret_gn_g = gain(ks[7], (N_EVEN, RET_WIDTH))
    ab_na_rpb = nrm(ks[8], (N_EVEN, NA_HEADS, 2 * NA_WIN_R - 1, 2 * NA_WIN_C - 1), 0.1)
    ab_w_out = nrm(ks[9], (N_EVEN, RET_WIDTH + NA_WIDTH, D_MODEL), (RET_WIDTH + NA_WIDTH) ** -0.5)
    c_w_in = nrm(ks[10], (N_ODD, D_MODEL, SSD_IN_DIM), D_MODEL ** -0.5)
    c_conv_w = nrm(ks[11], (N_ODD, SSD_CONV, SSD_XBC), SSD_CONV ** -0.5)
    c_conv_b = nrm(ks[12], (N_ODD, SSD_XBC), 0.02)
    dt0 = jnp.exp(jax.random.uniform(ks[13], (N_ODD, 2, SSD_HEADS), f32, math.log(1e-3), math.log(1e-1)))
    c_dt_bias = dt0 + jnp.log(-jnp.expm1(-dt0))
    c_a_log = jnp.log(jax.random.uniform(ks[14], (N_ODD, 2, SSD_HEADS), f32, 1.0, 16.0))
    c_d_skip = 1.0 + 0.1 * jax.random.normal(ks[15], (N_ODD, SSD_HEADS), f32)
    c_norm_g = gain(ks[16], (N_ODD, SSD_INNER))
    c_w_out = nrm(ks[17], (N_ODD, SSD_INNER, D_MODEL), SSD_INNER ** -0.5)
    ffn_w_up = nrm(ks[18], (DEPTH_2, D_MODEL, 2 * FFN_DIM), D_MODEL ** -0.5)
    ffn_conv_w = nrm(ks[19], (DEPTH_2, FFN_CONV, 2 * FFN_DIM), FFN_CONV ** -0.5)
    ffn_conv_b = nrm(ks[20], (DEPTH_2, 2 * FFN_DIM), 0.02)
    ffn_w_down = nrm(ks[21], (DEPTH_2, FFN_DIM, D_MODEL), FFN_DIM ** -0.5)
    return {'x': x, 'norm_mix_pre': norm_mix_pre, 'norm_mix_post': norm_mix_post,
            'norm_ffn_pre': norm_ffn_pre, 'norm_ffn_post': norm_ffn_post,
            'ab_w_in': ab_w_in, 'ab_ret_decay_logit': ab_ret_decay_logit, 'ab_ret_gn_g': ab_ret_gn_g,
            'ab_na_rpb': ab_na_rpb, 'ab_w_out': ab_w_out,
            'c_w_in': c_w_in, 'c_conv_w': c_conv_w, 'c_conv_b': c_conv_b, 'c_dt_bias': c_dt_bias,
            'c_a_log': c_a_log, 'c_d_skip': c_d_skip, 'c_norm_g': c_norm_g, 'c_w_out': c_w_out,
            'ffn_w_up': ffn_w_up, 'ffn_conv_w': ffn_conv_w, 'ffn_conv_b': ffn_conv_b, 'ffn_w_down': ffn_w_down}

def second_block(x, norm_mix_pre, norm_mix_post, norm_ffn_pre, norm_ffn_post,
              ab_w_in, ab_ret_decay_logit, ab_ret_gn_g, ab_na_rpb, ab_w_out,
              c_w_in, c_conv_w, c_conv_b, c_dt_bias, c_a_log, c_d_skip, c_norm_g, c_w_out,
              ffn_w_up, ffn_conv_w, ffn_conv_b, ffn_w_down):
    for layer in range(DEPTH_2):
        i = layer // 2
        hn = rms_norm(x, norm_mix_pre[layer])
        if layer % 2 == 0:
            m = retention_na_mixer(hn, ab_w_in[i], ab_ret_decay_logit[i], ab_ret_gn_g[i], ab_na_rpb[i], ab_w_out[i])
        else:
            m = ssd_mixer(hn, c_w_in[i], c_conv_w[i], c_conv_b[i], c_dt_bias[i], c_a_log[i],
                          c_d_skip[i], c_norm_g[i], c_w_out[i])
        x = x + rms_norm(m, norm_mix_post[layer])
        f = conv_geglu_ffn(rms_norm(x, norm_ffn_pre[layer]), ffn_w_up[layer], ffn_conv_w[layer],
                           ffn_conv_b[layer], ffn_w_down[layer])
        x = x + rms_norm(f, norm_ffn_post[layer])
    return x


def setup_inputs(seed=0):
    out = dict(first_inputs(seed))
    for name, value in second_inputs(seed + 1).items():
        if name != "x":
            out[name + "_2"] = value
    return out


def reference(
    x, mem, norm_g, w_in, pool_w, pool_scale, mem_norm_g, w_mem_kv, q_norm_g, k_norm_g, w_out,
    norm_mix_pre_2, norm_mix_post_2, norm_ffn_pre_2, norm_ffn_post_2, ab_w_in_2,
    ab_ret_decay_logit_2, ab_ret_gn_g_2, ab_na_rpb_2, ab_w_out_2, c_w_in_2, c_conv_w_2,
    c_conv_b_2, c_dt_bias_2, c_a_log_2, c_d_skip_2, c_norm_g_2, c_w_out_2, ffn_w_up_2,
    ffn_conv_w_2, ffn_conv_b_2, ffn_w_down_2,
):
    x = first_block(
        x, mem, norm_g, w_in, pool_w, pool_scale, mem_norm_g, w_mem_kv, q_norm_g, k_norm_g,
        w_out,
    )
    return second_block(
        x, norm_mix_pre_2, norm_mix_post_2, norm_ffn_pre_2, norm_ffn_post_2, ab_w_in_2,
        ab_ret_decay_logit_2, ab_ret_gn_g_2, ab_na_rpb_2, ab_w_out_2, c_w_in_2, c_conv_w_2,
        c_conv_b_2, c_dt_bias_2, c_a_log_2, c_d_skip_2, c_norm_g_2, c_w_out_2, ffn_w_up_2,
        ffn_conv_w_2, ffn_conv_b_2, ffn_w_down_2,
    )


_drawn_inputs = setup_inputs


def setup_inputs(seed=0):
    import zlib

    import numpy as np

    out = dict(_drawn_inputs(seed))
    spreads = {}
    factors = {'mem_norm_g': 8.0,
     'q_norm_g': 8.0,
     'k_norm_g': 8.0,
     'c_conv_b_2': 3.368,
     'pool_scale': 3.79,
     'ab_ret_gn_g_2': 8.632,
     'ab_na_rpb_2': 17.186,
     'c_d_skip_2': 3.177,
     'c_norm_g_2': 11.496,
     'ffn_conv_b_2': 4.068}
    for name, (base, spread) in spreads.items():
        noise = np.random.default_rng([zlib.crc32(name.encode()), seed]).standard_normal(out[name].shape)
        drawn = base * np.exp(spread * noise) if base else spread * noise
        out[name] = __import__('jax').numpy.asarray(drawn.astype(out[name].dtype))
    for name, factor in factors.items():
        out[name] = (out[name] * factor).astype(out[name].dtype)
    return out
```

```python
import numpy as np
from contextlib import ExitStack

import concourse.bass as bass
from concourse import mybir

ACT = mybir.ActivationFunctionType
ALU = mybir.AluOpType
AX = mybir.AxisListType
F32 = mybir.dt.float32
F32R = mybir.dt.float32r

P = 128
D = 1024
S = 512
KT = D // P
TT = S // P
EPS = 1e-6
LOGEXP = "natural_log_exp_and_others"

MEM = 256
DH = 64
SB_HEADS = 8
MEM_HEADS = 4
IN1_TILES = 24
POOL_V, POOL_G, SB_Q, SB_K, SB_V, SB_G, MEM_Q, MEM_G = 0, 2, 4, 8, 12, 16, 20, 22

WEIGHTS = [
    ("mem_kv", 4, [8]),
    ("in1", IN1_TILES, [8]),
    ("out1", 8, [8]),
    ("in2", 28, [8]),
    ("out2", 8, [8]),
    ("up0", 44, [8]),
    ("down0", 8, [8, 8, 6]),
    ("z", 16, [8]),
    ("xbc", 24, [8]),
    ("out3", 8, [8, 8]),
    ("up1", 44, [8]),
    ("down1", 8, [8, 8, 6]),
]
RING = 4


def stream_plan():
    slot, tile, plan = 0, 0, {}
    for name, tiles, blocks in WEIGHTS:
        plan[name] = dict(tiles=tiles, blocks=blocks, slot0=slot, tile0=tile, last=name == WEIGHTS[-1][0])
        slot += tiles * len(blocks)
        tile += tiles
    return plan


PLAN = stream_plan()

PARAMS = [("norm_g", 8), ("mem_norm_g", 8), ("pool_scale", 2), ("q_norm_g", 1), ("k_norm_g", 1),
          ("mix_pre0", 8), ("mix_post0", 8), ("ffn_pre0", 8), ("ffn_post0", 8), ("ret_gn_g", 4), ("decay", 16),
          ("ffn_w0", 132), ("ffn_b0", 44),
          ("mix_pre1", 8), ("mix_post1", 8), ("ffn_pre1", 8), ("ffn_post1", 8), ("ffn_w1", 132), ("ffn_b1", 44),
          ("conv_w", 120), ("conv_b", 24), ("d_skip", 16), ("ssd_g", 16), ("dt_bias", 64), ("a_log", 64)]
PCOL = {}
for _name, _n in PARAMS:
    PCOL[_name] = sum(n for _, n in PARAMS[:len(PCOL)])
NPAR = sum(n for _, n in PARAMS)

RH = NH = 8
GRID_W = 64
ROWS = S // GRID_W
QB, WIN_C = 16, 16
KEYW = QB + WIN_C
RET_Q, RET_K, RET_V, RET_G, NA_Q, NA_K, NA_V = 0, 4, 8, 12, 16, 20, 24
STRIP = 2 * S - P
RPB_W = 64
BIAS_RUN = (ROWS - 1) * RPB_W + KEYW + QB
NEG = -1e30
X_UPDATES = 4
FFN = 2816
FT = FFN // P

SG, HPG, HD, NS = 4, 8, 64, 128
SH = SG * HPG
XS_TILES = SH * HD // P
B_TILE, C_TILE = XS_TILES, XS_TILES + SG
GW = HPG * HD
SSD_CONSTS = ["gt", "lt", "le", "ge"]

CONSTS = ["ident", "ones", "ones64", "neg_tri", "neg_ones", "swap"]
KB = 1024


def program(nc, dr):
    ctx = ExitStack()
    with ctx:
        start = -(-nc.sbuf_base // 32) * 32
        ctx.enter_context(nc.sbuf_tensor("slab", [P, 207 * 256], F32))
        build(nc, dr, ctx, start)


def build(nc, dr, ctx, start):
    sems = {}

    def sem(name):
        if name not in sems:
            sems[name] = ctx.enter_context(nc.semaphore(name))
        return sems[name]

    def at(name, shape, kb, dt=F32):
        return nc.alloc_sbuf_tensor_at(name, shape, dt, offset=start + int(kb * KB))

    x = at("x", [P, KT, S], 0)
    raw = at("raw", [P, RING, 8 * P], 16)
    w_hi = at("w_hi", [P, RING, 8 * P], 32, F32R)
    w_lo = at("w_lo", [P, RING, 8 * P], 48, F32R)
    a_hi = at("a_hi", [P, KT, S], 64, F32R)
    a_lo = at("a_lo", [P, KT, S], 80, F32R)
    cst = at("cst", [P, len(CONSTS), P], 96)
    par = at("par", [P, NPAR], 99)
    C = {n: cst[:, i, :] for i, n in enumerate(CONSTS)}

    def pcol(name, k=0):
        return par[:, PCOL[name] + k:PCOL[name] + k + 1]

    ST = 104
    p2 = at("p2", [P, 28, S], ST)
    vt2 = at("vt2", [P, TT, RH * DH], ST + 56)
    aw2 = at("aw2", [P, 2, TT, S], ST + 64)
    strip = at("strip", [P, 2, STRIP], ST + 80)
    dist = at("dist", [P, STRIP], ST + 87)
    rope = at("rope", [P, 2, S], ST + 90.5)
    rtmp = at("rtmp", [P, 2, S], ST + 94.5)
    dec = at("dec", [P, 5, 16], ST + 98.5)
    gsq = at("gsq", [P, 2, S], ST + 64)
    grs = at("grs", [P, 2, S], ST + 68)
    gtmp = at("gtmp", [P, 2, S], ST + 72)
    vna = at("vna", [P, 4, 2, NH * DH], ST + 64)
    bt = at("bt", [P, 2, ROWS, RPB_W], ST + 80)
    bm = at("bm", [P, 2, 4, ROWS, KEYW], ST + 84)
    cmask = at("cmask", [P, 4, KEYW], ST + 92)
    nprob = at("nprob", [P, 2, 2, ROWS * KEYW], ST + 92.5)
    npt = at("npt", [P, 2, 4, P], ST + 96.5)
    nstat = at("nstat", [P, 4, 32], ST + 100.5)
    nvw = at("nvw", [P, 4, 4, ROWS * KEYW], ST + 8)
    m_mix = at("m_mix", [P, KT, S], ST)
    zt = at("zt", [P, XS_TILES, S], ST)
    xbc = at("xbc", [P, 24, S], ST + 32)
    tri = at("tri", [P, 4, P], ST + 80)
    da = at("da", [P, TT, 2, SH], ST + 82)
    dtv = at("dtv", [P, TT, 2, SH], ST + 83)
    dtt = at("dtt", [P, TT, 2, SH], ST + 84)
    cume = at("cume", [P, TT, 2, SH], ST + 85)
    tote = at("tote", [P, TT, 2, SH], ST + 86)
    wdt = at("wdt", [P, KT, 2 * SH], ST + 87)
    wdt_hi = at("wdt_hi", [P, KT, 2 * SH], ST + 89, F32R)
    wdt_lo = at("wdt_lo", [P, KT, 2 * SH], ST + 91, F32R)
    vfb = at("vfb", [P, 2, GW], ST + 87)
    gmask = at("gmask", [P, 2, 2, P], ST + 91)
    btok = at("btok", [P, TT, NS], ST + 93)
    xtok = at("xtok", [P, TT, GW], ST + 95)
    cv = at("cv", [P, 4, S], ST + 95)
    dtmp = at("dtmp", [P, 4, TT * 2 * SH], ST + 95)
    hst = at("hst", [P, 2, 3, GW], 64)
    erhs = at("erhs", [P, 2, 2, 4, P], 76)
    ew = [at("ew0", [P, 2, 4, P], 84), at("ew1", [P, 2, 4, P], 40)]
    mw = [at("mw0", [P, 2, 4, P], 88), at("mw1", [P, 2, 4, P], 44)]
    vtl = [at("vtl0", [P, 2, GW], 92), at("vtl1", [P, 2, GW], 56)]
    y_one = at("y_one", [P, 2, GW], 60)
    y_two = at("y_two", [P, 2, GW], 92)
    htmp = at("htmp", [P, GW], 60)
    y_hi = at("y_hi", [P, XS_TILES, S], ST, F32R)
    y_lo = at("y_lo", [P, XS_TILES, S], ST + 32, F32R)
    sq_c = [[at(f"sq_c{g}_{i}", [P, S], ST + 32 + 2 * (XS_TILES + SG * i + g)) for i in range(2)] for g in range(SG)]
    nrm_c = [at(f"nrm_c{g}", [P, 3, S], ST + 8 * g) for g in range(SG)]
    m_ssd = at("m_ssd", [P, KT, S], 64)
    aneg = at("aneg", [P, 2 * SH], ST + 102.5)
    m_ffn = at("m_ffn", [P, KT, S], 64)
    g_hi = at("g_hi", [P, FT, S], ST, F32R)
    g_lo = at("g_lo", [P, FT, S], ST + 44, F32R)
    u = at("u", [P, 4, S], ST + 88)
    gv = at("gv", [P, 2, S], ST + 96)
    sq_b = at("sq_b", [P, 2, S], ST + 88)
    nrm_b = at("nrm_b", [P, 3, S], ST + 92)
    p1 = at("p1", [P, IN1_TILES, S], ST)
    mix = at("mix", [P, KT, S], ST + 48)
    vt = at("vt", [P, TT, SB_HEADS * DH], ST + 64)
    kv = at("kv", [P, 4, MEM], ST + 72)
    memx = at("memx", [P, KT, MEM], ST + 76)
    mem_hi = at("mem_hi", [P, KT, MEM], ST + 84, F32R)
    mem_lo = at("mem_lo", [P, KT, MEM], ST + 92, F32R)
    sp = at("sp", [P, 2, 1280], ST + 76)
    aw = at("aw", [P, 2, 1280], ST + 86)
    sq = at("sq", [P, 2, S], ST + 48)
    nrm = at("nrm", [P, 3, S], ST + 52)
    hbuf = at("hbuf", [P, 4, S], ST + 58)
    pooled = at("pooled", [P, 2, S], ST + 76)
    psum_s = at("psum_s", [P, 2, S], ST + 80)
    invc = at("invc", [P, 2, S], ST + 84)
    poolw = at("poolw", [P, 2, P], ST + 88)

    bank = [ctx.enter_context(nc.psum_tensor(f"bank{i}", [P, S], F32)) for i in range(8)]
    block = ctx.enter_context(nc.Block())

    w_load = [sem(f"w_load{s}") for s in range(RING)]
    hi_done, lo_done, slot_done = sem("hi_done"), sem("lo_done"), sem("slot_done")
    evac = [sem(f"evac{b}") for b in range(4)]

    def loops(eng, name, body):
        g = PLAN[name]
        turns = g["tiles"] // 4
        if turns == 1:
            body(0)
        else:
            with eng.Fori(0, turns) as i:
                body(i)

    def load_weights(sp_, name):
        g = PLAN[name]
        n, blocks = len(g["blocks"]), g["blocks"]
        src = dr["w_" + name]

        def body(i):
            for q in range(4 * n):
                s, t0 = q % RING, g["slot0"] + q
                if t0 >= RING:
                    sp_.wait_ge(hi_done, 4 * n * i + t0 - RING + 1)
                    sp_.wait_ge(lo_done, 4 * n * i + t0 - RING + 1)
                j, part = q // n, q % n
                nb = blocks[part]
                if isinstance(i, int):
                    row = src[4 * i + j]
                else:
                    row = src[bass.ds(4 * i + j, 1)].rearrange("a p c -> (a p) c")
                sp_.dma_start(raw[:, s, 0:nb * P], row[:, part * 8 * P:(part * 8 + nb) * P]).then_inc(w_load[s], 16)
        loops(sp_, name, body)

    def split_hi(act, name, i, q):
        g = PLAN[name]
        n = len(g["blocks"])
        t0, s = g["slot0"] + q + 2, (q + 2) % RING
        width = g["blocks"][(q + 2) % n] * P
        act.wait_ge(w_load[s], 16 * (n * i) + 16 * (t0 // RING + 1))
        if t0 >= RING:
            act.wait_ge(slot_done, 4 * n * i + t0 - RING + 1)
        nc.scalar.activation(w_hi[:, s, 0:width], raw[:, s, 0:width], ACT.Copy).then_inc(hi_done, 1)

    def split_lo(dve, name, i, q):
        g = PLAN[name]
        n = len(g["blocks"])
        t0, s = g["slot0"] + q + 2, (q + 2) % RING
        width = g["blocks"][(q + 2) % n] * P
        dve.wait_ge(hi_done, 4 * n * i + t0 + 1)
        nc.vector.tensor_tensor(w_lo[:, s, 0:width], raw[:, s, 0:width], w_hi[:, s, 0:width].bitcast(F32),
                                ALU.subtract).then_inc(lo_done, 1)

    def product_pe(pe, name, rhs_hi, rhs_lo, width=S):
        g = PLAN[name]
        n = len(g["blocks"])

        def body(i):
            for j in range(4):
                tile0 = g["tile0"] + j
                pe.wait_ge(evac[j], i + tile0 // 4)
                for part, nb in enumerate(g["blocks"]):
                    q = j * n + part
                    s = q % RING
                    pe.wait_ge(lo_done, 4 * n * i + g["slot0"] + q + 1)
                    for b in range(nb):
                        k = part * 8 + b
                        first = k == 0
                        last = part == n - 1 and b == nb - 1
                        wh, wl = w_hi[:, s, b * P:(b + 1) * P], w_lo[:, s, b * P:(b + 1) * P]
                        out = bank[j][:, 0:width]
                        nc.tensor.matmul(out, wh, rhs_hi[:, k, :], start=first, stop=False)
                        nc.tensor.matmul(out, wh, rhs_lo[:, k, :], start=False, stop=False)
                        mm = nc.tensor.matmul(out, wl, rhs_hi[:, k, :], start=False, stop=last)
                    mm.then_inc(slot_done, 1)
        loops(pe, name, body)

    def product_split(eng, name, split, take):
        g = PLAN[name]
        n = len(g["blocks"])

        def turn(i, final=False):
            for j in range(4):
                for part in range(n):
                    if not (final and j * n + part + 2 >= 4 * n):
                        split(eng, name, i, j * n + part)
                take(i, j, (4 * n * i) + g["slot0"] + (j + 1) * n)
        turns = g["tiles"] // 4
        if g["last"]:
            if turns > 2:
                with eng.Fori(0, turns - 1) as i:
                    turn(i)
            elif turns == 2:
                turn(0)
            turn(turns - 1, True)
        else:
            loops(eng, name, turn)

    sq_done, sq_used, ms_done = sem("sq_done"), sem("sq_used"), sem("ms_done")
    ln_done, rstd_done = sem("ln_done"), sem("rstd_done")
    h_done, ahi_done, alo_done = sem("h_done"), sem("ahi_done"), sem("alo_done")
    chain = {"dve": sem("dve_chain"), "act": sem("act_chain"), "pool": sem("pool_chain")}
    count = {"dve": 0, "act": 0, "pool": 0}

    def link(who, eng, ins):
        count[who] += 1
        ins.then_inc(chain[who], 1)
        eng.wait_ge(chain[who], count[who])

    def norm_pe(pe, n, width, sq=sq):
        for k in range(KT):
            pe.wait_ge(sq_done, KT * n + k + 1)
            mm = nc.tensor.matmul(bank[4][:, 0:width], C["ones"], sq[:, k % 2, 0:width], start=k == 0, stop=k == KT - 1)
            mm.then_inc(sq_used, 1)

    def norm_act(act, n, src, width, ready=None, sq=sq, nrm=nrm):
        for k in range(KT):
            if ready:
                ready(k)
            if KT * n + k >= 2:
                act.wait_ge(sq_used, KT * n + k - 1)
            nc.scalar.activation(sq[:, k % 2, 0:width], src[:, k, :], ACT.Square).then_inc(sq_done, 1)
        act.wait_ge(sq_used, KT * (n + 1))
        nc.scalar.activation(nrm[:, 0, 0:width], bank[4][:, 0:width], ACT.Ln, scale=1.0 / D, bias=eps_col[:, :]).then_inc(ln_done, 1)
        act.wait_ge(ln_done, n + 1)
        nc.scalar.activation(nrm[:, 1, 0:width], nrm[:, 0, 0:width], ACT.Exp, scale=-0.5).then_inc(rstd_done, 1)

    def pre_norm_act(act, n, src, width, hi, m, ready=None):
        norm_act(act, n, src, width, ready)
        for k in range(KT):
            act.wait_ge(h_done, m + k + 1)
            nc.scalar.activation(hi[:, k, :], hbuf[:, k % 4, 0:width], ACT.Copy).then_inc(ahi_done, 1)

    def refine(dve, sums, scale, r, a, t):
        link("dve", dve, nc.vector.tensor_scalar(a, sums, scale, EPS, ALU.mult, ALU.add))
        link("dve", dve, nc.vector.tensor_tensor(t, a, r, ALU.mult))
        link("dve", dve, nc.vector.tensor_tensor(t, t, r, ALU.mult))
        link("dve", dve, nc.vector.tensor_scalar(t, t, -0.5, 1.5, ALU.mult, ALU.add))
        link("dve", dve, nc.vector.tensor_tensor(r, r, t, ALU.mult))

    def norm_dve(dve, n, width, nrm=nrm):
        dve.wait_ge(rstd_done, n + 1)
        refine(dve, bank[4][:, 0:width], 1.0 / D, nrm[:, 1, 0:width], nrm[:, 2, 0:width], nrm[:, 0, 0:width])

    def pre_norm_dve(dve, n, src, width, gain, hi, lo, m):
        norm_dve(dve, n, width)

        def low(k):
            dve.wait_ge(ahi_done, m + k + 1)
            nc.vector.tensor_tensor(lo[:, k, :], hbuf[:, k % 4, 0:width], hi[:, k, :].bitcast(F32), ALU.subtract).then_inc(alo_done, 1)
        for k in range(KT):
            if k >= 4:
                dve.wait_ge(alo_done, m + k - 3)
            elif m:
                dve.wait_ge(alo_done, m - 3 + k if k < 3 else m)
            nc.vector.scalar_tensor_tensor(out=hbuf[:, k % 4, 0:width], in0=src[:, k, :], scalar=pcol(gain, k),
                                           in1=nrm[:, 1, 0:width], op0=ALU.mult, op1=ALU.mult).then_inc(h_done, 1)
            if k >= 2:
                low(k - 2)
        low(KT - 2)
        low(KT - 1)

    def x_ready(eng, version):
        def ready(k):
            if version == 1:
                eng.wait_ge(evac[k % 4], PLAN["out1"]["tile0"] // 4 + k // 4 + 1)
            else:
                eng.wait_ge(x_done, KT * (version - 2) + k + 1)
        return ready

    def tile_ready(eng, name):
        return lambda k: eng.wait_ge(evac[k % 4], PLAN[name]["tile0"] // 4 + k // 4 + 1)

    def post_norm_dve(dve, n, m, gain, nrm=nrm):
        norm_dve(dve, n, S, nrm)
        for k in range(KT):
            link("dve", dve, nc.vector.scalar_tensor_tensor(out=m[:, k, :], in0=m[:, k, :], scalar=pcol(gain, k), in1=nrm[:, 1, :],
                                                            op0=ALU.mult, op1=ALU.mult))
            nc.vector.tensor_tensor(x[:, k, :], x[:, k, :], m[:, k, :], ALU.add).then_inc(x_done, 1)

    def copy_tiles(dst, parity):
        def take(i, j, done):
            if j % 2 != parity:
                return
            out = dst[:, 4 * i + j, :] if isinstance(i, int) else dst[:, bass.ds(4 * i + j, 1), :].rearrange("p a t -> p (a t)")
            if parity == 0:
                act_.wait_ge(slot_done, done)
                nc.scalar.activation(out, bank[j][:, :], ACT.Copy).then_inc(evac[j], 1)
            else:
                dve_.wait_ge(slot_done, done)
                nc.vector.tensor_copy(out, bank[j][:, :]).then_inc(evac[j], 1)
        return take

    act_, dve_ = nc.scalar, nc.vector

    tab_load, dist_load, neg_tab = sem("tab_load"), sem("dist_load"), sem("neg_tab")
    dec_e, dec_done = sem("dec_e"), sem("dec_done")
    silu2, swap_done, cos_done, sin_done, rot_done = sem("silu2"), sem("swap_done"), sem("cos_done"), sem("sin_done"), sem("rot_done")
    strip_l, strip_e = sem("strip_l"), sem("strip_e")
    rz, ra, ry, ryc = sem("rz"), sem("ra"), sem("ry"), sem("ryc")
    g_mean, g_cent, g_sq, g_var, g_ln, g_done = sem("g_mean"), sem("g_cent"), sem("g_sq"), sem("g_var"), sem("g_ln"), sem("g_done")

    def ret_pe(pe):
        for t in range(8):
            if t >= 4:
                pe.wait_ge(sin_done, t - 3)
            nc.tensor.matmul(bank[4 + t % 4][:, :], C["swap"], p2[:, t, :], start=True, stop=True).then_inc(swap_done, 1)
        for i in range(4):
            for j in range(TT):
                mm = nc.tensor.transpose(bank[i][:, j * P:(j + 1) * P], p2[:, RET_V + i, j * P:(j + 1) * P], C["ident"])
            mm.then_inc(vtp, 1)
        pe.wait_ge(vtc, 2 * TT)
        pe.wait_ge(rot_done, 8)

        def scores(h):
            b, th = DH * (h % 2), h // 2
            if h >= 2:
                pe.wait_ge(ryc, h - 1)
            for j in range(TT):
                nc.tensor.matmul(zbank(h, j)[:, :], p2[b:b + DH, RET_K + th, j * P:(j + 1) * P], p2[b:b + DH, RET_Q + th, :],
                                 start=True, stop=True).then_inc(rz, 1)

        def values(h):
            b = DH * (h % 2)
            for j in range(TT):
                pe.wait_ge(ra, TT * h + j + 1)
                mm = nc.tensor.matmul(zbank(h, 0)[b:b + DH, :], vt2[:, j, h * DH:(h + 1) * DH], aw2[:, h % 2, j, :],
                                      start=j == 0, stop=j == TT - 1)
            mm.then_inc(ry, 1)
        scores(0)
        for h in range(RH):
            if h + 1 < RH:
                scores(h + 1)
            values(h)
        for t in range(4):
            pe.wait_ge(ryc, RH)
            if t >= 2:
                pe.wait_ge(g_cent, t - 1)
            nc.tensor.matmul(bank[t % 2][:, :], C["ones64"], p2[:, RET_V + t, :], start=True, stop=True).then_inc(g_mean, 1)
            pe.wait_ge(g_sq, t + 1)
            if t >= 2:
                pe.wait_ge(g_done, t - 1)
            nc.tensor.matmul(bank[2 + t % 2][:, :], C["ones64"], gsq[:, t % 2, :], start=True, stop=True).then_inc(g_var, 1)

    def decay_act(act):
        act.wait_ge(neg_tab, 1)
        nc.scalar.activation(dec[:, 1, :], dec[:, 0, :], ACT.Exp).then_inc(dec_e, 1)
        act.wait_ge(neg_tab, 2)
        nc.scalar.activation(dec[:, 3, :], dec[:, 2, :], ACT.Ln).then_inc(dec_e, 1)

    def log1p_fix(dve, e, one_plus, log, tmp):
        link("dve", dve, nc.vector.tensor_scalar(tmp, one_plus, -1.0, None, ALU.add))
        link("dve", dve, nc.vector.tensor_tensor(tmp, e, tmp, ALU.subtract))
        link("dve", dve, nc.vector.reciprocal(one_plus, one_plus))
        link("dve", dve, nc.vector.tensor_tensor(tmp, tmp, one_plus, ALU.mult))
        link("dve", dve, nc.vector.tensor_tensor(log, log, tmp, ALU.add))

    def decay_dve(dve):
        logit = par[:, PCOL["decay"]:PCOL["decay"] + 16]
        nc.vector.tensor_scalar(dec[:, 0, :], logit, -1.0, 30.0, ALU.mult, ALU.min).then_inc(neg_tab, 1)
        dve.wait_ge(dec_e, 1)
        nc.vector.tensor_scalar(dec[:, 2, :], dec[:, 1, :], 1.0, None, ALU.add).then_inc(neg_tab, 1)
        dve.wait_ge(dec_e, 2)
        log1p_fix(dve, dec[:, 1, :], dec[:, 2, :], dec[:, 3, :], dec[:, 4, :])
        link("dve", dve, nc.vector.tensor_scalar(dec[:, 4, :], logit, -1.0, None, ALU.mult))
        link("dve", dve, nc.vector.tensor_tensor(dec[:, 3, :], dec[:, 3, :], dec[:, 4, :], ALU.max))
        link("dve", dve, nc.vector.tensor_scalar(dec[:, 4, :], dec[:, 3, :], -1.0, None, ALU.mult))

    def ret_act(act):
        decay_act(act)
        for i in range(4):
            act.wait_ge(vtp, TT + i + 1)
            nc.scalar.activation(vt2[:, :, i * P:(i + 1) * P], bank[i][:, :].rearrange("p (j c) -> p j c", c=P),
                                 ACT.Copy).then_inc(vtc, 1)
        for h in range(RH):
            act.wait_ge(strip_l, h + 1)
            nc.scalar.activation(strip[:, h % 2, :], strip[:, h % 2, :], ACT.Exp).then_inc(strip_e, 1)
        for t in range(4):
            act.wait_ge(g_cent, t + 1)
            nc.scalar.activation(gsq[:, t % 2, :], p2[:, RET_V + t, :], ACT.Square).then_inc(g_sq, 1)
            act.wait_ge(g_var, t + 1)
            if t >= 2:
                act.wait_ge(g_done, t - 1)
            nc.scalar.activation(grs[:, t % 2, :], bank[2 + t % 2][:, :], ACT.Ln, scale=1.0 / DH, bias=eps_col[:, :]).then_inc(g_ln, 1)
            act.wait_ge(g_ln, 2 * t + 1)
            nc.scalar.activation(grs[:, t % 2, :], grs[:, t % 2, :], ACT.Exp, scale=-0.5).then_inc(g_ln, 1)

    def ret_pool(pool):
        pool.wait_ge(tab_load, 16)
        for t in range(8):
            pool.wait_ge(swap_done, t + 1)
            nc.gpsimd.tensor_tensor(p2[:, t, :], p2[:, t, :], rope[:, 0, :], ALU.mult).then_inc(cos_done, 1)

    def ret_dve(dve):
        dve.wait_ge(tab_load, 16)
        dve.wait_ge(dist_load, 16)
        for t in range(8):
            dve.wait_ge(swap_done, t + 1)
            nc.vector.tensor_tensor(rtmp[:, t % 2, :], bank[4 + t % 4][:, :], rope[:, 1, :], ALU.mult).then_inc(sin_done, 1)
            dve.wait_ge(sin_done, t + 1)
            dve.wait_ge(cos_done, t + 1)
            nc.vector.tensor_tensor(p2[:, t, :], p2[:, t, :], rtmp[:, t % 2, :], ALU.add).then_inc(rot_done, 1)
        decay_dve(dve)

        def log_decay(h):
            if h >= 2:
                dve.wait_ge(ra, TT * (h - 1))
            link("dve", dve, nc.vector.tensor_scalar(strip[:, h % 2, :], dist[:, :], dec[:, 3, 8 + h:9 + h], None, ALU.mult))
            nc.vector.scalar_tensor_tensor(out=strip[:, h % 2, :], in0=dist[:, :], scalar=dec[:, 4, h:h + 1], in1=strip[:, h % 2, :],
                                           op0=ALU.mult, op1=ALU.min).then_inc(strip_l, 1)

        def weigh(h):
            dve.wait_ge(strip_e, h + 1)
            for j in range(TT):
                dve.wait_ge(rz, TT * h + j + 1)
                if h >= 2 and j == 0:
                    dve.wait_ge(ry, h - 1)
                nc.vector.scalar_tensor_tensor(out=aw2[:, h % 2, j, :], in0=zbank(h, j)[:, :], scalar=DH ** -0.5,
                                               in1=strip[:, h % 2, S - P - j * P:2 * S - P - j * P], op0=ALU.mult, op1=ALU.mult).then_inc(ra, 1)

        def keep(h):
            b, th = DH * (h % 2), h // 2
            dve.wait_ge(ry, h + 1)
            nc.vector.tensor_copy(p2[b:b + DH, RET_V + th, :], zbank(h, 0)[b:b + DH, :]).then_inc(ryc, 1)
        log_decay(0)
        for h in range(RH):
            if h + 1 < RH:
                log_decay(h + 1)
            weigh(h)
            if h:
                keep(h - 1)
        keep(RH - 1)
        for t in range(4):
            y = p2[:, RET_V + t, :]
            dve.wait_ge(g_mean, t + 1)
            nc.vector.scalar_tensor_tensor(out=y, in0=bank[t % 2][:, :], scalar=-1.0 / DH, in1=y, op0=ALU.mult, op1=ALU.add).then_inc(g_cent, 1)
            dve.wait_ge(g_ln, 2 * t + 2)
            r = grs[:, t % 2, :]
            refine(dve, bank[2 + t % 2][:, :], 1.0 / DH, r, gtmp[:, 0, :], gtmp[:, 1, :])
            link("dve", dve, nc.vector.scalar_tensor_tensor(out=y, in0=y, scalar=pcol("ret_gn_g", t), in1=r, op0=ALU.mult, op1=ALU.mult))
            nc.vector.tensor_tensor(p2[:, RET_G + t, :], p2[:, RET_G + t, :], y, ALU.mult).then_inc(g_done, 1)

    nvp, nvc, bt_load, bm_done = sem("nvp"), sem("nvc"), [sem("bt_load0"), sem("bt_load1")], sem("bm_done")
    cm_load, nvw_done, nq_done = sem("cm_load"), sem("nvw_done"), sem("nq_done")
    nz, ns, nmax, nexp, nnorm, ntp, ntc, ny, nyc = (sem(n) for n in ("nz", "ns", "nmax", "nexp", "nnorm", "ntp", "ntc", "ny", "nyc"))
    WIN0 = [min(max(QB * c - WIN_C // 2, 0), GRID_W - KEYW) for c in range(4)]
    NU = 2 * NH

    def grid(tile, b0=0, b1=P):
        return p2[b0:b1, tile, :].rearrange("p (r c) -> p r c", c=GRID_W)

    def na_pe(pe):
        pe.wait_ge(g_done, 4)
        pe.wait_ge(nvw_done, 16)
        for c in range(4):
            for f in range(2):
                n = 2 * c + f
                for i in range(4):
                    mm = nc.tensor.transpose(bank[n][:, i * P:(i + 1) * P], nvw[:, c, i, f * P:(f + 1) * P], C["ident"])
                mm.then_inc(nvp, 1)
        pe.wait_ge(nvc, 8)
        pe.wait_ge(nq_done, 4)

        def scores(un):
            h, i = un // 2, un % 2
            b, th = DH * (h % 2), h // 2
            if un >= 2:
                pe.wait_ge(ns, un - 1)
            for r in range(2):
                c = 2 * i + r
                mm = nc.tensor.matmul(bank[un % 2][:, r * 256:(r + 1) * 256], p2[b:b + DH, RET_Q + th, c * P:(c + 1) * P],
                                      grid(NA_K + th, b, b + DH)[:, :, WIN0[c]:WIN0[c] + KEYW], start=True, stop=True)
            mm.then_inc(nz, 1)

        def turn(un):
            pe.wait_ge(nnorm, un + 1)
            if un >= 2:
                pe.wait_ge(ntc, un - 1)
            for r in range(2):
                for f in range(2):
                    mm = nc.tensor.transpose(bank[2 + un % 2][:, (2 * r + f) * P:(2 * r + f + 1) * P],
                                             nprob[:, un % 2, r, f * P:(f + 1) * P], C["ident"])
            mm.then_inc(ntp, 1)

        def values(un):
            h, i = un // 2, un % 2
            b = DH * (h % 2)
            pe.wait_ge(ntc, un + 1)
            if i == 0 and h >= 2:
                pe.wait_ge(nyc, h - 1)
            for r in range(2):
                c = 2 * i + r
                for f in range(2):
                    mm = nc.tensor.matmul(bank[4 + h % 2][b:b + DH, c * P:(c + 1) * P], vna[:, c, f, h * DH:(h + 1) * DH],
                                          npt[:, un % 2, 2 * r + f, :], start=f == 0, stop=f == 1)
            if i:
                mm.then_inc(ny, 1)
        scores(0)
        for un in range(NU):
            if un + 1 < NU:
                scores(un + 1)
            if un:
                values(un - 1)
            turn(un)
        values(NU - 1)

    def load_bias(act, h):
        act.dma_start(bt[:, h % 2, :, :].rearrange("p r c -> p (r c)")[:, 0:BIAS_RUN], dr["rpb"][h]).then_inc(bt_load[h % 2], 16)

    def na_act(act):
        act.wait_ge(g_done, 4)
        act.dma_start(cmask[:, :, :], dr["col_mask"]).then_inc(cm_load, 16)
        load_bias(act, 0)
        load_bias(act, 1)
        for n in range(8):
            act.wait_ge(nvp, n + 1)
            nc.scalar.activation(vna[:, n // 2, n % 2, :], bank[n][:, :], ACT.Copy).then_inc(nvc, 1)
        for un in range(NU):
            if un % 2 == 0 and un // 2 + 2 < NH:
                act.wait_ge(bm_done, un // 2 + 1)
                load_bias(act, un // 2 + 2)
            act.wait_ge(nmax, un + 1)
            for r in range(2):
                c = 2 * un + r
                e = nc.scalar.activation(nprob[:, un % 2, r, :], nprob[:, un % 2, r, :], ACT.Exp, bias=nstat[:, 0, c:c + 1],
                                         accum_out=nstat[:, 1, c:c + 1])
            e.then_inc(nexp, 1)

    def na_pool(pool):
        pool.wait_ge(g_done, 4)
        for t in range(4):
            nc.gpsimd.tensor_copy(p2[:, RET_Q + t, :].rearrange("p (c r q) -> p c r q", c=4, q=QB),
                                  p2[:, NA_Q + t, :].rearrange("p (r c q) -> p c r q", c=4, q=QB)).then_inc(nq_done, 1)
        pool.wait_ge(cm_load, 16)
        for h in range(NH):
            pool.wait_ge(bt_load[h % 2], 16 * (h // 2 + 1))
            if h >= 2:
                pool.wait_ge(ns, 2 * (h - 1))
            for c in range(4):
                o = WIN0[c] - QB * c + WIN_C
                add = nc.gpsimd.tensor_tensor(bm[:, h % 2, c, :, :], bt[:, h % 2, :, o:o + KEYW],
                                              cmask[:, c:c + 1, :].to_broadcast([P, ROWS, KEYW]), ALU.add)
            add.then_inc(bm_done, 1)

    def na_dve(dve):
        dve.wait_ge(g_done, 4)
        for c in range(4):
            for i in range(4):
                nc.vector.tensor_copy(nvw[:, c, i, :].rearrange("p (r k) -> p r k", k=KEYW),
                                      grid(NA_V + i)[:, :, WIN0[c]:WIN0[c] + KEYW]).then_inc(nvw_done, 1)

        def shift(un):
            h, i = un // 2, un % 2
            dve.wait_ge(nz, un + 1)
            dve.wait_ge(bm_done, h + 1)
            if un >= 2:
                dve.wait_ge(ntp, un - 1)
            nc.vector.scalar_tensor_tensor(out=nprob[:, un % 2, :, :].rearrange("p r k -> p (r k)"), in0=bank[un % 2][:, :], scalar=DH ** -0.5,
                                           in1=bm[:, h % 2, 2 * i:2 * i + 2, :, :].rearrange("p c r k -> p (c r k)"),
                                           op0=ALU.mult, op1=ALU.add).then_inc(ns, 1)
            dve.wait_ge(ns, un + 1)
            nc.vector.tensor_reduce(nstat[:, 0, 2 * un:2 * un + 2], nprob[:, un % 2, :, :], AX.X, ALU.max, negate=True).then_inc(nmax, 1)

        def norm(un):
            dve.wait_ge(nexp, un + 1)
            link("dve", dve, nc.vector.reciprocal(nstat[:, 2, 2 * un:2 * un + 2], nstat[:, 1, 2 * un:2 * un + 2]))
            for r in range(2):
                c = 2 * un + r
                m = nc.vector.tensor_scalar(nprob[:, un % 2, r, :], nprob[:, un % 2, r, :], nstat[:, 2, c:c + 1], None, ALU.mult)
            m.then_inc(nnorm, 1)

        def turned(un):
            h = un // 2
            b, th = DH * (h % 2), h // 2
            dve.wait_ge(ntp, un + 1)
            nc.vector.tensor_copy(npt[:, un % 2, :, :].rearrange("p a q -> p (a q)"), bank[2 + un % 2][:, :]).then_inc(ntc, 1)
            if un % 2 == 0 and h:
                keep(h - 1)

        def keep(h):
            b, th = DH * (h % 2), h // 2
            dve.wait_ge(ny, h + 1)
            nc.vector.tensor_copy(p2[b:b + DH, NA_Q + th, :].rearrange("p (r c q) -> p c r q", c=4, q=QB),
                                  bank[4 + h % 2][b:b + DH, :].rearrange("p (c r q) -> p c r q", c=4, q=QB)).then_inc(nyc, 1)
        shift(0)
        for un in range(NU):
            if un + 1 < NU:
                shift(un + 1)
            norm(un)
            turned(un)
        keep(NH - 1)


    def mix2(k):
        return p2[:, RET_G + k, :] if k < 4 else p2[:, NA_Q + k - 4, :]

    def split_mix2_act(act):
        for k in range(KT):
            act.wait_ge(g_done, 4) if k == 0 else None
            if k == 4:
                act.wait_ge(nyc, NH)
            nc.scalar.activation(a_hi[:, k, :], mix2(k), ACT.Copy).then_inc(mixhi, 1)

    def split_mix2_dve(dve):
        for k in range(KT):
            dve.wait_ge(mixhi, KT + k + 1)
            nc.vector.tensor_tensor(a_lo[:, k, :], mix2(k), a_hi[:, k, :].bitcast(F32), ALU.subtract).then_inc(mixlo, 1)

    mid, left, gel, prod, ghi, glo = (sem(n) for n in ("mid", "left", "gel", "prod", "ghi", "glo"))

    def col(table, width, i, j, tap=0):
        if isinstance(i, int):
            c = PCOL[table] + width * (4 * i + j) + tap
            return par[:, c:c + 1]
        return par[:, bass.ds(4 * width * i + (PCOL[table] + width * j + tap), 1)]

    def row(buf, i, r):
        if isinstance(i, int):
            return buf[:, 2 * i + r, :]
        return buf[:, bass.ds(2 * i + r, 1), :].rearrange("p a t -> p (a t)")

    def up_act(layer):
        def high(i, r):
            act_.wait_ge(prod, 2 * i + r + 3 + FT * layer)
            nc.scalar.activation(row(g_hi, i, r), gv[:, r, :], ACT.Copy).then_inc(ghi, 1)

        def take(i, j, done):
            act_.wait_ge(slot_done, done)
            act_.wait_ge(prod, 2 * i + j // 2 + 1 + FT * layer)
            nc.scalar.activation(u[:, j, :], bank[j][:, :], ACT.Identity, scale=col(f"ffn_w{layer}", 3, i, j, 1),
                                 bias=col(f"ffn_b{layer}", 1, i, j)).then_inc(mid, 1)
            if j == 2:
                high(i, 0)
            if j % 2:
                act_.wait_ge(evac[j - 1], i + (PLAN[f"up{layer}"]["tile0"] // 4 + 1))
                nc.scalar.activation(u[:, j - 1, :], u[:, j - 1, :], ACT.Gelu_apprx_tanh).then_inc(gel, 1)
            if j == 3:
                high(i, 1)
        return take

    def up_dve(layer):
        def low(i, r):
            dve_.wait_ge(ghi, 2 * i + r + 1 + FT * layer)
            nc.vector.tensor_tensor(row(g_lo, i, r), gv[:, r, :], row(g_hi, i, r).bitcast(F32), ALU.subtract).then_inc(glo, 1)

        def take(i, j, done):
            w = f"ffn_w{layer}"
            dve_.wait_ge(mid, 4 * i + j + 1 + 2 * FT * layer)
            nc.vector.scalar_tensor_tensor(out=u[:, j, 1:S], in0=bank[j][:, 0:S - 1], scalar=col(w, 3, i, j, 0), in1=u[:, j, 1:S],
                                           op0=ALU.mult, op1=ALU.add).then_inc(left, 1)
            dve_.wait_ge(left, 4 * i + j + 1 + 2 * FT * layer)
            nc.vector.scalar_tensor_tensor(out=u[:, j, 0:S - 1], in0=bank[j][:, 1:S], scalar=col(w, 3, i, j, 2), in1=u[:, j, 0:S - 1],
                                           op0=ALU.mult, op1=ALU.add).then_inc(evac[j], 1)
            if j == 2:
                low(i, 0)
            if j == 3:
                low(i, 1)
        return take

    def up_pool(pool, layer):
        with pool.Fori(0, FT // 2) as i:
            for r in range(2):
                pool.wait_ge(gel, 2 * i + r + 1 + FT * layer)
                pool.wait_ge(evac[2 * r + 1], i + (PLAN[f"up{layer}"]["tile0"] // 4 + 1))
                pool.wait_ge(glo, 2 * i + r + 1 + FT * layer)
                nc.gpsimd.tensor_tensor(gv[:, r, :], u[:, 2 * r, :], u[:, 2 * r + 1, :], ALU.mult).then_inc(prod, 1)

    eps_col = at("eps_col", [P, 1], 103.5)
    x_load, mem_load, cst_load, par_load, poolc_load = sem("x_load"), sem("mem_load"), sem("cst_load"), sem("par_load"), sem("poolc_load")
    x_done, out_done, eps_done = sem("x_done"), sem("out_done"), sem("eps_done")

    M_MEM, M_IN1 = 0, 8

    silu_done, pooled_done, poolmm, pool_y = sem("silu_done"), sem("pooled_done"), sem("poolmm"), sem("pool_y")
    vtp, vtc, q_scaled = sem("vtp"), sem("vtc"), sem("q_scaled")
    z_done, na_done, e_done, sp_done, spm_done = sem("z_done"), sem("na_done"), sem("e_done"), sem("sp_done"), sem("spm_done")
    la_done, a_done, am_done, y_done, y_read = sem("la_done"), sem("a_done"), sem("am_done"), sem("y_done"), sem("y_read")
    mixhi, mixlo = sem("mixhi"), sem("mixlo")

    KCOL = [0, 512, 896, 1152]
    KW = [S - P * j for j in range(TT)]

    def seg(buf, h, j, a=0, b=None):
        return buf[:, h % 2, KCOL[j] + a:KCOL[j] + (KW[j] if b is None else b)]

    def zbank(h, j):
        return bank[4 * (h % 2) + j]

    def stick_pe(pe):
        for i in range(4):
            for j in range(TT):
                mm = nc.tensor.transpose(bank[i][:, j * P:(j + 1) * P], p1[:, SB_V + i, j * P:(j + 1) * P], C["ident"])
            mm.then_inc(vtp, 1)

        def scores(h):
            b, th = DH * (h % 2), h // 2
            if h == 0:
                pe.wait_ge(q_scaled, 4)
            if h < 2:
                pe.wait_ge(vtc, 4)
            else:
                pe.wait_ge(y_read, h - 1)
            for j in range(TT):
                nc.tensor.matmul(zbank(h, j)[:, 0:KW[j]], p1[b:b + DH, SB_K + th, j * P:(j + 1) * P],
                                 p1[b:b + DH, SB_Q + th, j * P:S], start=True, stop=True).then_inc(z_done, 1)

        def suffix(h):
            pe.wait_ge(spm_done, TT * (h + 1))
            for j in range(TT):
                for jj in range(j, TT):
                    mm = nc.tensor.matmul(zbank(h, j)[:, (jj - j) * P:KW[j]], C["neg_tri"] if jj == j else C["neg_ones"],
                                          seg(sp, h, jj), start=False, stop=jj == TT - 1, skip_group_check=True)
                mm.then_inc(la_done, 1)

        def values(h):
            b = DH * (h % 2)
            for j in range(TT):
                pe.wait_ge(am_done, TT * h + j + 1)
                mm = nc.tensor.matmul(zbank(h, 0)[b:b + DH, j * P:S], vt[:, j, h * DH:(h + 1) * DH], seg(aw, h, j),
                                      start=j == 0, stop=j == TT - 1)
            mm.then_inc(y_done, 1)

        scores(0)
        for h in range(SB_HEADS):
            if h + 1 < SB_HEADS:
                scores(h + 1)
            suffix(h)
            values(h)

    def stick_act(act):
        for i in range(4):
            act.wait_ge(vtp, i + 1)
            nc.scalar.activation(vt[:, :, i * P:(i + 1) * P], bank[i][:, :].rearrange("p (j c) -> p j c", c=P),
                                 ACT.Copy).then_inc(vtc, 1)

        def softplus(h):
            for j in range(TT):
                n = TT * h + j
                act.wait_ge(na_done, n + 1)
                nc.scalar.activation(seg(sp, h, j), seg(sp, h, j), ACT.Exp).then_inc(e_done, 1)
                act.wait_ge(e_done, 2 * n + 1)
                nc.scalar.activation(seg(sp, h, j), seg(sp, h, j), ACT.Ln, bias=1.0).then_inc(e_done, 1)

        def weights(h):
            for j in range(TT):
                n = TT * h + j
                act.wait_ge(la_done, n + 1)
                if h >= 2:
                    act.wait_ge(y_done, h - 1)
                nc.scalar.activation(seg(aw, h, j), zbank(h, j)[:, 0:KW[j]], ACT.Exp).then_inc(a_done, 1)
        softplus(0)
        for h in range(SB_HEADS):
            if h + 1 < SB_HEADS:
                softplus(h + 1)
            weights(h)

    def stick_dve(dve):
        def softplus(h):
            for j in range(TT):
                n = TT * h + j
                dve.wait_ge(z_done, n + 1)
                if h >= 2:
                    dve.wait_ge(la_done, TT * (h - 1))
                nc.vector.tensor_scalar(seg(sp, h, j), zbank(h, j)[:, 0:KW[j]], 30.0, None, ALU.min).then_inc(na_done, 1)
            for j in range(TT):
                n = TT * h + j
                dve.wait_ge(e_done, 2 * n + 2)
                nc.vector.tensor_tensor(seg(sp, h, j), zbank(h, j)[:, 0:KW[j]], seg(sp, h, j), ALU.max).then_inc(sp_done, 1)

        def gate(h):
            b, th = DH * (h % 2), h // 2
            dve.wait_ge(y_done, h + 1)
            nc.vector.tensor_tensor(mix[b:b + DH, 2 + th, :], zbank(h, 0)[b:b + DH, :], p1[b:b + DH, SB_G + th, :],
                                    ALU.mult).then_inc(y_read, 1)
        softplus(0)
        for h in range(SB_HEADS):
            if h + 1 < SB_HEADS:
                softplus(h + 1)
            gate(h)

    def stick_pool(pool):
        def mask(src, done, out):
            nc.gpsimd.affine_select(out=src, in_=src, compare_op=ALU.is_gt, fill=0.0, base=0, pattern=[[1, P]],
                                    channel_multiplier=-1).then_inc(out, 1)

        def softplus(h):
            for j in range(TT):
                pool.wait_ge(sp_done, TT * h + j + 1)
                mask(seg(sp, h, j, 0, P), sp_done, spm_done)

        def weights(h):
            for j in range(TT):
                pool.wait_ge(a_done, TT * h + j + 1)
                mask(seg(aw, h, j, 0, P), a_done, am_done)
        softplus(0)
        for h in range(SB_HEADS):
            if h + 1 < SB_HEADS:
                softplus(h + 1)
            weights(h)

    def pool_pool(pool):
        pool.wait_ge(evac[0], PLAN["in1"]["tile0"] // 4 + 1)
        pool.wait_ge(evac[1], PLAN["in1"]["tile0"] // 4 + 1)
        nc.gpsimd.memset(poolw[:, :, :], 0.0).then_inc(sem("poolw_zero"), 1)
        pool.wait_ge(poolc_load, 16)
        for t in range(2):
            u, cur, w = p1[:, POOL_V + t, :], p1[:, POOL_V + t, :], 1
            lo_stop = 2 if t == 0 else 8
            for stage in range(2 if t == 0 else 4):
                nxt = psum_s[:, stage % 2, :]
                link("pool", pool, nc.gpsimd.tensor_copy(nxt[:, 0:w], cur[:, 0:w]))
                link("pool", pool, nc.gpsimd.tensor_tensor(nxt[:, w:S], cur[:, w:S], cur[:, 0:S - w], ALU.add))
                w *= 2
                cur = nxt
                if w == lo_stop:
                    link("pool", pool, nc.gpsimd.tensor_tensor(pooled[0:DH, t, :], cur[0:DH, :], invc[0:DH, t, :], ALU.mult))
            link("pool", pool, nc.gpsimd.tensor_tensor(pooled[DH:P, t, :], cur[DH:P, :], invc[DH:P, t, :], ALU.mult))
            nc.gpsimd.tensor_tensor(pooled[:, t, :], pooled[:, t, :], u, ALU.subtract).then_inc(pooled_done, 1)

    def pool_pe(pe):
        pe.wait_ge(sem("poolw_load"), 64)
        pe.wait_ge(evac[0], PLAN["out1"]["tile0"] // 4)
        for t in range(2):
            pe.wait_ge(pooled_done, t + 1)
            nc.tensor.matmul(bank[4 + t][:, :], poolw[:, t, :], pooled[:, t, :], start=True, stop=True).then_inc(poolmm, 1)

    def pool_dve(dve):
        dve.wait_ge(silu_done, 2)
        for t in range(2):
            dve.wait_ge(poolmm, t + 1)
            nc.vector.scalar_tensor_tensor(out=mix[:, t, :], in0=bank[4 + t][:, :], scalar=pcol("pool_scale", t),
                                           in1=p1[:, POOL_G + t, :], op0=ALU.mult, op1=ALU.mult).then_inc(pool_y, 1)

    mq = at("mq", [P, 2, S], ST + 76)
    mk = at("mk", [P, 2, MEM], ST + 80)
    msq = at("msq", [P, S], ST + 82)
    mrs = at("mrs", [P, S], ST + 84)
    mtmp = at("mtmp", [P, 2, S], ST + 88)
    mvt = at("mvt", [P, 2, MEM], ST + 86)
    prob = at("prob", [P, 2, 2, MEM], ST + 88)
    pt = at("pt", [P, 2, S], ST + 92)
    mstat = at("mstat", [P, 4, 16], ST + 96)
    msq_done, mms_done, mln_done, mrs_done, mn_done = sem("msq_done"), sem("mms_done"), sem("mln_done"), sem("mrs_done"), sem("mn_done")
    mvp, mvc, ms_rdy, mmax, mexp, mnorm = sem("mvp"), sem("mvc"), sem("ms_rdy"), sem("mmax"), sem("mexp"), sem("mnorm")
    mtp, mtc, my_done, my_read = sem("mtp"), sem("mtc"), sem("my_done"), sem("my_read")
    NORMS = [(p1, MEM_Q, S, "q_norm_g", 0), (p1, MEM_Q + 1, S, "q_norm_g", 1), (kv, 0, MEM, "k_norm_g", 0), (kv, 1, MEM, "k_norm_g", 1)]

    def mem_pe(pe):
        pe.wait_ge(y_read, SB_HEADS)
        for n, (src, t, w, g, o) in enumerate(NORMS):
            pe.wait_ge(msq_done, n + 1)
            if n:
                pe.wait_ge(mn_done, n)
            nc.tensor.matmul(bank[0][:, 0:w], C["ones64"], msq[:, 0:w], start=True, stop=True).then_inc(mms_done, 1)
        for t in range(2):
            for m in range(2):
                mm = nc.tensor.transpose(bank[1][:, (2 * m + t) * P:(2 * m + t + 1) * P], kv[:, 2 + t, m * P:(m + 1) * P], C["ident"])
        mm.then_inc(mvp, 1)
        pe.wait_ge(mn_done, 4)
        for h in range(MEM_HEADS):
            b, th = DH * (h % 2), h // 2
            for i in range(2):
                u = 2 * h + i
                if u >= 2:
                    pe.wait_ge(mexp, u - 1)
                for r in range(2):
                    mm = nc.tensor.matmul(bank[2 + u % 2][:, r * MEM:(r + 1) * MEM], mq[b:b + DH, th, (2 * i + r) * P:(2 * i + r + 1) * P],
                                          mk[b:b + DH, th, :], start=True, stop=True)
                mm.then_inc(ms_rdy, 1)
            for i in range(2):
                u = 2 * h + i
                pe.wait_ge(mnorm, u + 1)
                if u >= 2:
                    pe.wait_ge(mtc, u - 1)
                for m in range(2):
                    for r in range(2):
                        mm = nc.tensor.transpose(bank[4 + u % 2][:, (2 * m + r) * P:(2 * m + r + 1) * P],
                                                 prob[:, u % 2, r, m * P:(m + 1) * P], C["ident"])
                mm.then_inc(mtp, 1)
            pe.wait_ge(mtc, 2 * h + 2)
            pe.wait_ge(mvc, 1)
            if h >= 2:
                pe.wait_ge(my_read, h - 1)
            for m in range(2):
                mm = nc.tensor.matmul(bank[6 + h % 2][b:b + DH, :], mvt[:, m, h * DH:(h + 1) * DH], pt[:, m, :], start=m == 0, stop=m == 1)
            mm.then_inc(my_done, 1)

    def mem_act(act):
        act.wait_ge(pool_y, 2)
        act.wait_ge(y_done, SB_HEADS)
        for n, (src, t, w, g, o) in enumerate(NORMS):
            if n:
                act.wait_ge(mms_done, n)
            nc.scalar.activation(msq[:, 0:w], src[:, t, :], ACT.Square).then_inc(msq_done, 1)
            act.wait_ge(mms_done, n + 1)
            if n:
                act.wait_ge(mn_done, n)
            nc.scalar.activation(mrs[:, 0:w], bank[0][:, 0:w], ACT.Ln, scale=1.0 / DH, bias=eps_col[:, :]).then_inc(mln_done, 1)
            act.wait_ge(mln_done, 2 * n + 1)
            nc.scalar.activation(mrs[:, 0:w], mrs[:, 0:w], ACT.Exp, scale=-0.5).then_inc(mln_done, 1)
        act.wait_ge(mvp, 1)
        nc.scalar.activation(mvt[:, :, :], bank[1][:, :].rearrange("p (m c) -> p m c", m=2), ACT.Copy).then_inc(mvc, 1)
        for u in range(2 * MEM_HEADS):
            act.wait_ge(mmax, u + 1)
            if u >= 2:
                act.wait_ge(mtp, u - 1)
            for r in range(2):
                c = 2 * u + r
                e = nc.scalar.activation(prob[:, u % 2, r, :], bank[2 + u % 2][:, r * MEM:(r + 1) * MEM], ACT.Exp,
                                         bias=mstat[:, 1, c:c + 1], scale=DH ** -0.5, accum_out=mstat[:, 2, c:c + 1])
            e.then_inc(mexp, 1)

    def mem_dve(dve):
        for n, (src, t, w, g, o) in enumerate(NORMS):
            dve.wait_ge(mln_done, 2 * n + 2)
            dst = mq if src is p1 else mk
            refine(dve, bank[0][:, 0:w], 1.0 / DH, mrs[:, 0:w], mtmp[:, 0, 0:w], mtmp[:, 1, 0:w])
            nc.vector.scalar_tensor_tensor(out=dst[:, o, :], in0=src[:, t, :], scalar=pcol(g), in1=mrs[:, 0:w],
                                           op0=ALU.mult, op1=ALU.mult).then_inc(mn_done, 1)

        def top(u):
            dve.wait_ge(ms_rdy, u + 1)
            link("dve", dve, nc.vector.tensor_reduce(mstat[:, 0, 2 * u:2 * u + 2], bank[2 + u % 2][:, :].rearrange("p (r m) -> p r m", r=2),
                                                     AX.X, ALU.max))
            nc.vector.tensor_scalar(mstat[:, 1, 2 * u:2 * u + 2], mstat[:, 0, 2 * u:2 * u + 2], -DH ** -0.5, None, ALU.mult).then_inc(mmax, 1)

        def norm(u):
            dve.wait_ge(mexp, u + 1)
            link("dve", dve, nc.vector.reciprocal(mstat[:, 3, 2 * u:2 * u + 2], mstat[:, 2, 2 * u:2 * u + 2]))
            for r in range(2):
                c = 2 * u + r
                m = nc.vector.tensor_scalar(prob[:, u % 2, r, :], prob[:, u % 2, r, :], mstat[:, 3, c:c + 1], None, ALU.mult)
            m.then_inc(mnorm, 1)

        def turned(u):
            h, i = u // 2, u % 2
            dve.wait_ge(mtp, u + 1)
            if i == 0 and h:
                dve.wait_ge(my_done, h)
            nc.vector.tensor_copy(pt[:, :, 2 * i * P:2 * (i + 1) * P], bank[4 + u % 2][:, :].rearrange("p (m r) -> p m r", m=2)).then_inc(mtc, 1)

        for h in range(MEM_HEADS):
            top(2 * h)
            top(2 * h + 1)
            norm(2 * h)
            norm(2 * h + 1)
            turned(2 * h)
            turned(2 * h + 1)
            b, th = DH * (h % 2), h // 2
            dve.wait_ge(my_done, h + 1)
            nc.vector.tensor_tensor(mix[b:b + DH, 6 + th, :], bank[6 + h % 2][b:b + DH, :], p1[b:b + DH, MEM_G + th, :],
                                    ALU.mult).then_inc(my_read, 1)

    def split_mix_act(act):
        for k in range(KT):
            if k == 0:
                act.wait_ge(pool_y, 2)
            if k == 2:
                act.wait_ge(y_read, SB_HEADS)
            if k == 6:
                act.wait_ge(my_read, MEM_HEADS)
            nc.scalar.activation(a_hi[:, k, :], mix[:, k, :], ACT.Copy).then_inc(mixhi, 1)

    def split_mix_dve(dve):
        for k in range(KT):
            dve.wait_ge(mixhi, k + 1)
            nc.vector.tensor_tensor(a_lo[:, k, :], mix[:, k, :], a_hi[:, k, :].bitcast(F32), ALU.subtract).then_inc(mixlo, 1)

    (dtw_load, dtw_hi, dtw_lo, dtp, dt_v, dt_a, cump, cum_x, dt_ok, tri_load) = (
        sem(n) for n in ("dtw_load", "dtw_hi", "dtw_lo", "dtp", "dt_v", "dt_a", "cump", "cum_x", "dt_ok", "tri_load"))
    xmid, xtap, xsilu = sem("xmid"), sem("xtap"), sem("xsilu")
    (tbp, tbc, txp, xtc, vt_done, stp, hu, h_ready, gp, gl_done, rhs_done, xp, e_x, mlu, v_done) = (
        sem(n) for n in ("tbp", "tbc", "txp", "xtc", "vt_done", "stp", "hu", "h_ready", "gp", "gl_done", "rhs_done", "xp", "e_x", "mlu", "v_done"))
    (intra, inter, comb, ysum, typ, yev, gated, ysq, ysqu, yln, yn, yhi, ylo) = (
        sem(n) for n in ("intra", "inter", "comb", "ysum", "typ", "yev", "gated", "ysq", "ysqu", "yln", "yn", "yhi", "ylo"))
    M = {n: tri[:, i, :] for i, n in enumerate(SSD_CONSTS)}

    def chunk(tile, c):
        return xbc[:, tile, c * P:(c + 1) * P]

    def tbank(c):
        return bank[0 if c % 2 == 0 else 7]

    def heads(buf, c, d, g):
        return buf[:, c, d, HPG * g:HPG * (g + 1)].unsqueeze(2).to_broadcast([P, HPG, HD])

    def wide(ap):
        return ap.rearrange("p (h c) -> p h c", c=HD)

    def dt_pe(pe):
        pe.wait_ge(dtw_lo, 1)
        for j in range(TT):
            for k in range(KT):
                out = bank[5][:, j * 2 * SH:(j + 1) * 2 * SH]
                xh, xl = a_hi[:, k, j * P:(j + 1) * P], a_lo[:, k, j * P:(j + 1) * P]
                nc.tensor.matmul(out, xh, wdt_hi[:, k, :], start=k == 0, stop=False)
                nc.tensor.matmul(out, xh, wdt_lo[:, k, :], start=False, stop=False)
                mm = nc.tensor.matmul(out, xl, wdt_hi[:, k, :], start=False, stop=k == KT - 1)
        mm.then_inc(dtp, 1)

    def dt_act(act):
        act.wait_ge(dt_v, 1)
        nc.scalar.activation(dtmp[:, 1, :], dtmp[:, 0, :], ACT.Exp).then_inc(dt_a, 1)
        nc.scalar.activation(aneg[:, :], par[:, PCOL["a_log"]:PCOL["a_log"] + 2 * SH], ACT.Exp).then_inc(dt_a, 1)
        act.wait_ge(dt_v, 2)
        nc.scalar.activation(dtmp[:, 3, :], dtmp[:, 2, :], ACT.Ln).then_inc(dt_a, 1)

    def dt_dve(dve):
        dve.wait_ge(dtp, 1)
        v = dtv[:, :, :, :].rearrange("p j d h -> p (j d h)")
        bias = par[:, PCOL["dt_bias"]:PCOL["dt_bias"] + 2 * SH].unsqueeze(1).to_broadcast([P, TT, 2 * SH])
        link("dve", dve, nc.vector.tensor_tensor(v.rearrange("p (j n) -> p j n", j=TT),
                                                 bank[5][:, 0:TT * 2 * SH].rearrange("p (j n) -> p j n", j=TT), bias, ALU.add))
        nc.vector.tensor_scalar(dtmp[:, 0, :], v, 30.0, None, ALU.min).then_inc(dt_v, 1)
        dve.wait_ge(dt_a, 2)
        nc.vector.tensor_scalar(dtmp[:, 2, :], dtmp[:, 1, :], 1.0, None, ALU.add).then_inc(dt_v, 1)
        dve.wait_ge(dt_a, 3)
        log1p_fix(dve, dtmp[:, 1, :], dtmp[:, 2, :], dtmp[:, 3, :], dtmp[:, 0, :])
        link("dve", dve, nc.vector.tensor_tensor(v, v, dtmp[:, 3, :], ALU.max))
        link("dve", dve, nc.vector.tensor_scalar(dtmp[:, 0, :], v, -1.0, None, ALU.mult))
        nc.vector.tensor_tensor(da[:, :, :, :].rearrange("p j d h -> p j (d h)"), dtmp[:, 0, :].rearrange("p (j n) -> p j n", j=TT),
                                aneg[:, :].unsqueeze(1).to_broadcast([P, TT, 2 * SH]), ALU.mult).then_inc(dt_ok, 1)

    def cum_pe(pe):
        pe.wait_ge(dt_ok, 1)
        pe.wait_ge(tri_load, 16)
        for half, (mf, mb) in enumerate((("gt", "lt"), ("le", "ge"))):
            out = bank[6][:, 256 * half:256 * (half + 1)].rearrange("p (c d h) -> p c d h", c=TT, d=2)
            nc.tensor.matmul(out[:, :, 0, :], M[mf], da[:, :, 0, :], start=True, stop=True)
            nc.tensor.matmul(out[:, :, 1, :], M[mb], da[:, :, 1, :], start=True, stop=True)
        nc.tensor.matmul(bank[7][:, 0:256], C["ones"], da[:, :, :, :].rearrange("p c d h -> p (c d h)"), start=True, stop=True).then_inc(cump, 1)

    def cum_act(act):
        act.wait_ge(cump, 1)
        for dst, src in ((dtt, bank[6][:, 0:256]), (cume, bank[6][:, 256:512]), (tote, bank[7][:, 0:256])):
            nc.scalar.activation(dst[:, :, :, :].rearrange("p c d h -> p (c d h)"), src, ACT.Exp).then_inc(cum_x, 1)

    def ssd_pe(pe):
        pe.wait_ge(cum_x, 3)

        def exponents(g, c):
            n = TT * g + c
            if c:
                pe.wait_ge(gl_done, n)
            else:
                pe.wait_ge(tbc, g + 1)
                if g:
                    pe.wait_ge(yn, 4 * g)
            nc.tensor.matmul(bank[1][:, 0:P], chunk(B_TILE + g, c), chunk(C_TILE + g, c), start=True, stop=True).then_inc(gp, 1)
            for hf in range(2):
                q = 2 * n + hf
                pe.wait_ge(rhs_done, q + 1)
                if q >= 2:
                    pe.wait_ge(e_x, q - 1)
                out = bank[2 + hf][:, :]
                nc.tensor.matmul(out, M["gt"], erhs[:, hf, 0, :, :].rearrange("p h t -> p (h t)"), start=True, stop=False)
                nc.tensor.matmul(out, M["lt"], erhs[:, hf, 1, :, :].rearrange("p h t -> p (h t)"), start=False, stop=True).then_inc(xp, 1)

        def between(g, c):
            n = TT * g + c
            pe.wait_ge(comb, n) if c else pe.wait_ge(h_ready, g + 1)
            if c > 0:
                mm = nc.tensor.matmul(bank[5][:, :], chunk(C_TILE + g, c), hst[:, 0, c - 1, :], start=True, stop=True)
            if c < TT - 1:
                mm = nc.tensor.matmul(bank[6][:, :], chunk(C_TILE + g, c), hst[:, 1, c, :], start=True, stop=True)
            mm.then_inc(inter, 1)

        def inside(g, c):
            n = TT * g + c
            pe.wait_ge(mlu, 2 * n + 2)
            pe.wait_ge(v_done, n + 1)
            if n:
                pe.wait_ge(ysum, n)
            for h in range(HPG):
                out = bank[4][:, h * HD:(h + 1) * HD]
                nc.tensor.matmul(out, mw[c % 2][:, h // 4, h % 4, :], vfb[:, 0, h * HD:(h + 1) * HD], start=True, stop=False)
                mm = nc.tensor.matmul(out, ew[c % 2][:, h // 4, h % 4, :], vfb[:, 1, h * HD:(h + 1) * HD], start=False, stop=True)
            mm.then_inc(intra, 1)

        def turn_y(g, c):
            n = TT * g + c
            pe.wait_ge(ysum, n + 1)
            if c >= 2:
                pe.wait_ge(yev, n - 1)
            for i in range(4):
                mm = nc.tensor.transpose(tbank(c)[:, i * P:(i + 1) * P], y_one[:, c % 2, i * P:(i + 1) * P], C["ident"])
            mm.then_inc(typ, 1)

        def turn_x(g, c):
            n = TT * g + c
            if c < 2 and g:
                pe.wait_ge(yev, TT * g)
            if c >= 2:
                pe.wait_ge(vt_done, n - 1)
            for i in range(4):
                mm = nc.tensor.transpose(tbank(c)[:, i * P:(i + 1) * P], chunk(4 * g + i, c), C["ident"])
            mm.then_inc(txp, 1)

        def states(g, c):
            n = TT * g + c
            pe.wait_ge(vt_done, n + 1)
            if c == 0 and g:
                pe.wait_ge(comb, n)
            if c:
                pe.wait_ge(hub, n)
            if c == 2:
                pe.wait_ge(hu, 2 * g + 1)
            if c < TT - 1:
                mm = nc.tensor.matmul(bank[5][:, :], btok[:, c, :], vtl[c % 2][:, 0, :], start=True, stop=True)
            if c > 0:
                mm = nc.tensor.matmul(bank[6][:, :], btok[:, c, :], vtl[c % 2][:, 1, :], start=True, stop=True)
            mm.then_inc(stp, 1)

        def norm_sums(g):
            for i in range(4):
                pe.wait_ge(ysq, 4 * g + i + 1)
                nc.tensor.matmul(bank[1][:, :], C["ones"], sq_c[g][i % 2][:, :], start=i == 0, stop=i == 3).then_inc(ysqu, 1)

        for g in range(SG):
            if g:
                pe.wait_ge(gl_done, TT * g)
            for c in range(TT):
                mm = nc.tensor.transpose(bank[1][:, c * P:(c + 1) * P], chunk(B_TILE + g, c), C["ident"])
            mm.then_inc(tbp, 1)
            turn_x(g, 0)
            turn_x(g, 1)
            pe.wait_ge(tbc, g + 1)
            for c in range(TT):
                states(g, c)
                if c + 2 < TT:
                    turn_x(g, c + 2)
            if g:
                norm_sums(g - 1)
            exponents(g, 0)
            between(g, 0)
            for c in range(TT):
                if c + 1 < TT:
                    exponents(g, c + 1)
                inside(g, c)
                if c + 1 < TT:
                    between(g, c + 1)
                if c:
                    turn_y(g, c - 1)
            turn_y(g, TT - 1)
        pe.wait_ge(gl_done, SG * TT)
        norm_sums(SG - 1)

    def ssd_act(act):
        def token_major(g, c):
            n = TT * g + c
            act.wait_ge(txp, n + 1)
            if g and c == 0:
                act.wait_ge(v_done, TT * g)
            nc.scalar.activation(xtok[:, c, :], tbank(c)[:, :], ACT.Copy).then_inc(xtc, 1)

        def roots(g):
            for i in range(4):
                k = 4 * g + i
                act.wait_ge(gated, k + 1)
                if i >= 2:
                    act.wait_ge(ysqu, k - 1)
                nc.scalar.activation(sq_c[g][i % 2][:, :], xbc[:, k, :], ACT.Square).then_inc(ysq, 1)
            act.wait_ge(ysqu, 4 * (g + 1))
            nc.scalar.activation(nrm_c[g][:, 0, :], bank[1][:, :], ACT.Ln, scale=1.0 / GW, bias=eps_col[:, :]).then_inc(yln, 1)
            act.wait_ge(yln, 2 * g + 1)
            nc.scalar.activation(nrm_c[g][:, 1, :], nrm_c[g][:, 0, :], ACT.Exp, scale=-0.5).then_inc(yln, 1)

        def high(g):
            act.wait_ge(yn, 4 * (g + 1))
            for i in range(4):
                k = 4 * g + i
                nc.scalar.activation(y_hi[:, k, :], xbc[:, k, :], ACT.Copy).then_inc(yhi, 1)

        for g in range(SG):
            act.wait_ge(tbp, g + 1)
            if g:
                act.wait_ge(stp, TT * g)
            nc.scalar.activation(btok[:, :, :].rearrange("p c n -> p (c n)"), bank[1][:, :], ACT.Copy).then_inc(tbc, 1)
            token_major(g, 0)
            token_major(g, 1)
            for c in range(TT):
                n = TT * g + c
                act.wait_ge(stp, n + 1)
                if c == 0:
                    if g:
                        act.wait_ge(inter, n)
                    nc.scalar.activation(hst[:, 0, 0, :], bank[5][:, :], ACT.Copy).then_inc(hub, 1)
                else:
                    nc.scalar.activation(hst[:, 1, c - 1, :], bank[6][:, :], ACT.Copy).then_inc(hub, 1)
                if c + 2 < TT:
                    token_major(g, c + 2)
            if g:
                roots(g - 1)
            for c in range(TT):
                n = TT * g + c
                for hf in range(2):
                    q = 2 * n + hf
                    act.wait_ge(xp, q + 1)
                    if n >= 2 and hf == 0:
                        act.wait_ge(intra, n - 1)
                    nc.scalar.activation(ew[c % 2][:, hf, :, :].rearrange("p h t -> p (h t)"), bank[2 + hf][:, :], ACT.Exp).then_inc(e_x, 1)
                if c == 1 and g:
                    high(g - 1)
        roots(SG - 1)
        high(SG - 1)

    def ssd_pool(pool):
        pool.wait_ge(dt_ok, 1)
        pool.wait_ge(tri_load, 16)
        pool.wait_ge(dt_fin, 1)

        def operands(g, c):
            for hf in range(2):
                q = 2 * (TT * g + c) + hf
                if q >= 2:
                    pool.wait_ge(xp, q - 1)
                for d, m in enumerate(("le", "ge")):
                    h0 = HPG * g + 4 * hf
                    t = nc.gpsimd.tensor_tensor(erhs[:, hf, d, :, :], M[m].unsqueeze(1).to_broadcast([P, 4, P]),
                                                da[:, c, d, h0:h0 + 4].unsqueeze(2).to_broadcast([P, 4, P]), ALU.mult)
                t.then_inc(rhs_done, 1)

        def stepped(g, c):
            n = TT * g + c
            pool.wait_ge(xtc, n + 1)
            if n:
                pool.wait_ge(intra, n)
            for d in range(2):
                t = nc.gpsimd.tensor_tensor(wide(vfb[:, d, :]), wide(xtok[:, c, :]), heads(dtv, c, d, g), ALU.mult)
            t.then_inc(v_done, 1)
        for g in range(SG):
            operands(g, 0)
            for c in range(TT):
                if c + 1 < TT:
                    operands(g, c + 1)
                stepped(g, c)
            pool.wait_ge(yev, TT * (g + 1))
            for i in range(4):
                k = 4 * g + i
                nc.gpsimd.tensor_tensor(xbc[:, k, :], xbc[:, k, :], zt[:, k, :], ALU.mult).then_inc(gated, 1)

    def ssd_dve(dve):
        dve.wait_ge(cum_x, 3)
        nc.vector.tensor_tensor(dtt[:, :, :, :].rearrange("p c d h -> p (c d h)"), dtt[:, :, :, :].rearrange("p c d h -> p (c d h)"),
                                dtv[:, :, :, :].rearrange("p c d h -> p (c d h)"), ALU.mult).then_inc(dt_fin, 1)
        dve.wait_ge(dt_fin, 1)

        def grow(state, d, c, g):
            return nc.vector.tensor_tensor(wide(htmp[:, :]), wide(hst[:, d, state, :]), heads(tote, c, d, g), ALU.mult)

        def tailed(g, c):
            n = TT * g + c
            dve.wait_ge(xtc, n + 1)
            if n >= 2:
                dve.wait_ge(stp, n - 1)
            if c == 0 and g:
                dve.wait_ge(typ, n)
            for d in range(2):
                t = nc.vector.tensor_tensor(wide(vtl[c % 2][:, d, :]), wide(tbank(c)[:, :]), heads(dtt, c, d, g), ALU.mult)
            t.then_inc(vt_done, 1)

        def roots(g):
            dve.wait_ge(yln, 2 * g + 2)
            refine(dve, bank[1][:, :], 1.0 / GW, nrm_c[g][:, 1, :], nrm_c[g][:, 2, :], nrm_c[g][:, 0, :])
            for i in range(4):
                k = 4 * g + i
                nc.vector.scalar_tensor_tensor(out=xbc[:, k, :], in0=xbc[:, k, :], scalar=pcol("ssd_g", k), in1=nrm_c[g][:, 1, :],
                                               op0=ALU.mult, op1=ALU.mult).then_inc(yn, 1)

        def low(g):
            for i in range(4):
                k = 4 * g + i
                dve.wait_ge(yhi, k + 1)
                nc.vector.tensor_tensor(y_lo[:, k, :], xbc[:, k, :], y_hi[:, k, :].bitcast(F32), ALU.subtract).then_inc(ylo, 1)

        def masked(g, c):
            n = TT * g + c
            dve.wait_ge(gp, n + 1)
            gm = gmask[:, c % 2, :, :]
            nc.vector.tensor_tensor(gm[:, 0, :], bank[1][:, 0:P], M["le"], ALU.mult)
            nc.vector.tensor_tensor(gm[:, 1, :], bank[1][:, 0:P], M["gt"], ALU.mult).then_inc(gl_done, 1)
            dve.wait_ge(gl_done, n + 1)
            for hf in range(2):
                dve.wait_ge(e_x, 2 * n + hf + 1)
                link("dve", dve, nc.vector.tensor_tensor(mw[c % 2][:, hf, :, :], ew[c % 2][:, hf, :, :],
                                                         gm[:, 0:1, :].to_broadcast([P, 4, P]), ALU.mult))
                nc.vector.tensor_tensor(ew[c % 2][:, hf, :, :], ew[c % 2][:, hf, :, :],
                                        gm[:, 1:2, :].to_broadcast([P, 4, P]), ALU.mult).then_inc(mlu, 1)

        def evac_y(g, c):
            dve.wait_ge(typ, TT * g + c + 1)
            for i in range(4):
                k = 4 * g + i
                t = nc.vector.scalar_tensor_tensor(out=chunk(k, c), in0=chunk(k, c), scalar=pcol("d_skip", k),
                                                   in1=tbank(c)[:, i * P:(i + 1) * P], op0=ALU.mult, op1=ALU.add)
            t.then_inc(yev, 1)

        for g in range(SG):
            tailed(g, 0)
            for c in range(TT):
                if c + 1 < TT:
                    tailed(g, c + 1)
                if 0 < c < TT - 1:
                    dve.wait_ge(hub, TT * g + 1)
                    link("dve", dve, grow(c - 1, 0, c, g))
                    dve.wait_ge(stp, TT * g + c + 1)
                    nc.vector.tensor_tensor(hst[:, 0, c, :], htmp[:, :], bank[5][:, :], ALU.add).then_inc(hu, 1)
                    dve.wait_ge(hu, 2 * g + c)
            dve.wait_ge(hub, TT * (g + 1))
            for c in (2, 1):
                link("dve", dve, grow(c, 1, c, g))
                t = nc.vector.tensor_tensor(hst[:, 1, c - 1, :], hst[:, 1, c - 1, :], htmp[:, :], ALU.add)
                if c == 2:
                    link("dve", dve, t)
            t.then_inc(h_ready, 1)
            if g:
                roots(g - 1)
            masked(g, 0)
            for c in range(TT):
                n = TT * g + c
                if c + 1 < TT:
                    masked(g, c + 1)
                dve.wait_ge(inter, n + 1)
                if c >= 2:
                    dve.wait_ge(typ, n - 1)
                y1, y2 = y_one[:, c % 2, :], y_two[:, c % 2, :]
                if c > 0:
                    t = nc.vector.tensor_tensor(wide(y1), wide(bank[5][:, :]), heads(cume, c, 0, g), ALU.mult)
                if c < TT - 1:
                    t = nc.vector.tensor_tensor(wide(y2 if c else y1), wide(bank[6][:, :]), heads(cume, c, 1, g), ALU.mult)
                t.then_inc(comb, 1)
                dve.wait_ge(comb, n + 1)
                if 0 < c < TT - 1:
                    link("dve", dve, nc.vector.tensor_tensor(y1, y1, y2, ALU.add))
                dve.wait_ge(intra, n + 1)
                nc.vector.tensor_tensor(y1, y1, bank[4][:, :], ALU.add).then_inc(ysum, 1)
                if c:
                    evac_y(g, c - 1)
                if c == 2 and g:
                    low(g - 1)
            evac_y(g, TT - 1)
        roots(SG - 1)
        low(SG - 1)

    dt_fin, hub = sem("dt_fin"), sem("hub")

    def tile_of(buf, i, j):
        return buf[:, 4 * i + j, :] if isinstance(i, int) else buf[:, bass.ds(4 * i + j, 1), :].rearrange("p a t -> p (a t)")

    def z_take(i, j, done):
        act_.wait_ge(slot_done, done)
        nc.scalar.activation(tile_of(zt, i, j), bank[j][:, :], ACT.Silu).then_inc(evac[j], 1)

    def xbc_act(i, j, done):
        def silu(jj):
            act_.wait_ge(evac[jj], i + PLAN["xbc"]["tile0"] // 4 + 1)
            nc.scalar.activation(tile_of(xbc, i, jj), cv[:, jj, :], ACT.Silu).then_inc(xsilu, 1)
        act_.wait_ge(slot_done, done)
        nc.scalar.activation(cv[:, j, :], bank[j][:, :], ACT.Identity, scale=col("conv_w", 5, i, j, 2),
                             bias=col("conv_b", 1, i, j)).then_inc(xmid, 1)
        if j:
            silu(j - 1)
        if j == 3:
            silu(3)

    def xbc_dve(i, j, done):
        dve_.wait_ge(xmid, 4 * i + j + 1)
        for n, (tap, by) in enumerate(((0, -2), (1, -1), (3, 1), (4, 2))):
            a, b = max(0, -by), S - max(0, by)
            dst = cv[:, j, a:b]
            if n:
                dve_.wait_ge(xtap, 12 * i + 3 * j + n)
            nc.vector.scalar_tensor_tensor(out=dst, in0=bank[j][:, a + by:b + by], scalar=col("conv_w", 5, i, j, tap), in1=dst,
                                           op0=ALU.mult, op1=ALU.add).then_inc(evac[j] if n == 3 else xtap, 1)

    @block.sync
    def _(sp_):
        sp_.dma_start(memx[:, :, :], dr["memT"]).then_inc(mem_load, 16)
        for name, _, _ in WEIGHTS:
            load_weights(sp_, name)
        sp_.wait_ge(x_done, 8 * X_UPDATES)
        sp_.dma_start(dr["out"], x[:, :, :]).then_inc(out_done, 16)
        sp_.wait_ge(out_done, 16)

    @block.gpsimd
    def _(pool):
        nc.gpsimd.memset(eps_col[:, :], EPS).then_inc(eps_done, 1)
        nc.gpsimd.engine_nop().then_inc(prod, 2)
        pool_pool(pool)
        stick_pool(pool)
        ret_pool(pool)
        na_pool(pool)
        up_pool(pool, 0)
        ssd_pool(pool)
        up_pool(pool, 1)

    @block.scalar
    def _(act):
        act.dma_start(cst[:, :, :], dr["consts"]).then_inc(cst_load, 16)
        act.dma_start(par[:, :], dr["params"]).then_inc(par_load, 16)
        act.dma_start(x[:, :, :], dr["xT"]).then_inc(x_load, 16)
        act.wait_ge(eps_done, 1)
        for s in range(2):
            act.wait_ge(w_load[s], 16)
            nc.scalar.activation(w_hi[:, s, :], raw[:, s, :], ACT.Copy).then_inc(hi_done, 1)
        nc.scalar.preload_act_table_set(LOGEXP)
        act.wait_ge(mem_load, 16)
        pre_norm_act(act, 0, memx, MEM, mem_hi, M_MEM)
        act.wait_ge(x_load, 16)
        pre_norm_act(act, 1, x, S, a_hi, M_IN1)

        def take_kv(i, j, done):
            act.wait_ge(slot_done, done)
            nc.scalar.activation(kv[:, j, :], bank[j][:, 0:MEM], ACT.Copy).then_inc(evac[j], 1)
        product_split(act, "mem_kv", split_hi, take_kv)
        act.wait_ge(slot_done, PLAN["in1"]["slot0"])
        act.dma_start(invc[:, :, :], dr["inv_count"]).then_inc(poolc_load, 16)

        def take_p1(i, j, done):
            if j % 2 == 0:
                act.wait_ge(slot_done, done)
                dst = p1[:, 4 * i + j, :] if isinstance(i, int) else p1[:, bass.ds(4 * i + j, 1), :].rearrange("p a t -> p (a t)")
                nc.scalar.activation(dst, bank[j][:, :], ACT.Copy).then_inc(evac[j], 1)
        product_split(act, "in1", split_hi, take_p1)
        act.wait_ge(evac[1], PLAN["out1"]["tile0"] // 4)
        act.wait_ge(evac[3], PLAN["out1"]["tile0"] // 4)
        act.wait_ge(sem("poolw_zero"), 1)
        for t in range(2):
            for g in range(2):
                act.dma_start(poolw[g * DH:(g + 1) * DH, t, g * DH:(g + 1) * DH], dr["pool_w"][2 * t + g]).then_inc(sem("poolw_load"), 16)
        for t in (POOL_G, POOL_G + 1, SB_G, SB_G + 1, SB_G + 2, SB_G + 3, MEM_G, MEM_G + 1):
            nc.scalar.activation(p1[:, t, :], p1[:, t, :], ACT.Silu).then_inc(silu_done, 1)
        nc.scalar.preload_act_table_set(LOGEXP)
        stick_act(act)
        mem_act(act)
        split_mix_act(act)
        product_split(act, "out1", split_hi, lambda i, j, done: None)
        act.wait_ge(evac[0], PLAN["in2"]["tile0"] // 4)
        act.dma_start(rope[:, :, :], dr["rope"]).then_inc(tab_load, 16)
        act.dma_start(dist[:, :], dr["dist"]).then_inc(dist_load, 16)
        pre_norm_act(act, 2, x, S, a_hi, 16, x_ready(act, 1))
        product_split(act, "in2", split_hi, copy_tiles(p2, 0))
        for j in (1, 3):
            act.wait_ge(evac[j], PLAN["out2"]["tile0"] // 4)
        for t in range(4):
            nc.scalar.activation(p2[:, RET_G + t, :], p2[:, RET_G + t, :], ACT.Silu).then_inc(silu2, 1)
        nc.scalar.preload_act_table_set(LOGEXP)
        ret_act(act)
        na_act(act)
        split_mix2_act(act)
        product_split(act, "out2", split_hi, copy_tiles(m_mix, 0))
        norm_act(act, 3, m_mix, S, tile_ready(act, "out2"))
        pre_norm_act(act, 4, x, S, a_hi, 24, x_ready(act, 2))
        nc.scalar.preload_act_table(ACT.Gelu_apprx_tanh)
        product_split(act, "up0", split_hi, up_act(0))
        product_split(act, "down0", split_hi, copy_tiles(m_ffn, 0))
        norm_act(act, 5, m_ffn, S, tile_ready(act, "down0"), sq_b, nrm_b)
        pre_norm_act(act, 6, x, S, a_hi, 32, x_ready(act, 3))
        act.dma_start(tri[:, :, :], dr["tri"]).then_inc(tri_load, 16)
        act.dma_start(wdt[:, :, :], dr["w_dt"]).then_inc(dtw_load, 16)
        act.wait_ge(dtw_load, 16)
        nc.scalar.activation(wdt_hi[:, :, :], wdt[:, :, :], ACT.Copy).then_inc(dtw_hi, 1)
        nc.scalar.preload_act_table(ACT.Silu)
        product_split(act, "z", split_hi, z_take)
        nc.scalar.preload_act_table_set(LOGEXP)
        dt_act(act)
        nc.scalar.preload_act_table(ACT.Silu)
        act.wait_ge(dt_ok, 1)
        product_split(act, "xbc", split_hi, xbc_act)
        nc.scalar.preload_act_table_set(LOGEXP)
        cum_act(act)
        ssd_act(act)
        product_split(act, "out3", split_hi, copy_tiles(m_ssd, 0))
        norm_act(act, 7, m_ssd, S, tile_ready(act, "out3"), sq_b, nrm_b)
        pre_norm_act(act, 8, x, S, a_hi, 40, x_ready(act, 4))
        nc.scalar.preload_act_table(ACT.Gelu_apprx_tanh)
        product_split(act, "up1", split_hi, up_act(1))
        product_split(act, "down1", split_hi, copy_tiles(m_ffn, 0))
        norm_act(act, 9, m_ffn, S, tile_ready(act, "down1"), sq_b, nrm_b)

    @block.vector
    def _(dve):
        for s in range(2):
            dve.wait_ge(hi_done, s + 1)
            nc.vector.tensor_tensor(w_lo[:, s, :], raw[:, s, :], w_hi[:, s, :].bitcast(F32), ALU.subtract).then_inc(lo_done, 1)
        dve.wait_ge(par_load, 16)
        pre_norm_dve(dve, 0, memx, MEM, "mem_norm_g", mem_hi, mem_lo, M_MEM)
        pre_norm_dve(dve, 1, x, S, "norm_g", a_hi, a_lo, M_IN1)
        product_split(dve, "mem_kv", split_lo, lambda i, j, done: None)

        def take_p1(i, j, done):
            if j % 2 == 1:
                dve.wait_ge(slot_done, done)
                dst = p1[:, 4 * i + j, :] if isinstance(i, int) else p1[:, bass.ds(4 * i + j, 1), :].rearrange("p a t -> p (a t)")
                nc.vector.tensor_copy(dst, bank[j][:, :]).then_inc(evac[j], 1)
        product_split(dve, "in1", split_lo, take_p1)
        dve.wait_ge(evac[0], PLAN["out1"]["tile0"] // 4)
        dve.wait_ge(evac[2], PLAN["out1"]["tile0"] // 4)
        for t in range(4):
            nc.vector.tensor_scalar(p1[:, SB_Q + t, :], p1[:, SB_Q + t, :], DH ** -0.5, None, ALU.mult).then_inc(q_scaled, 1)
        pool_dve(dve)
        dve.wait_ge(silu_done, 8)
        stick_dve(dve)
        mem_dve(dve)
        split_mix_dve(dve)

        def add_x(i, j, done):
            dve.wait_ge(slot_done, done)
            nc.vector.tensor_tensor(x[:, 4 * i + j, :], x[:, 4 * i + j, :], bank[j][:, :], ALU.add).then_inc(evac[j], 1)
        product_split(dve, "out1", split_lo, add_x)
        pre_norm_dve(dve, 2, x, S, "mix_pre0", a_hi, a_lo, 16)
        product_split(dve, "in2", split_lo, copy_tiles(p2, 1))
        dve.wait_ge(silu2, 4)
        ret_dve(dve)
        na_dve(dve)
        split_mix2_dve(dve)
        product_split(dve, "out2", split_lo, copy_tiles(m_mix, 1))
        post_norm_dve(dve, 3, m_mix, "mix_post0")
        pre_norm_dve(dve, 4, x, S, "ffn_pre0", a_hi, a_lo, 24)
        nc.vector.engine_nop().then_inc(glo, 2)
        product_split(dve, "up0", split_lo, up_dve(0))
        product_split(dve, "down0", split_lo, copy_tiles(m_ffn, 1))
        post_norm_dve(dve, 5, m_ffn, "ffn_post0", nrm_b)
        pre_norm_dve(dve, 6, x, S, "mix_pre1", a_hi, a_lo, 32)
        dve.wait_ge(dtw_hi, 1)
        nc.vector.tensor_tensor(wdt_lo[:, :, :], wdt[:, :, :], wdt_hi[:, :, :].bitcast(F32), ALU.subtract).then_inc(dtw_lo, 1)
        product_split(dve, "z", split_lo, lambda i, j, done: None)
        dt_dve(dve)
        product_split(dve, "xbc", split_lo, xbc_dve)
        ssd_dve(dve)
        product_split(dve, "out3", split_lo, copy_tiles(m_ssd, 1))
        post_norm_dve(dve, 7, m_ssd, "mix_post1", nrm_b)
        pre_norm_dve(dve, 8, x, S, "ffn_pre1", a_hi, a_lo, 40)
        product_split(dve, "up1", split_lo, up_dve(1))
        product_split(dve, "down1", split_lo, copy_tiles(m_ffn, 1))
        post_norm_dve(dve, 9, m_ffn, "ffn_post1", nrm_b)

    @block.tensor
    def _(pe):
        pe.wait_ge(cst_load, 16)
        norm_pe(pe, 0, MEM)
        pe.wait_ge(h_done, M_MEM + 1)
        norm_pe(pe, 1, S)
        pe.wait_ge(alo_done, M_MEM + 8)
        product_pe(pe, "mem_kv", mem_hi, mem_lo, MEM)
        pe.wait_ge(alo_done, M_IN1 + 8)
        product_pe(pe, "in1", a_hi, a_lo)
        for b in range(4):
            pe.wait_ge(evac[b], PLAN["out1"]["tile0"] // 4)
        pool_pe(pe)
        pe.wait_ge(pool_y, 2)
        stick_pe(pe)
        mem_pe(pe)
        pe.wait_ge(my_read, MEM_HEADS)
        pe.wait_ge(mixlo, 8)
        product_pe(pe, "out1", a_hi, a_lo)
        norm_pe(pe, 2, S)
        pe.wait_ge(alo_done, 24)
        product_pe(pe, "in2", a_hi, a_lo)
        for b in range(4):
            pe.wait_ge(evac[b], PLAN["out2"]["tile0"] // 4)
        ret_pe(pe)
        na_pe(pe)
        pe.wait_ge(mixlo, 2 * KT)
        product_pe(pe, "out2", a_hi, a_lo)
        norm_pe(pe, 3, S)
        norm_pe(pe, 4, S)
        pe.wait_ge(alo_done, 32)
        product_pe(pe, "up0", a_hi, a_lo)
        pe.wait_ge(glo, FT + 2)
        product_pe(pe, "down0", g_hi, g_lo)
        norm_pe(pe, 5, S, sq_b)
        norm_pe(pe, 6, S)
        pe.wait_ge(alo_done, 40)
        dt_pe(pe)
        product_pe(pe, "z", a_hi, a_lo)
        product_pe(pe, "xbc", a_hi, a_lo)
        for b in range(4):
            pe.wait_ge(evac[b], PLAN["out3"]["tile0"] // 4)
        pe.wait_ge(xsilu, 24)
        cum_pe(pe)
        ssd_pe(pe)
        pe.wait_ge(ylo, 16)
        product_pe(pe, "out3", y_hi, y_lo)
        norm_pe(pe, 7, S, sq_b)
        norm_pe(pe, 8, S)
        pe.wait_ge(alo_done, 48)
        product_pe(pe, "up1", a_hi, a_lo)
        pe.wait_ge(glo, 2 * FT + 2)
        product_pe(pe, "down1", g_hi, g_lo)
        norm_pe(pe, 9, S, sq_b)


def blocks(w):
    k, n = w.shape
    return np.ascontiguousarray(w.reshape(k // P, P, n // P, P).transpose(2, 1, 0, 3).reshape(n // P, P, k))


def features(v):
    return np.ascontiguousarray(v.reshape(-1, P).T)


def rotation_tables():
    half = DH // 2
    inv = (1.0 / (np.float32(10000.0) ** (np.arange(half, dtype=np.float32) / np.float32(half)))).astype(np.float32)
    ang = np.arange(S, dtype=np.float32)[None, :] * inv[np.arange(P) % half][:, None]
    return np.ascontiguousarray(np.stack([np.cos(ang), np.sin(ang)], 1).astype(np.float32))


def swap_matrix():
    m = np.zeros((P, P), np.float32)
    for j in range(P):
        if j % DH < DH // 2:
            m[j + DH // 2, j] = -1
        else:
            m[j - DH // 2, j] = 1
    return m


def distances():
    return (np.arange(STRIP)[None, :] - (S - P) - np.arange(P)[:, None]).astype(np.float32)


def column_mask():
    out = np.full((P, 4, KEYW), NEG, np.float32)
    for c in range(4):
        first = min(max(QB * c - WIN_C // 2, 0), GRID_W - KEYW)
        for p in range(P):
            q = QB * c + p % QB
            a = min(max(q - WIN_C // 2, 0), GRID_W - WIN_C) - first
            out[p, c, a:a + WIN_C] = 0
    return out


def interleave(a):
    k = a.shape[:-1]
    return np.ascontiguousarray(a.reshape(*k, 2, FT, P).swapaxes(-3, -2).reshape(*k, 2 * FFN))


def taps(w):
    return np.ascontiguousarray(w.reshape(w.shape[0], -1, P).transpose(2, 1, 0).reshape(P, -1))


def constants():
    i = np.arange(P)
    c = {
        "ident": np.eye(P), "ones": np.ones((P, P)), "ones64": (i[:, None] // DH == i[None, :] // DH),
        "neg_tri": -(i[:, None] >= i[None, :]).astype(np.float32), "neg_ones": -np.ones((P, P)),
        "swap": swap_matrix(),
    }
    return np.ascontiguousarray(np.stack([c[n].astype(np.float32) for n in CONSTS], 1))


def triangles():
    r, c = np.arange(P)[:, None], np.arange(P)[None, :]
    return np.ascontiguousarray(np.stack([r > c, r < c, r <= c, r >= c], 1).astype(np.float32))


def inv_count():
    out = np.zeros((P, 2, S), np.float32)
    t = np.arange(S)
    for g, w in enumerate((2, 4, 8, 16)):
        out[(g % 2) * DH:(g % 2 + 1) * DH, g // 2] = 1.0 / np.minimum(t + 1, w)
    return out


def kernel(**inp):
    import concourse.bacc as bacc
    from concourse.bass_utils import run_bass_kernel_spmd

    a = {k: np.asarray(v) for k, v in inp.items()}
    par = {
        "norm_g": features(a["norm_g"][0]), "mem_norm_g": features(a["mem_norm_g"][0]),
        "pool_scale": features(a["pool_scale"][0]),
        "q_norm_g": np.concatenate([a["q_norm_g"][0]] * 2)[:, None], "k_norm_g": np.concatenate([a["k_norm_g"][0]] * 2)[:, None],
    }
    for l in range(2):
        for n in ("mix_pre", "mix_post", "ffn_pre", "ffn_post"):
            par[f"{n}{l}"] = features(a[f"norm_{n}_2"][l])
        par[f"ffn_w{l}"] = taps(interleave(a["ffn_conv_w_2"][l]))
        par[f"ffn_b{l}"] = features(interleave(a["ffn_conv_b_2"][l]))
    par["conv_w"], par["conv_b"] = taps(a["c_conv_w_2"][0]), features(a["c_conv_b_2"][0])
    par["d_skip"] = features(np.repeat(a["c_d_skip_2"][0], HD))
    par["ssd_g"] = features(a["c_norm_g_2"][0])
    par["dt_bias"] = np.broadcast_to(a["c_dt_bias_2"][0].reshape(1, -1), (P, 2 * SH))
    par["a_log"] = np.broadcast_to(a["c_a_log_2"][0].reshape(1, -1), (P, 2 * SH))
    w_in3, inner = a["c_w_in_2"][0], SH * HD
    conv = inner + 2 * SG * NS
    par["ret_gn_g"] = features(a["ab_ret_gn_g_2"][0])
    par["decay"] = np.broadcast_to(a["ab_ret_decay_logit_2"][0].reshape(1, 16), (P, 16))
    rpb = np.zeros((NH, 2 * ROWS - 1, RPB_W), np.float32)
    rpb[:, :, WIN_C:WIN_C + 2 * WIN_C - 1] = a["ab_na_rpb_2"][0]
    rpb = np.stack([[rpb[h].reshape(-1)[(ROWS - 1 - r) * RPB_W + QB - 1 - q:][:BIAS_RUN] for r in range(ROWS) for q in range(QB)]
                    for h in range(NH)])
    arrays = {
        "rope": rotation_tables(), "dist": distances(), "col_mask": column_mask(), "rpb": rpb,
        "w_in2": blocks(a["ab_w_in_2"][0]), "w_out2": blocks(a["ab_w_out_2"][0]),
        "w_z": blocks(w_in3[:, :inner]), "w_xbc": blocks(w_in3[:, inner:inner + conv]),
        "w_dt": np.ascontiguousarray(w_in3[:, inner + conv:].reshape(KT, P, 2 * SH).transpose(1, 0, 2)),
        "w_out3": blocks(a["c_w_out_2"][0]), "tri": triangles(),
        "w_up1": blocks(interleave(a["ffn_w_up_2"][1])), "w_down1": blocks(a["ffn_w_down_2"][1]),
        "w_up0": blocks(interleave(a["ffn_w_up_2"][0])), "w_down0": blocks(a["ffn_w_down_2"][0]),
        "xT": np.ascontiguousarray(a["x"][0].reshape(S, KT, P).transpose(2, 1, 0)),
        "memT": np.ascontiguousarray(a["mem"][0].reshape(MEM, KT, P).transpose(2, 1, 0)),
        "consts": constants(), "inv_count": inv_count(),
        "params": np.ascontiguousarray(np.concatenate([par[n] for n, _ in PARAMS], 1)),
        "pool_w": a["pool_w"][0],
        "w_mem_kv": blocks(a["w_mem_kv"][0]), "w_in1": blocks(a["w_in"][0]), "w_out1": blocks(a["w_out"][0]),
    }
    nc = bacc.Bacc("TRN2", target_bir_lowering=False, num_devices=1)
    dr = {k: nc.dram_tensor("in_" + k, v.shape, F32, kind="ExternalInput").ap() for k, v in arrays.items()}
    dr["out"] = nc.dram_tensor("out", (P, KT, S), F32, kind="ExternalOutput").ap()
    program(nc, dr)
    r = run_bass_kernel_spmd(nc, [{"in_" + k: v for k, v in arrays.items()}], core_ids=[0])
    out = r.results[0]["out"]
    return np.ascontiguousarray(out.transpose(2, 1, 0).reshape(1, S, D))
```

```python
import numpy as np
from contextlib import ExitStack

import concourse.bass as bass
from concourse import mybir

ACT = mybir.ActivationFunctionType
ALU = mybir.AluOpType
AX = mybir.AxisListType
F32 = mybir.dt.float32
F32R = mybir.dt.float32r

P = 128
D = 1024
S = 512
KT = D // P
TT = S // P
EPS = 1e-6
LOGEXP = "natural_log_exp_and_others"

MEM = 256
DH = 64
SB_HEADS = 8
MEM_HEADS = 4
IN1_TILES = 24
POOL_V, POOL_G, SB_Q, SB_K, SB_V, SB_G, MEM_Q, MEM_G = 0, 2, 4, 8, 12, 16, 20, 22

WEIGHTS = [
    ("mem_kv", 4, [8]),
    ("in1", IN1_TILES, [8]),
    ("out1", 8, [8]),
    ("in2", 28, [8]),
    ("out2", 8, [8]),
    ("up0", 44, [8]),
    ("down0", 8, [8, 8, 6]),
    ("z", 16, [8]),
    ("xbc", 24, [8]),
    ("out3", 8, [8, 8]),
    ("up1", 44, [8]),
    ("down1", 8, [8, 8, 6]),
]
RING = 4


def stream_plan():
    slot, tile, plan = 0, 0, {}
    for name, tiles, blocks in WEIGHTS:
        plan[name] = dict(tiles=tiles, blocks=blocks, slot0=slot, tile0=tile, last=name == WEIGHTS[-1][0])
        slot += tiles * len(blocks)
        tile += tiles
    return plan


PLAN = stream_plan()

PARAMS = [("norm_g", 8), ("mem_norm_g", 8), ("pool_scale", 2), ("q_norm_g", 1), ("k_norm_g", 1),
          ("mix_pre0", 8), ("mix_post0", 8), ("ffn_pre0", 8), ("ffn_post0", 8), ("ret_gn_g", 4), ("decay", 16),
          ("ffn_w0", 132), ("ffn_b0", 44),
          ("mix_pre1", 8), ("mix_post1", 8), ("ffn_pre1", 8), ("ffn_post1", 8), ("ffn_w1", 132), ("ffn_b1", 44),
          ("conv_w", 120), ("conv_b", 24), ("d_skip", 16), ("ssd_g", 16), ("dt_bias", 64), ("a_log", 64)]
PCOL = {}
for _name, _n in PARAMS:
    PCOL[_name] = sum(n for _, n in PARAMS[:len(PCOL)])
NPAR = sum(n for _, n in PARAMS)

RH = NH = 8
GRID_W = 64
ROWS = S // GRID_W
QB, WIN_C = 16, 16
KEYW = QB + WIN_C
RET_Q, RET_K, RET_V, RET_G, NA_Q, NA_K, NA_V = 0, 4, 8, 12, 16, 20, 24
STRIP = 2 * S - P
RPB_W = 64
BIAS_RUN = (ROWS - 1) * RPB_W + KEYW + QB
NEG = -1e30
X_UPDATES = 4
FFN = 2816
FT = FFN // P

SG, HPG, HD, NS = 4, 8, 64, 128
SH = SG * HPG
XS_TILES = SH * HD // P
B_TILE, C_TILE = XS_TILES, XS_TILES + SG
GW = HPG * HD
SSD_CONSTS = ["gt", "lt", "le", "ge"]

CONSTS = ["ident", "ones", "ones64", "neg_tri", "neg_ones", "swap"]
KB = 1024


def program(nc, dr):
    ctx = ExitStack()
    with ctx:
        start = -(-nc.sbuf_base // 32) * 32
        ctx.enter_context(nc.sbuf_tensor("slab", [P, 207 * 256], F32))
        build(nc, dr, ctx, start)


def build(nc, dr, ctx, start):
    sems = {}

    def sem(name):
        if name not in sems:
            sems[name] = ctx.enter_context(nc.semaphore(name))
        return sems[name]

    def at(name, shape, kb, dt=F32):
        return nc.alloc_sbuf_tensor_at(name, shape, dt, offset=start + int(kb * KB))

    x = at("x", [P, KT, S], 0)
    raw = at("raw", [P, RING, 8 * P], 16)
    w_hi = at("w_hi", [P, RING, 8 * P], 32, F32R)
    w_lo = at("w_lo", [P, RING, 8 * P], 48, F32R)
    a_hi = at("a_hi", [P, KT, S], 64, F32R)
    a_lo = at("a_lo", [P, KT, S], 80, F32R)
    cst = at("cst", [P, len(CONSTS), P], 96)
    par = at("par", [P, NPAR], 99)
    C = {n: cst[:, i, :] for i, n in enumerate(CONSTS)}

    def pcol(name, k=0):
        return par[:, PCOL[name] + k:PCOL[name] + k + 1]

    ST = 104
    p2 = at("p2", [P, 28, S], ST)
    vt2 = at("vt2", [P, TT, RH * DH], ST + 56)
    aw2 = at("aw2", [P, 2, TT, S], ST + 64)
    strip = at("strip", [P, 2, STRIP], ST + 80)
    dist = at("dist", [P, STRIP], ST + 87)
    rope = at("rope", [P, 2, S], ST + 90.5)
    rtmp = at("rtmp", [P, 2, S], ST + 94.5)
    dec = at("dec", [P, 5, 16], ST + 98.5)
    gsq = at("gsq", [P, 4, S], 80)
    grs = at("grs", [P, 4, S], 88)
    ghalf = at("ghalf", [P, S], ST + 94.5)
    vna = at("vna", [P, 4, 2, NH * DH], ST + 64)
    bt = at("bt", [P, 2, ROWS, RPB_W], ST + 80)
    bm = at("bm", [P, 2, 4, ROWS, KEYW], ST + 84)
    cmask = at("cmask", [P, 4, KEYW], ST + 92)
    nprob = at("nprob", [P, 2, 2, ROWS * KEYW], ST + 92.5)
    npt = at("npt", [P, 2, 4, P], ST + 96.5)
    nstat = at("nstat", [P, 4, 32], ST + 100.5)
    nvw = at("nvw", [P, 4, 4, ROWS * KEYW], 64)
    m_mix = at("m_mix", [P, KT, S], ST)
    zt = at("zt", [P, XS_TILES, S], ST)
    xbc = at("xbc", [P, 24, S], ST + 32)
    tri = at("tri", [P, 4, P], ST + 80)
    da = at("da", [P, TT, 2, SH], ST + 82)
    dtv = at("dtv", [P, TT, 2, SH], ST + 83)
    dtt = at("dtt", [P, TT, 2, SH], ST + 84)
    cume = at("cume", [P, TT, 2, SH], ST + 85)
    tote = at("tote", [P, TT, 2, SH], ST + 86)
    wdt = at("wdt", [P, KT, 2 * SH], ST + 87)
    wdt_hi = at("wdt_hi", [P, KT, 2 * SH], ST + 89, F32R)
    wdt_lo = at("wdt_lo", [P, KT, 2 * SH], ST + 91, F32R)
    vfb = at("vfb", [P, 2, GW], ST + 87)
    gmask = at("gmask", [P, 2, 2, P], ST + 91)
    btok = at("btok", [P, TT, NS], ST + 93)
    xtok = at("xtok", [P, TT, GW], ST + 95)
    cv = at("cv", [P, 4, S], ST + 95)
    dtmp = at("dtmp", [P, 4, TT * 2 * SH], ST + 95)
    hst = at("hst", [P, 2, 3, GW], 64)
    erhs = at("erhs", [P, 2, 2, 4, P], 76)
    ew = [at("ew0", [P, 2, 4, P], 84), at("ew1", [P, 2, 4, P], 40)]
    mw = [at("mw0", [P, 2, 4, P], 88), at("mw1", [P, 2, 4, P], 44)]
    vtl = [at("vtl0", [P, 2, GW], 92), at("vtl1", [P, 2, GW], 56)]
    y_one = at("y_one", [P, 2, GW], 60)
    y_two = at("y_two", [P, 2, GW], 92)
    htmp = at("htmp", [P, GW], 60)
    y_hi = at("y_hi", [P, XS_TILES, S], ST, F32R)
    y_lo = at("y_lo", [P, XS_TILES, S], ST + 32, F32R)
    sq_c = [[at(f"sq_c{g}_{i}", [P, S], ST + 32 + 2 * (XS_TILES + SG * i + g)) for i in range(2)] for g in range(SG)]
    nrm_c = [at(f"nrm_c{g}", [P, 3, S], ST + 8 * g) for g in range(SG)]
    m_ssd = at("m_ssd", [P, KT, S], 64)
    aneg = at("aneg", [P, 2 * SH], ST + 102.5)
    m_ffn = at("m_ffn", [P, KT, S], 64)
    g_hi = at("g_hi", [P, FT, S], ST, F32R)
    g_lo = at("g_lo", [P, FT, S], ST + 44, F32R)
    u = at("u", [P, 4, S], ST + 88)
    gv = at("gv", [P, 2, S], ST + 96)
    sq_b = at("sq_b", [P, 2, S], ST + 88)
    nrm_b = at("nrm_b", [P, 3, S], ST + 92)
    p1 = at("p1", [P, IN1_TILES, S], ST)
    mix = at("mix", [P, KT, S], ST + 48)
    vt = at("vt", [P, TT, SB_HEADS * DH], ST + 64)
    kv = at("kv", [P, 4, MEM], ST + 72)
    memx = at("memx", [P, KT, MEM], ST + 76)
    mem_hi = at("mem_hi", [P, KT, MEM], ST + 84, F32R)
    mem_lo = at("mem_lo", [P, KT, MEM], ST + 92, F32R)
    sp = at("sp", [P, 2, 1280], ST + 76)
    aw = at("aw", [P, 2, 1280], ST + 86)
    sq = at("sq", [P, 2, S], ST + 48)
    nrm = at("nrm", [P, 3, S], ST + 52)
    hbuf = at("hbuf", [P, 4, S], ST + 58)
    pooled = at("pooled", [P, 2, S], ST + 76)
    psum_s = at("psum_s", [P, 2, S], ST + 80)
    invc = at("invc", [P, 2, S], ST + 84)
    poolw = at("poolw", [P, 2, P], ST + 88)

    bank = [ctx.enter_context(nc.psum_tensor(f"bank{i}", [P, S], F32)) for i in range(8)]
    block = ctx.enter_context(nc.Block())

    w_load = [sem(f"w_load{s}") for s in range(RING)]
    hi_done, lo_done, slot_done = sem("hi_done"), sem("lo_done"), sem("slot_done")
    evac = [sem(f"evac{b}") for b in range(4)]

    def loops(eng, name, body):
        g = PLAN[name]
        turns = g["tiles"] // 4
        if turns == 1:
            body(0)
        else:
            with eng.Fori(0, turns) as i:
                body(i)

    def load_weights(sp_, name):
        g = PLAN[name]
        n, blocks = len(g["blocks"]), g["blocks"]
        src = dr["w_" + name]

        def body(i):
            for q in range(4 * n):
                s, t0 = q % RING, g["slot0"] + q
                if t0 >= RING:
                    sp_.wait_ge(hi_done, 4 * n * i + t0 - RING + 1)
                    sp_.wait_ge(lo_done, 4 * n * i + t0 - RING + 1)
                j, part = q // n, q % n
                nb = blocks[part]
                if isinstance(i, int):
                    row = src[4 * i + j]
                else:
                    row = src[bass.ds(4 * i + j, 1)].rearrange("a p c -> (a p) c")
                sp_.dma_start(raw[:, s, 0:nb * P], row[:, part * 8 * P:(part * 8 + nb) * P]).then_inc(w_load[s], 16)
        loops(sp_, name, body)

    def split_hi(act, name, i, q):
        g = PLAN[name]
        n = len(g["blocks"])
        t0, s = g["slot0"] + q + 2, (q + 2) % RING
        width = g["blocks"][(q + 2) % n] * P
        act.wait_ge(w_load[s], 16 * (n * i) + 16 * (t0 // RING + 1))
        if t0 >= RING:
            act.wait_ge(slot_done, 4 * n * i + t0 - RING + 1)
        nc.scalar.activation(w_hi[:, s, 0:width], raw[:, s, 0:width], ACT.Copy).then_inc(hi_done, 1)

    def split_lo(dve, name, i, q):
        g = PLAN[name]
        n = len(g["blocks"])
        t0, s = g["slot0"] + q + 2, (q + 2) % RING
        width = g["blocks"][(q + 2) % n] * P
        dve.wait_ge(hi_done, 4 * n * i + t0 + 1)
        nc.vector.tensor_tensor(w_lo[:, s, 0:width], raw[:, s, 0:width], w_hi[:, s, 0:width].bitcast(F32),
                                ALU.subtract).then_inc(lo_done, 1)

    def product_pe(pe, name, rhs_hi, rhs_lo, width=S, ready=None):
        g = PLAN[name]
        n = len(g["blocks"])

        def body(i):
            for j in range(4):
                tile0 = g["tile0"] + j
                pe.wait_ge(evac[j], i + tile0 // 4)
                for part, nb in enumerate(g["blocks"]):
                    q = j * n + part
                    s = q % RING
                    pe.wait_ge(lo_done, 4 * n * i + g["slot0"] + q + 1)
                    for b in range(nb):
                        k = part * 8 + b
                        first = k == 0
                        last = part == n - 1 and b == nb - 1
                        if ready and j == 0:
                            ready(k)
                        wh, wl = w_hi[:, s, b * P:(b + 1) * P], w_lo[:, s, b * P:(b + 1) * P]
                        out = bank[j][:, 0:width]
                        nc.tensor.matmul(out, wh, rhs_hi[:, k, :], start=first, stop=False)
                        nc.tensor.matmul(out, wh, rhs_lo[:, k, :], start=False, stop=False)
                        mm = nc.tensor.matmul(out, wl, rhs_hi[:, k, :], start=False, stop=last)
                    mm.then_inc(slot_done, 1)
        loops(pe, name, body)

    def product_split(eng, name, split, take, ahead=0):
        g = PLAN[name]
        n = len(g["blocks"])

        def turn(i, final=False):
            for j in range(4):
                for part in range(n):
                    if not (final and j * n + part + 2 >= 4 * n) and j * n + part >= ahead:
                        split(eng, name, i, j * n + part)
                take(i, j, (4 * n * i) + g["slot0"] + (j + 1) * n)
        turns = g["tiles"] // 4
        if g["last"]:
            if turns > 2:
                with eng.Fori(0, turns - 1) as i:
                    turn(i)
            elif turns == 2:
                turn(0)
            turn(turns - 1, True)
        else:
            loops(eng, name, turn)

    sq_done, sq_used = sem("sq_done"), sem("sq_used")
    psq_done, psq_used = sem("psq_done"), sem("psq_used")
    ln_done, rstd_done = sem("ln_done"), sem("rstd_done")
    h_done, ahi_done, alo_done, alo_pool = sem("h_done"), sem("ahi_done"), sem("alo_done"), sem("alo_pool")
    x_done, x_pool = sem("x_done"), sem("x_pool")
    chain = {"dve": sem("dve_chain"), "act": sem("act_chain"), "pool": sem("pool_chain")}
    count = {"dve": 0, "act": 0, "pool": 0}

    def link(who, eng, ins):
        count[who] += 1
        ins.then_inc(chain[who], 1)
        eng.wait_ge(chain[who], count[who])

    nrm_x = at("nrm_x", [P, 3, S], ST)

    def norm_pe(pe, s, width, b=4):
        for k in range(KT):
            pe.wait_ge(sq_done, KT * s + k + 1)
            mm = nc.tensor.matmul(bank[b][:, 0:width], C["ones"], sq[:, k % 2, 0:width], start=k == 0, stop=k == KT - 1)
            mm.then_inc(sq_used, 1)

    def roots_act(act, n, width, nrm, b=4):
        nc.scalar.activation(nrm[:, 0, 0:width], bank[b][:, 0:width], ACT.Ln, scale=1.0 / D, bias=eps_col[:, :]).then_inc(ln_done, 1)
        act.wait_ge(ln_done, n + 1)
        nc.scalar.activation(nrm[:, 1, 0:width], nrm[:, 0, 0:width], ACT.Exp, scale=-0.5).then_inc(rstd_done, 1)

    def norm_act(act, n, s, src, width, ready=None, nrm=nrm, b=4, beside=None):
        for k in range(KT):
            if ready:
                ready(k)
            if KT * s + k >= 2:
                act.wait_ge(sq_used, KT * s + k - 1)
            nc.scalar.activation(sq[:, k % 2, 0:width], src[:, k, :], ACT.Square).then_inc(sq_done, 1)
            if beside:
                beside(k)
        act.wait_ge(sq_used, KT * (s + 1))
        roots_act(act, n, width, nrm, b)

    def high_act(act, p, width, hi, tiles=range(KT)):
        for k in tiles:
            act.wait_ge(h_done, KT * p + k + 1)
            nc.scalar.activation(hi[:, k, :], hbuf[:, k % 4, 0:width], ACT.Copy).then_inc(ahi_done, 1)

    def square_act(e, buf, i, j, src):
        act_.wait_ge(psq_used, KT * e + 4 * i + j + 1)
        nc.scalar.activation(buf[:, j % 2, :], src, ACT.Square).then_inc(psq_done, 1)

    def sums_pool(pool, e, buf, acc):
        for k in range(1, KT - 1):
            pool.wait_ge(psq_done, KT * e + k + 1)
            pool.wait_ge(psq_used, KT * e + 2 + (0 if k == 1 else k))
            a = buf[:, 0, :] if k == 1 else acc
            nc.gpsimd.tensor_tensor(acc, a, buf[:, k % 2, :], ALU.add).then_inc(psq_used, 2 if k == 1 else 1)

    def sums_pe(pe, e, buf, acc):
        pe.wait_ge(psq_used, KT * e + 2 + KT - 1)
        nc.tensor.matmul(bank[4][:, :], C["ones"], acc, start=True, stop=False)
        pe.wait_ge(psq_done, KT * (e + 1))
        nc.tensor.matmul(bank[4][:, :], C["ones"], buf[:, 1, :], start=False, stop=True).then_inc(psq_used, 1)

    def sums_act(act, n, e, nrm):
        act.wait_ge(psq_used, KT * (e + 1) + 2)
        roots_act(act, n, S, nrm)

    def halve(dve, sums, scale, a):
        link("dve", dve, nc.vector.tensor_scalar(a, sums, -0.5 * scale, -0.5 * EPS, ALU.mult, ALU.add))

    def refine(dve, r, a, t):
        link("dve", dve, nc.vector.tensor_tensor(t, a, r, ALU.mult))
        link("dve", dve, nc.vector.tensor_tensor(t, t, r, ALU.mult))
        link("dve", dve, nc.vector.scalar_tensor_tensor(out=r, in0=t, scalar=1.5, in1=r, op0=ALU.add, op1=ALU.mult))

    def norm_dve(dve, n, width, nrm=nrm, b=4):
        dve.wait_ge(ln_done, n + 1)
        halve(dve, bank[b][:, 0:width], 1.0 / D, nrm[:, 2, 0:width])
        dve.wait_ge(rstd_done, n + 1)
        refine(dve, nrm[:, 1, 0:width], nrm[:, 2, 0:width], nrm[:, 0, 0:width])

    def split_done(eng, p, k):
        eng.wait_ge(alo_done if k % 2 else alo_pool, KT // 2 * p + k // 2 + 1)

    def low_pool(pool, p, width, hi, lo):
        for k in range(0, KT, 2):
            pool.wait_ge(ahi_done, KT * p + k + 1)
            nc.gpsimd.tensor_tensor(lo[:, k, :], hbuf[:, k % 4, 0:width], hi[:, k, :].bitcast(F32), ALU.subtract).then_inc(alo_pool, 1)

    def pre_norm_dve(dve, n, p, src, width, gain, hi, lo, nrm=nrm, b=4):
        norm_dve(dve, n, width, nrm, b)

        def low(k):
            dve.wait_ge(ahi_done, KT * p + k + 1)
            nc.vector.tensor_tensor(lo[:, k, :], hbuf[:, k % 4, 0:width], hi[:, k, :].bitcast(F32), ALU.subtract).then_inc(alo_done, 1)
        for k in range(KT):
            if k >= 4:
                split_done(dve, p, k - 4)
            elif p:
                split_done(dve, p - 1, k + 4)
            nc.vector.scalar_tensor_tensor(out=hbuf[:, k % 4, 0:width], in0=src[:, k, :], scalar=pcol(gain, k),
                                           in1=nrm[:, 1, 0:width], op0=ALU.mult, op1=ALU.mult).then_inc(h_done, 1)
            if k >= 3 and k % 2:
                low(k - 2)
        low(KT - 1)

    def updated(eng, v, k):
        eng.wait_ge(x_done if k % 2 else x_pool, KT // 2 * v + k // 2 + 1)

    def post_norm_dve(dve, n, v, m, gain, nrm=nrm):
        norm_dve(dve, n, S, nrm)

        def add(k):
            nc.vector.tensor_tensor(x[:, k, :], x[:, k, :], m[:, k, :], ALU.add).then_inc(x_done, 1)
        for k in range(KT):
            nc.vector.scalar_tensor_tensor(out=m[:, k, :], in0=m[:, k, :], scalar=pcol(gain, k), in1=nrm[:, 1, :],
                                           op0=ALU.mult, op1=ALU.mult).then_inc(m_done, 1)
            if k >= 2 and k % 2 == 0:
                dve.wait_ge(m_done, KT * v + k)
                add(k - 1)
        dve.wait_ge(m_done, KT * (v + 1))
        add(KT - 1)

    def post_norm_pool(pool, v, m):
        for k in range(0, KT, 2):
            pool.wait_ge(m_done, KT * v + k + 1)
            nc.gpsimd.tensor_tensor(x[:, k, :], x[:, k, :], m[:, k, :], ALU.add).then_inc(x_pool, 1)

    m_done = sem("m_done")

    def out_act(e, buf):
        def take(i, j, done):
            act_.wait_ge(slot_done, done)
            square_act(e, buf, i, j, bank[j][:, :])
        return take

    def out_dve(e, dst):
        def take(i, j, done):
            dve_.wait_ge(psq_done, KT * e + 4 * i + j + 1)
            out = dst[:, 4 * i + j, :] if isinstance(i, int) else dst[:, bass.ds(4 * i + j, 1), :].rearrange("p a t -> p (a t)")
            nc.vector.tensor_copy(out, bank[j][:, :]).then_inc(evac[j], 1)
        return take

    def copy_tiles(dst, parity):
        def take(i, j, done):
            if j % 2 != parity:
                return
            out = dst[:, 4 * i + j, :] if isinstance(i, int) else dst[:, bass.ds(4 * i + j, 1), :].rearrange("p a t -> p (a t)")
            if parity == 0:
                act_.wait_ge(slot_done, done)
                nc.scalar.activation(out, bank[j][:, :], ACT.Copy).then_inc(evac[j], 1)
            else:
                dve_.wait_ge(slot_done, done)
                nc.vector.tensor_copy(out, bank[j][:, :]).then_inc(evac[j], 1)
        return take

    act_, dve_ = nc.scalar, nc.vector

    tab_load, dist_load, neg_tab = sem("tab_load"), sem("dist_load"), sem("neg_tab")
    dec_e = sem("dec_e")
    swap_done, cos_done, sin_done, rot_done = sem("swap_done"), sem("cos_done"), sem("sin_done"), sem("rot_done")
    strip_l, strip_e = sem("strip_l"), sem("strip_e")
    rz, ra, ry, ryc = sem("rz"), sem("ra"), sem("ry"), sem("ryc")
    g_mean, g_cent, g_sq, g_var, g_ln, g_done = sem("g_mean"), sem("g_cent"), sem("g_sq"), sem("g_var"), sem("g_ln"), sem("g_done")

    KEY_ORDER = (1, 2, 3, 0)

    def ret_pe(pe):
        for t in range(8):
            if t >= 4:
                pe.wait_ge(sin_done, t - 3)
            nc.tensor.matmul(bank[4 + t % 4][:, :], C["swap"], p2[:, t, :], start=True, stop=True).then_inc(swap_done, 1)
        for i in range(4):
            for j in range(TT):
                mm = nc.tensor.transpose(bank[i][:, j * P:(j + 1) * P], p2[:, RET_V + i, j * P:(j + 1) * P], C["ident"])
            mm.then_inc(vtp, 1)
        pe.wait_ge(vtc, 2 * TT)
        pe.wait_ge(rot_done, 8)

        def scores(h):
            b, th = DH * (h % 2), h // 2
            for j in KEY_ORDER:
                if j == 0 and h >= 2:
                    pe.wait_ge(ryc, h - 1)
                nc.tensor.matmul(zbank(h, j)[:, :], p2[b:b + DH, RET_K + th, j * P:(j + 1) * P], p2[b:b + DH, RET_Q + th, :],
                                 start=True, stop=True).then_inc(rz, 1)

        def values(h):
            b = DH * (h % 2)
            pe.wait_ge(ra, TT * (h + 1))
            for n, j in enumerate(KEY_ORDER):
                mm = nc.tensor.matmul(zbank(h, 0)[b:b + DH, :], vt2[:, j, h * DH:(h + 1) * DH], aw2[:, h % 2, j, :],
                                      start=n == 0, stop=n == TT - 1)
            mm.then_inc(ry, 1)
        scores(0)
        for h in range(RH):
            if h + 1 < RH:
                scores(h + 1)
            values(h)
        pe.wait_ge(ryc, RH)
        for t in range(4):
            nc.tensor.matmul(bank[t][:, :], C["ones64"], p2[:, RET_V + t, :], start=True, stop=True).then_inc(g_mean, 1)
        for t in range(4):
            pe.wait_ge(g_sq, t + 1)
            nc.tensor.matmul(bank[4 + t][:, :], C["ones64"], gsq[:, t, :], start=True, stop=True).then_inc(g_var, 1)

    def decay_act(act):
        act.wait_ge(neg_tab, 1)
        nc.scalar.activation(dec[:, 1, :], dec[:, 0, :], ACT.Exp).then_inc(dec_e, 1)
        act.wait_ge(neg_tab, 2)
        nc.scalar.activation(dec[:, 3, :], dec[:, 2, :], ACT.Ln).then_inc(dec_e, 1)

    def log1p_fix(dve, e, one_plus, log, tmp):
        link("dve", dve, nc.vector.tensor_scalar(tmp, one_plus, -1.0, None, ALU.add))
        link("dve", dve, nc.vector.tensor_tensor(tmp, e, tmp, ALU.subtract))
        link("dve", dve, nc.vector.reciprocal(one_plus, one_plus))
        link("dve", dve, nc.vector.tensor_tensor(tmp, tmp, one_plus, ALU.mult))
        link("dve", dve, nc.vector.tensor_tensor(log, log, tmp, ALU.add))

    def decay_dve(dve):
        logit = par[:, PCOL["decay"]:PCOL["decay"] + 16]
        nc.vector.tensor_scalar(dec[:, 0, :], logit, -1.0, 30.0, ALU.mult, ALU.min).then_inc(neg_tab, 1)
        dve.wait_ge(dec_e, 1)
        nc.vector.tensor_scalar(dec[:, 2, :], dec[:, 1, :], 1.0, None, ALU.add).then_inc(neg_tab, 1)
        dve.wait_ge(dec_e, 2)
        log1p_fix(dve, dec[:, 1, :], dec[:, 2, :], dec[:, 3, :], dec[:, 4, :])
        link("dve", dve, nc.vector.tensor_scalar(dec[:, 4, :], logit, -1.0, None, ALU.mult))
        link("dve", dve, nc.vector.tensor_tensor(dec[:, 3, :], dec[:, 3, :], dec[:, 4, :], ALU.max))
        link("dve", dve, nc.vector.tensor_scalar(dec[:, 4, :], dec[:, 3, :], -1.0, None, ALU.mult))

    def ret_act(act):
        decay_act(act)
        for i in range(4):
            act.wait_ge(vtp, TT + i + 1)
            nc.scalar.activation(vt2[:, :, i * P:(i + 1) * P], bank[i][:, :].rearrange("p (j c) -> p j c", c=P),
                                 ACT.Copy).then_inc(vtc, 1)
        for h in range(RH):
            act.wait_ge(strip_l, h + 1)
            nc.scalar.activation(strip[:, h % 2, :], strip[:, h % 2, :], ACT.Exp).then_inc(strip_e, 1)
        act.wait_ge(ryc, RH)
        act.dma_start(cmask[:, :, :], dr["col_mask"]).then_inc(cm_load, 16)
        load_bias(act, 0)
        load_bias(act, 1)
        for t in range(4):
            act.wait_ge(g_cent, t + 1)
            nc.scalar.activation(gsq[:, t, :], p2[:, RET_V + t, :], ACT.Square).then_inc(g_sq, 1)
        for t in range(4):
            act.wait_ge(g_var, t + 1)
            nc.scalar.activation(grs[:, t, :], bank[4 + t][:, :], ACT.Ln, scale=1.0 / DH, bias=eps_col[:, :]).then_inc(g_ln, 1)
            act.wait_ge(g_ln, 2 * t + 1)
            nc.scalar.activation(grs[:, t, :], grs[:, t, :], ACT.Exp, scale=-0.5).then_inc(g_ln, 1)

    def ret_pool(pool):
        pool.wait_ge(tab_load, 16)
        for t in range(8):
            pool.wait_ge(swap_done, t + 1)
            nc.gpsimd.tensor_tensor(p2[:, t, :], p2[:, t, :], rope[:, 0, :], ALU.mult).then_inc(cos_done, 1)

    def ret_gate_pool(pool):
        pool.wait_ge(ryc, RH)
        for t in range(4):
            nc.gpsimd.tensor_copy(p2[:, RET_Q + t, :].rearrange("p (c r q) -> p c r q", c=4, q=QB),
                                  p2[:, NA_Q + t, :].rearrange("p (r c q) -> p c r q", c=4, q=QB)).then_inc(nq_done, 1)
        for t in range(4):
            pool.wait_ge(g_cent, 4 + t + 1)
            nc.gpsimd.tensor_tensor(p2[:, RET_G + t, :], p2[:, RET_G + t, :], p2[:, RET_V + t, :], ALU.mult).then_inc(g_done, 1)

    def ret_dve(dve):
        dve.wait_ge(tab_load, 16)
        dve.wait_ge(dist_load, 16)
        for t in range(8):
            dve.wait_ge(swap_done, t + 1)
            nc.vector.tensor_tensor(rtmp[:, t % 2, :], bank[4 + t % 4][:, :], rope[:, 1, :], ALU.mult).then_inc(sin_done, 1)
            dve.wait_ge(sin_done, t + 1)
            dve.wait_ge(cos_done, t + 1)
            nc.vector.tensor_tensor(p2[:, t, :], p2[:, t, :], rtmp[:, t % 2, :], ALU.add).then_inc(rot_done, 1)
        decay_dve(dve)

        def log_decay(h):
            if h >= 2:
                dve.wait_ge(ra, TT * (h - 1))
            link("dve", dve, nc.vector.tensor_scalar(strip[:, h % 2, :], dist[:, :], dec[:, 3, 8 + h:9 + h], None, ALU.mult))
            nc.vector.scalar_tensor_tensor(out=strip[:, h % 2, :], in0=dist[:, :], scalar=dec[:, 4, h:h + 1], in1=strip[:, h % 2, :],
                                           op0=ALU.mult, op1=ALU.min).then_inc(strip_l, 1)

        def weigh(h):
            dve.wait_ge(strip_e, h + 1)
            for n, j in enumerate(KEY_ORDER):
                dve.wait_ge(rz, TT * h + n + 1)
                if h >= 2 and n == 0:
                    dve.wait_ge(ry, h - 1)
                nc.vector.scalar_tensor_tensor(out=aw2[:, h % 2, j, :], in0=zbank(h, j)[:, :], scalar=DH ** -0.5,
                                               in1=strip[:, h % 2, S - P - j * P:2 * S - P - j * P], op0=ALU.mult, op1=ALU.mult).then_inc(ra, 1)

        def keep(h):
            b, th = DH * (h % 2), h // 2
            dve.wait_ge(ry, h + 1)
            nc.vector.tensor_copy(p2[b:b + DH, RET_V + th, :], zbank(h, 0)[b:b + DH, :]).then_inc(ryc, 1)
        log_decay(0)
        log_decay(1)
        for h in range(RH):
            weigh(h)
            if h + 2 < RH:
                log_decay(h + 2)
            if h:
                keep(h - 1)
        keep(RH - 1)
        for t in range(4):
            y = p2[:, RET_V + t, :]
            dve.wait_ge(g_mean, t + 1)
            nc.vector.scalar_tensor_tensor(out=y, in0=bank[t][:, :], scalar=-1.0 / DH, in1=y, op0=ALU.mult, op1=ALU.add).then_inc(g_cent, 1)
        for c in range(4):
            for i in range(4):
                nc.vector.tensor_copy(nvw[:, c, i, :].rearrange("p (r k) -> p r k", k=KEYW),
                                      grid(NA_V + i)[:, :, WIN0[c]:WIN0[c] + KEYW]).then_inc(nvw_done, 1)
        for t in range(4):
            y = p2[:, RET_V + t, :]
            dve.wait_ge(g_ln, 2 * t + 1)
            halve(dve, bank[4 + t][:, :], 1.0 / DH, ghalf[:, :])
            dve.wait_ge(g_ln, 2 * t + 2)
            refine(dve, grs[:, t, :], ghalf[:, :], gsq[:, t, :])
            nc.vector.scalar_tensor_tensor(out=y, in0=y, scalar=pcol("ret_gn_g", t), in1=grs[:, t, :],
                                           op0=ALU.mult, op1=ALU.mult).then_inc(g_cent, 1)

    nvp, nvc, bt_load, bm_done = sem("nvp"), sem("nvc"), [sem("bt_load0"), sem("bt_load1")], sem("bm_done")
    cm_load, nvw_done, nq_done = sem("cm_load"), sem("nvw_done"), sem("nq_done")
    nz, ns, nmax, nexp, nnorm, ntp, ntc, ny, nyc = (sem(n) for n in ("nz", "ns", "nmax", "nexp", "nnorm", "ntp", "ntc", "ny", "nyc"))
    WIN0 = [min(max(QB * c - WIN_C // 2, 0), GRID_W - KEYW) for c in range(4)]
    NU = 2 * NH

    def grid(tile, b0=0, b1=P):
        return p2[b0:b1, tile, :].rearrange("p (r c) -> p r c", c=GRID_W)

    def sbank(un):
        return bank[(0, 1, 6, 7)[un % 4]]

    def na_pe(pe):
        pe.wait_ge(nvw_done, 16)
        for c in range(4):
            for f in range(2):
                n = 2 * c + f
                if n < 4:
                    pe.wait_ge(g_cent, 4)
                else:
                    pe.wait_ge(nvc, n - 3)
                for i in range(4):
                    mm = nc.tensor.transpose(bank[n % 4][:, i * P:(i + 1) * P], nvw[:, c, i, f * P:(f + 1) * P], C["ident"])
                mm.then_inc(nvp, 1)
        pe.wait_ge(nvc, 8)
        pe.wait_ge(nq_done, 4)

        def scores(un):
            h, i = un // 2, un % 2
            b, th = DH * (h % 2), h // 2
            if un == 2:
                pe.wait_ge(g_cent, 8)
            if un >= 4:
                pe.wait_ge(ns, un - 3)
            for r in range(2):
                c = 2 * i + r
                mm = nc.tensor.matmul(sbank(un)[:, r * 256:(r + 1) * 256], p2[b:b + DH, RET_Q + th, c * P:(c + 1) * P],
                                      grid(NA_K + th, b, b + DH)[:, :, WIN0[c]:WIN0[c] + KEYW], start=True, stop=True)
            mm.then_inc(nz, 1)

        def turn(un):
            pe.wait_ge(nnorm, un + 1)
            if un >= 2:
                pe.wait_ge(ntc, un - 1)
            for r in range(2):
                for f in range(2):
                    mm = nc.tensor.transpose(bank[2 + un % 2][:, (2 * r + f) * P:(2 * r + f + 1) * P],
                                             nprob[:, un % 2, r, f * P:(f + 1) * P], C["ident"])
            mm.then_inc(ntp, 1)

        def values(un):
            h, i = un // 2, un % 2
            b = DH * (h % 2)
            pe.wait_ge(ntc, un + 1)
            if i == 0 and h >= 2:
                pe.wait_ge(nyc, h - 1)
            for r in range(2):
                c = 2 * i + r
                for f in range(2):
                    mm = nc.tensor.matmul(bank[4 + h % 2][b:b + DH, c * P:(c + 1) * P], vna[:, c, f, h * DH:(h + 1) * DH],
                                          npt[:, un % 2, 2 * r + f, :], start=f == 0, stop=f == 1)
            if i:
                mm.then_inc(ny, 1)
        scores(0)
        scores(1)
        for un in range(NU):
            if un + 2 < NU:
                scores(un + 2)
            turn(un)
            if un:
                values(un - 1)
        values(NU - 1)

    def load_bias(act, h):
        act.dma_start(bt[:, h % 2, :, :].rearrange("p r c -> p (r c)")[:, 0:BIAS_RUN], dr["rpb"][h]).then_inc(bt_load[h % 2], 16)

    def na_act(act):
        for n in range(8):
            act.wait_ge(nvp, n + 1)
            nc.scalar.activation(vna[:, n // 2, n % 2, :], bank[n % 4][:, :], ACT.Copy).then_inc(nvc, 1)
        for un in range(NU):
            if un % 2 == 0 and un // 2 + 2 < NH:
                act.wait_ge(bm_done, un // 2 + 1)
                load_bias(act, un // 2 + 2)
            act.wait_ge(nmax, un + 1)
            for r in range(2):
                c = 2 * un + r
                e = nc.scalar.activation(nprob[:, un % 2, r, :], nprob[:, un % 2, r, :], ACT.Exp, bias=nstat[:, 0, c:c + 1],
                                         accum_out=nstat[:, 1, c:c + 1])
            e.then_inc(nexp, 1)

    def na_pool(pool):
        pool.wait_ge(cm_load, 16)
        for h in range(NH):
            pool.wait_ge(bt_load[h % 2], 16 * (h // 2 + 1))
            if h >= 2:
                pool.wait_ge(ns, 2 * (h - 1))
            for c in range(4):
                o = WIN0[c] - QB * c + WIN_C
                add = nc.gpsimd.tensor_tensor(bm[:, h % 2, c, :, :], bt[:, h % 2, :, o:o + KEYW],
                                              cmask[:, c:c + 1, :].to_broadcast([P, ROWS, KEYW]), ALU.add)
            add.then_inc(bm_done, 1)

    def na_dve(dve):
        def shift(un):
            h, i = un // 2, un % 2
            dve.wait_ge(nz, un + 1)
            dve.wait_ge(bm_done, h + 1)
            if un >= 2:
                dve.wait_ge(ntp, un - 1)
            nc.vector.scalar_tensor_tensor(out=nprob[:, un % 2, :, :].rearrange("p r k -> p (r k)"), in0=sbank(un)[:, :], scalar=DH ** -0.5,
                                           in1=bm[:, h % 2, 2 * i:2 * i + 2, :, :].rearrange("p c r k -> p (c r k)"),
                                           op0=ALU.mult, op1=ALU.add).then_inc(ns, 1)
            dve.wait_ge(ns, un + 1)
            nc.vector.tensor_reduce(nstat[:, 0, 2 * un:2 * un + 2], nprob[:, un % 2, :, :], AX.X, ALU.max, negate=True).then_inc(nmax, 1)

        def norm(un):
            dve.wait_ge(nexp, un + 1)
            link("dve", dve, nc.vector.reciprocal(nstat[:, 2, 2 * un:2 * un + 2], nstat[:, 1, 2 * un:2 * un + 2]))
            for r in range(2):
                c = 2 * un + r
                m = nc.vector.tensor_scalar(nprob[:, un % 2, r, :], nprob[:, un % 2, r, :], nstat[:, 2, c:c + 1], None, ALU.mult)
            m.then_inc(nnorm, 1)

        def turned(un):
            h = un // 2
            b, th = DH * (h % 2), h // 2
            dve.wait_ge(ntp, un + 1)
            nc.vector.tensor_copy(npt[:, un % 2, :, :].rearrange("p a q -> p (a q)"), bank[2 + un % 2][:, :]).then_inc(ntc, 1)
            if un % 2 == 0 and h:
                keep(h - 1)

        def keep(h):
            b, th = DH * (h % 2), h // 2
            dve.wait_ge(ny, h + 1)
            nc.vector.tensor_copy(p2[b:b + DH, NA_Q + th, :].rearrange("p (r c q) -> p c r q", c=4, q=QB),
                                  bank[4 + h % 2][b:b + DH, :].rearrange("p (c r q) -> p c r q", c=4, q=QB)).then_inc(nyc, 1)
        shift(0)
        for un in range(NU):
            if un + 1 < NU:
                shift(un + 1)
            norm(un)
            if un:
                turned(un - 1)
        turned(NU - 1)
        keep(NH - 1)


    def mix2(k):
        return p2[:, RET_G + k, :] if k < 4 else p2[:, NA_Q + k - 4, :]

    def split_mix2_act(act):
        for k in range(KT):
            act.wait_ge(g_done, 4) if k == 0 else None
            if k == 4:
                act.wait_ge(nyc, NH)
            nc.scalar.activation(a_hi[:, k, :], mix2(k), ACT.Copy).then_inc(mixhi, 1)

    def split_mix2_dve(dve):
        for k in range(KT):
            dve.wait_ge(mixhi, KT + k + 1)
            nc.vector.tensor_tensor(a_lo[:, k, :], mix2(k), a_hi[:, k, :].bitcast(F32), ALU.subtract).then_inc(mixlo, 1)

    mid, left, gel, prod, ghi, glo = (sem(n) for n in ("mid", "left", "gel", "prod", "ghi", "glo"))

    def col(table, width, i, j, tap=0):
        if isinstance(i, int):
            c = PCOL[table] + width * (4 * i + j) + tap
            return par[:, c:c + 1]
        return par[:, bass.ds(4 * width * i + (PCOL[table] + width * j + tap), 1)]

    def row(buf, i, r):
        if isinstance(i, int):
            return buf[:, 2 * i + r, :]
        return buf[:, bass.ds(2 * i + r, 1), :].rearrange("p a t -> p (a t)")

    def up_act(layer):
        def high(i, r):
            act_.wait_ge(prod, 2 * i + r + 3 + FT * layer)
            nc.scalar.activation(row(g_hi, i, r), gv[:, r, :], ACT.Copy).then_inc(ghi, 1)

        def take(i, j, done):
            act_.wait_ge(slot_done, done)
            act_.wait_ge(prod, 2 * i + j // 2 + 1 + FT * layer)
            nc.scalar.activation(u[:, j, :], bank[j][:, :], ACT.Identity, scale=col(f"ffn_w{layer}", 3, i, j, 1),
                                 bias=col(f"ffn_b{layer}", 1, i, j)).then_inc(mid, 1)
            if j == 2:
                high(i, 0)
            if j % 2:
                act_.wait_ge(evac[j - 1], i + (PLAN[f"up{layer}"]["tile0"] // 4 + 1))
                nc.scalar.activation(u[:, j - 1, :], u[:, j - 1, :], ACT.Gelu_apprx_tanh).then_inc(gel, 1)
            if j == 3:
                high(i, 1)
        return take

    def up_dve(layer):
        def low(i, r):
            dve_.wait_ge(ghi, 2 * i + r + 1 + FT * layer)
            nc.vector.tensor_tensor(row(g_lo, i, r), gv[:, r, :], row(g_hi, i, r).bitcast(F32), ALU.subtract).then_inc(glo, 1)

        def take(i, j, done):
            w = f"ffn_w{layer}"
            dve_.wait_ge(mid, 4 * i + j + 1 + 2 * FT * layer)
            nc.vector.scalar_tensor_tensor(out=u[:, j, 1:S], in0=bank[j][:, 0:S - 1], scalar=col(w, 3, i, j, 0), in1=u[:, j, 1:S],
                                           op0=ALU.mult, op1=ALU.add).then_inc(left, 1)
            dve_.wait_ge(left, 4 * i + j + 1 + 2 * FT * layer)
            nc.vector.scalar_tensor_tensor(out=u[:, j, 0:S - 1], in0=bank[j][:, 1:S], scalar=col(w, 3, i, j, 2), in1=u[:, j, 0:S - 1],
                                           op0=ALU.mult, op1=ALU.add).then_inc(evac[j], 1)
            if j == 2:
                low(i, 0)
            if j == 3:
                low(i, 1)
        return take

    def up_pool(pool, layer):
        with pool.Fori(0, FT // 2) as i:
            for r in range(2):
                pool.wait_ge(gel, 2 * i + r + 1 + FT * layer)
                pool.wait_ge(evac[2 * r + 1], i + (PLAN[f"up{layer}"]["tile0"] // 4 + 1))
                pool.wait_ge(glo, 2 * i + r + 1 + FT * layer)
                nc.gpsimd.tensor_tensor(gv[:, r, :], u[:, 2 * r, :], u[:, 2 * r + 1, :], ALU.mult).then_inc(prod, 1)

    eps_col = at("eps_col", [P, 1], 103.5)
    x_load, mem_load, cst_load, par_load, poolc_load = sem("x_load"), sem("mem_load"), sem("cst_load"), sem("par_load"), sem("poolc_load")
    out_done, eps_done = sem("out_done"), sem("eps_done")


    silu_done, pooled_done, poolmm, pool_y = sem("silu_done"), sem("pooled_done"), sem("poolmm"), sem("pool_y")
    vtp, vtc, q_scaled = sem("vtp"), sem("vtc"), sem("q_scaled")
    z_done, na_done, e_done, sp_done, spm_done = sem("z_done"), sem("na_done"), sem("e_done"), sem("sp_done"), sem("spm_done")
    la_done, a_done, am_done, y_done, y_read = sem("la_done"), sem("a_done"), sem("am_done"), sem("y_done"), sem("y_read")
    mixhi, mixlo = sem("mixhi"), sem("mixlo")

    KCOL = [0, 512, 896, 1152]
    KW = [S - P * j for j in range(TT)]

    def seg(buf, h, j, a=0, b=None):
        return buf[:, h % 2, KCOL[j] + a:KCOL[j] + (KW[j] if b is None else b)]

    def zbank(h, j):
        return bank[4 * (h % 2) + j]

    def stick_pe(pe):
        for i in range(4):
            pe.wait_ge(mh_done, i + 1)
            for j in range(TT):
                mm = nc.tensor.transpose(bank[i][:, j * P:(j + 1) * P], p1[:, SB_V + i, j * P:(j + 1) * P], C["ident"])
            mm.then_inc(vtp, 1)

        def scores(h):
            b, th = DH * (h % 2), h // 2
            if h == 0:
                pe.wait_ge(q_scaled, 4)
            if h < 2:
                pe.wait_ge(vtc, 4)
                pe.wait_ge(mvc, 1)
            else:
                pe.wait_ge(y_read, h - 1)
            for j in range(TT):
                nc.tensor.matmul(zbank(h, j)[:, 0:KW[j]], p1[b:b + DH, SB_K + th, j * P:(j + 1) * P],
                                 p1[b:b + DH, SB_Q + th, j * P:S], start=True, stop=True).then_inc(z_done, 1)

        def suffix(h):
            pe.wait_ge(spm_done, TT * (h + 1))
            for j in range(TT):
                for jj in range(j, TT):
                    mm = nc.tensor.matmul(zbank(h, j)[:, (jj - j) * P:KW[j]], C["neg_tri"] if jj == j else C["neg_ones"],
                                          seg(sp, h, jj), start=False, stop=jj == TT - 1, skip_group_check=True)
                mm.then_inc(la_done, 1)

        def values(h):
            b = DH * (h % 2)
            for j in range(TT):
                pe.wait_ge(am_done, TT * h + j + 1)
                mm = nc.tensor.matmul(zbank(h, 0)[b:b + DH, j * P:S], vt[:, j, h * DH:(h + 1) * DH], seg(aw, h, j),
                                      start=j == 0, stop=j == TT - 1)
            mm.then_inc(y_done, 1)

        scores(0)
        for h in range(SB_HEADS):
            if h + 1 < SB_HEADS:
                scores(h + 1)
            suffix(h)
            values(h)

    def stick_act(act):
        for i in range(4):
            act.wait_ge(vtp, i + 1)
            nc.scalar.activation(vt[:, :, i * P:(i + 1) * P], bank[i][:, :].rearrange("p (j c) -> p j c", c=P),
                                 ACT.Copy).then_inc(vtc, 1)

        def softplus(h):
            for j in range(TT):
                n = TT * h + j
                act.wait_ge(na_done, n + 1)
                nc.scalar.activation(seg(sp, h, j), seg(sp, h, j), ACT.Exp).then_inc(e_done, 1)
                act.wait_ge(e_done, 2 * n + 1)
                nc.scalar.activation(seg(sp, h, j), seg(sp, h, j), ACT.Ln, bias=1.0).then_inc(e_done, 1)

        def weights(h):
            for j in range(TT):
                n = TT * h + j
                act.wait_ge(la_done, n + 1)
                if h >= 2:
                    act.wait_ge(y_done, h - 1)
                nc.scalar.activation(seg(aw, h, j), zbank(h, j)[:, 0:KW[j]], ACT.Exp).then_inc(a_done, 1)
        softplus(0)
        for h in range(SB_HEADS):
            if h + 1 < SB_HEADS:
                softplus(h + 1)
            weights(h)

    def stick_dve(dve):
        def softplus(h):
            for j in range(TT):
                n = TT * h + j
                dve.wait_ge(z_done, n + 1)
                if h >= 2:
                    dve.wait_ge(la_done, TT * (h - 1))
                nc.vector.tensor_scalar(seg(sp, h, j), zbank(h, j)[:, 0:KW[j]], 30.0, None, ALU.min).then_inc(na_done, 1)
            for j in range(TT):
                n = TT * h + j
                dve.wait_ge(e_done, 2 * n + 2)
                nc.vector.tensor_tensor(seg(sp, h, j), zbank(h, j)[:, 0:KW[j]], seg(sp, h, j), ALU.max).then_inc(sp_done, 1)

        def gate(h):
            b, th = DH * (h % 2), h // 2
            dve.wait_ge(y_done, h + 1)
            nc.vector.tensor_tensor(mix[b:b + DH, 2 + th, :], zbank(h, 0)[b:b + DH, :], p1[b:b + DH, SB_G + th, :],
                                    ALU.mult).then_inc(y_read, 1)
        softplus(0)
        for h in range(SB_HEADS):
            if h + 1 < SB_HEADS:
                softplus(h + 1)
            if 1 <= h <= 4:
                mem_norm_dve(dve, h - 1)
            gate(h)

    def stick_pool(pool):
        def mask(src, done, out):
            nc.gpsimd.affine_select(out=src, in_=src, compare_op=ALU.is_gt, fill=0.0, base=0, pattern=[[1, P]],
                                    channel_multiplier=-1).then_inc(out, 1)

        def softplus(h):
            for j in range(TT):
                pool.wait_ge(sp_done, TT * h + j + 1)
                mask(seg(sp, h, j, 0, P), sp_done, spm_done)

        def weights(h):
            for j in range(TT):
                pool.wait_ge(a_done, TT * h + j + 1)
                mask(seg(aw, h, j, 0, P), a_done, am_done)
        softplus(0)
        for h in range(SB_HEADS):
            if h + 1 < SB_HEADS:
                softplus(h + 1)
            weights(h)

    def pool_pool(pool):
        pool.wait_ge(evac[0], PLAN["in1"]["tile0"] // 4 + 1)
        pool.wait_ge(evac[1], PLAN["in1"]["tile0"] // 4 + 1)
        nc.gpsimd.memset(poolw[:, :, :], 0.0).then_inc(sem("poolw_zero"), 1)
        pool.wait_ge(poolc_load, 16)
        for t in range(2):
            u, cur, w = p1[:, POOL_V + t, :], p1[:, POOL_V + t, :], 1
            lo_stop = 2 if t == 0 else 8
            for stage in range(2 if t == 0 else 4):
                nxt = psum_s[:, stage % 2, :]
                link("pool", pool, nc.gpsimd.tensor_copy(nxt[:, 0:w], cur[:, 0:w]))
                link("pool", pool, nc.gpsimd.tensor_tensor(nxt[:, w:S], cur[:, w:S], cur[:, 0:S - w], ALU.add))
                w *= 2
                cur = nxt
                if w == lo_stop:
                    link("pool", pool, nc.gpsimd.tensor_tensor(pooled[0:DH, t, :], cur[0:DH, :], invc[0:DH, t, :], ALU.mult))
            link("pool", pool, nc.gpsimd.tensor_tensor(pooled[DH:P, t, :], cur[DH:P, :], invc[DH:P, t, :], ALU.mult))
            nc.gpsimd.tensor_tensor(pooled[:, t, :], pooled[:, t, :], u, ALU.subtract).then_inc(pooled_done, 1)

    def pool_pe(pe):
        pe.wait_ge(sem("poolw_load"), 64)
        pe.wait_ge(evac[0], PLAN["out1"]["tile0"] // 4)
        for t in range(2):
            pe.wait_ge(pooled_done, t + 1)
            nc.tensor.matmul(bank[4 + t][:, :], poolw[:, t, :], pooled[:, t, :], start=True, stop=True).then_inc(poolmm, 1)

    def pool_dve(dve):
        dve.wait_ge(silu_done, 2)
        for t in range(2):
            dve.wait_ge(poolmm, t + 1)
            nc.vector.scalar_tensor_tensor(out=mix[:, t, :], in0=bank[4 + t][:, :], scalar=pcol("pool_scale", t),
                                           in1=p1[:, POOL_G + t, :], op0=ALU.mult, op1=ALU.mult).then_inc(pool_y, 1)

    msq = at("msq", [P, 4, S], 64)
    mrs = at("mrs", [P, 4, S], 72)
    mhalf = at("mhalf", [P, 4, S], 80)
    mq = at("mq", [P, 2, S], 88)
    mk = at("mk", [P, 2, MEM], 92)
    mvt = at("mvt", [P, 2, MEM], 94)
    prob = at("prob", [P, 4, 2, MEM], ST + 80)
    pt = at("pt", [P, 2, S], ST + 92)
    mstat = at("mstat", [P, 4, 16], ST + 96)
    msq_done, mms_done, mln_done, mn_done = sem("msq_done"), sem("mms_done"), sem("mln_done"), sem("mn_done")
    mh_done, mvp, mvc, ms_rdy, mmax, mexp, mnorm = sem("mh_done"), sem("mvp"), sem("mvc"), sem("ms_rdy"), sem("mmax"), sem("mexp"), sem("mnorm")
    mtp, mtc, my_done, my_read = sem("mtp"), sem("mtc"), sem("my_done"), sem("my_read")
    NORMS = [(p1, MEM_Q, S, "q_norm_g", 0), (p1, MEM_Q + 1, S, "q_norm_g", 1), (kv, 0, MEM, "k_norm_g", 0), (kv, 1, MEM, "k_norm_g", 1)]

    def mem_norm_pe(pe):
        for n, (src, t, w, g, o) in enumerate(NORMS):
            pe.wait_ge(msq_done, n + 1)
            nc.tensor.matmul(bank[n][:, 0:w], C["ones64"], msq[:, n, 0:w], start=True, stop=True).then_inc(mms_done, 1)
        for t in range(2):
            for m in range(2):
                mm = nc.tensor.transpose(bank[6][:, (2 * m + t) * P:(2 * m + t + 1) * P], kv[:, 2 + t, m * P:(m + 1) * P], C["ident"])
        mm.then_inc(mvp, 1)

    def mem_norm_act(act):
        for n, (src, t, w, g, o) in enumerate(NORMS):
            act.wait_ge(mms_done, n + 1)
            nc.scalar.activation(mrs[:, n, 0:w], bank[n][:, 0:w], ACT.Ln, scale=1.0 / DH, bias=eps_col[:, :]).then_inc(mln_done, 1)
            act.wait_ge(mln_done, 2 * n + 1)
            nc.scalar.activation(mrs[:, n, 0:w], mrs[:, n, 0:w], ACT.Exp, scale=-0.5).then_inc(mln_done, 1)
        act.wait_ge(mvp, 1)
        nc.scalar.activation(mvt[:, :, :], bank[6][:, :].rearrange("p (m c) -> p m c", m=2), ACT.Copy).then_inc(mvc, 1)

    def mem_half_dve(dve):
        for n, (src, t, w, g, o) in enumerate(NORMS):
            dve.wait_ge(mln_done, 2 * n + 1)
            nc.vector.tensor_scalar(mhalf[:, n, 0:w], bank[n][:, 0:w], -0.5 / DH, -0.5 * EPS, ALU.mult, ALU.add).then_inc(mh_done, 1)

    def mem_norm_dve(dve, n):
        src, t, w, g, o = NORMS[n]
        dve.wait_ge(mln_done, 2 * n + 2)
        dve.wait_ge(mh_done, n + 1)
        refine(dve, mrs[:, n, 0:w], mhalf[:, n, 0:w], msq[:, n, 0:w])
        nc.vector.scalar_tensor_tensor(out=(mq if src is p1 else mk)[:, o, :], in0=src[:, t, :], scalar=pcol(g), in1=mrs[:, n, 0:w],
                                       op0=ALU.mult, op1=ALU.mult).then_inc(mn_done, 1)

    def mbank(u):
        return bank[(2, 3, 0, 1)[u % 4]]

    def mem_pe(pe):
        pe.wait_ge(y_read, SB_HEADS)
        pe.wait_ge(mn_done, 4)

        def scores(h):
            b, th = DH * (h % 2), h // 2
            for i in range(2):
                u = 2 * h + i
                if u >= 4:
                    pe.wait_ge(mexp, u - 3)
                for r in range(2):
                    mm = nc.tensor.matmul(mbank(u)[:, r * MEM:(r + 1) * MEM], mq[b:b + DH, th, (2 * i + r) * P:(2 * i + r + 1) * P],
                                          mk[b:b + DH, th, :], start=True, stop=True)
                mm.then_inc(ms_rdy, 1)

        def turn(u):
            pe.wait_ge(mnorm, u + 1)
            if u >= 2:
                pe.wait_ge(mtc, u - 1)
            for m in range(2):
                for r in range(2):
                    mm = nc.tensor.transpose(bank[4 + u % 2][:, (2 * m + r) * P:(2 * m + r + 1) * P],
                                             prob[:, u % 4, r, m * P:(m + 1) * P], C["ident"])
            mm.then_inc(mtp, 1)

        scores(0)
        scores(1)
        for h in range(MEM_HEADS):
            b = DH * (h % 2)
            turn(2 * h)
            turn(2 * h + 1)
            if h + 2 < MEM_HEADS:
                scores(h + 2)
            pe.wait_ge(mtc, 2 * h + 2)
            pe.wait_ge(mvc, 1)
            if h >= 2:
                pe.wait_ge(my_read, h - 1)
            for m in range(2):
                mm = nc.tensor.matmul(bank[6 + h % 2][b:b + DH, :], mvt[:, m, h * DH:(h + 1) * DH], pt[:, m, :], start=m == 0, stop=m == 1)
            mm.then_inc(my_done, 1)

    def mem_act(act):
        act.wait_ge(y_done, SB_HEADS)
        for u in range(2 * MEM_HEADS):
            act.wait_ge(mmax, u + 1)
            if u >= 4:
                act.wait_ge(mtp, u - 3)
            for r in range(2):
                c = 2 * u + r
                e = nc.scalar.activation(prob[:, u % 4, r, :], mbank(u)[:, r * MEM:(r + 1) * MEM], ACT.Exp,
                                         bias=mstat[:, 1, c:c + 1], scale=DH ** -0.5, accum_out=mstat[:, 2, c:c + 1])
            e.then_inc(mexp, 1)

    def mem_dve(dve):
        def top(u):
            dve.wait_ge(ms_rdy, u + 1)
            link("dve", dve, nc.vector.tensor_reduce(mstat[:, 0, 2 * u:2 * u + 2], mbank(u)[:, :].rearrange("p (r m) -> p r m", r=2),
                                                     AX.X, ALU.max))
            nc.vector.tensor_scalar(mstat[:, 1, 2 * u:2 * u + 2], mstat[:, 0, 2 * u:2 * u + 2], -DH ** -0.5, None, ALU.mult).then_inc(mmax, 1)

        def norm(u):
            dve.wait_ge(mexp, u + 1)
            link("dve", dve, nc.vector.reciprocal(mstat[:, 3, 2 * u:2 * u + 2], mstat[:, 2, 2 * u:2 * u + 2]))
            for r in range(2):
                c = 2 * u + r
                m = nc.vector.tensor_scalar(prob[:, u % 4, r, :], prob[:, u % 4, r, :], mstat[:, 3, c:c + 1], None, ALU.mult)
            m.then_inc(mnorm, 1)

        def turned(u):
            h, i = u // 2, u % 2
            dve.wait_ge(mtp, u + 1)
            if i == 0 and h:
                dve.wait_ge(my_done, h)
            nc.vector.tensor_copy(pt[:, :, 2 * i * P:2 * (i + 1) * P], bank[4 + u % 2][:, :].rearrange("p (m r) -> p m r", m=2)).then_inc(mtc, 1)

        def gate(h):
            b, th = DH * (h % 2), h // 2
            dve.wait_ge(my_done, h + 1)
            nc.vector.tensor_tensor(mix[b:b + DH, 6 + th, :], bank[6 + h % 2][b:b + DH, :], p1[b:b + DH, MEM_G + th, :],
                                    ALU.mult).then_inc(my_read, 1)

        for u in range(4):
            top(u)
        for h in range(MEM_HEADS):
            norm(2 * h)
            norm(2 * h + 1)
            if h:
                gate(h - 1)
            turned(2 * h)
            turned(2 * h + 1)
            if h + 2 < MEM_HEADS:
                top(2 * h + 4)
                top(2 * h + 5)
        gate(MEM_HEADS - 1)

    def split_mix_act(act):
        for k in range(KT):
            if k == 0:
                act.wait_ge(pool_y, 2)
            if k == 2:
                act.wait_ge(y_read, SB_HEADS)
            if k == 6:
                act.wait_ge(my_read, MEM_HEADS)
            nc.scalar.activation(a_hi[:, k, :], mix[:, k, :], ACT.Copy).then_inc(mixhi, 1)

    def split_mix_dve(dve):
        for k in range(KT):
            dve.wait_ge(mixhi, k + 1)
            nc.vector.tensor_tensor(a_lo[:, k, :], mix[:, k, :], a_hi[:, k, :].bitcast(F32), ALU.subtract).then_inc(mixlo, 1)

    (dtw_load, dtw_hi, dtw_lo, dtp, dt_v, dt_a, cump, cum_x, dt_ok, tri_load) = (
        sem(n) for n in ("dtw_load", "dtw_hi", "dtw_lo", "dtp", "dt_v", "dt_a", "cump", "cum_x", "dt_ok", "tri_load"))
    dtc = sem("dtc")
    dt_ch = at("dt_ch", [P, S], ST + 87)
    xmid, xtap, xsilu = sem("xmid"), sem("xtap"), sem("xsilu")
    (tbp, tbc, txp, xtc, vt_done, stp, hu, h_ready, gp, gl_done, rhs_done, xp, e_x, mlu, v_done) = (
        sem(n) for n in ("tbp", "tbc", "txp", "xtc", "vt_done", "stp", "hu", "h_ready", "gp", "gl_done", "rhs_done", "xp", "e_x", "mlu", "v_done"))
    (intra, inter, comb, ysum, typ, yev, gated, ysq, ysqu, yln, yn, yhi, ylo) = (
        sem(n) for n in ("intra", "inter", "comb", "ysum", "typ", "yev", "gated", "ysq", "ysqu", "yln", "yn", "yhi", "ylo"))
    M = {n: tri[:, i, :] for i, n in enumerate(SSD_CONSTS)}

    def chunk(tile, c):
        return xbc[:, tile, c * P:(c + 1) * P]

    def nbank(g):
        return bank[0 if g < SG - 1 else 4]

    def tbank(c):
        return bank[0 if c % 2 == 0 else 7]

    def heads(buf, c, d, g):
        return buf[:, c, d, HPG * g:HPG * (g + 1)].unsqueeze(2).to_broadcast([P, HPG, HD])

    def wide(ap):
        return ap.rearrange("p (h c) -> p h c", c=HD)

    def dt_pe(pe):
        pe.wait_ge(dtw_lo, 1)
        for k in range(KT):
            out = bank[5][0:2 * SH, :]
            nc.tensor.matmul(out, wdt_hi[:, k, :], a_hi[:, k, :], start=k == 0, stop=False)
            nc.tensor.matmul(out, wdt_hi[:, k, :], a_lo[:, k, :], start=False, stop=False)
            mm = nc.tensor.matmul(out, wdt_lo[:, k, :], a_hi[:, k, :], start=False, stop=k == KT - 1)
        mm.then_inc(dtp, 1)
        pe.wait_ge(dtc, 1)
        for j in range(TT):
            mm = nc.tensor.transpose(bank[6][:, j * 2 * SH:(j + 1) * 2 * SH], dt_ch[0:2 * SH, j * P:(j + 1) * P],
                                     cst[0:2 * SH, 0, 0:2 * SH])
        mm.then_inc(dtp, 1)

    def dt_act(act):
        act.wait_ge(dt_v, 1)
        nc.scalar.activation(dtmp[:, 1, :], dtmp[:, 0, :], ACT.Exp).then_inc(dt_a, 1)
        nc.scalar.activation(aneg[:, :], par[:, PCOL["a_log"]:PCOL["a_log"] + 2 * SH], ACT.Exp).then_inc(dt_a, 1)
        act.wait_ge(dt_v, 2)
        nc.scalar.activation(dtmp[:, 3, :], dtmp[:, 2, :], ACT.Ln).then_inc(dt_a, 1)

    def dt_dve(dve):
        dve.wait_ge(dtp, 1)
        nc.vector.tensor_copy(dt_ch[0:2 * SH, :], bank[5][0:2 * SH, :]).then_inc(dtc, 1)
        dve.wait_ge(dtp, 2)
        v = dtv[:, :, :, :].rearrange("p j d h -> p (j d h)")
        bias = par[:, PCOL["dt_bias"]:PCOL["dt_bias"] + 2 * SH].unsqueeze(1).to_broadcast([P, TT, 2 * SH])
        link("dve", dve, nc.vector.tensor_tensor(v.rearrange("p (j n) -> p j n", j=TT),
                                                 bank[6][:, 0:TT * 2 * SH].rearrange("p (j n) -> p j n", j=TT), bias, ALU.add))
        nc.vector.tensor_scalar(dtmp[:, 0, :], v, 30.0, None, ALU.min).then_inc(dt_v, 1)
        dve.wait_ge(dt_a, 2)
        nc.vector.tensor_scalar(dtmp[:, 2, :], dtmp[:, 1, :], 1.0, None, ALU.add).then_inc(dt_v, 1)
        dve.wait_ge(dt_a, 3)
        log1p_fix(dve, dtmp[:, 1, :], dtmp[:, 2, :], dtmp[:, 3, :], dtmp[:, 0, :])
        link("dve", dve, nc.vector.tensor_tensor(v, v, dtmp[:, 3, :], ALU.max))
        link("dve", dve, nc.vector.tensor_scalar(dtmp[:, 0, :], v, -1.0, None, ALU.mult))
        nc.vector.tensor_tensor(da[:, :, :, :].rearrange("p j d h -> p j (d h)"), dtmp[:, 0, :].rearrange("p (j n) -> p j n", j=TT),
                                aneg[:, :].unsqueeze(1).to_broadcast([P, TT, 2 * SH]), ALU.mult).then_inc(dt_ok, 1)

    def cum_pe(pe):
        pe.wait_ge(dt_ok, 1)
        pe.wait_ge(tri_load, 16)
        for half, (mf, mb) in enumerate((("gt", "lt"), ("le", "ge"))):
            out = bank[6][:, 256 * half:256 * (half + 1)].rearrange("p (c d h) -> p c d h", c=TT, d=2)
            nc.tensor.matmul(out[:, :, 0, :], M[mf], da[:, :, 0, :], start=True, stop=True)
            nc.tensor.matmul(out[:, :, 1, :], M[mb], da[:, :, 1, :], start=True, stop=True)
        nc.tensor.matmul(bank[7][:, 0:256], C["ones"], da[:, :, :, :].rearrange("p c d h -> p (c d h)"), start=True, stop=True).then_inc(cump, 1)

    def cum_act(act):
        act.wait_ge(cump, 1)
        for dst, src in ((dtt, bank[6][:, 0:256]), (cume, bank[6][:, 256:512]), (tote, bank[7][:, 0:256])):
            nc.scalar.activation(dst[:, :, :, :].rearrange("p c d h -> p (c d h)"), src, ACT.Exp).then_inc(cum_x, 1)

    def ssd_pe(pe):
        pe.wait_ge(cum_x, 3)

        def pairs(g, c):
            if c:
                pe.wait_ge(gl_done, TT * g + c)
            else:
                pe.wait_ge(tbc, g + 1)
            nc.tensor.matmul(bank[1][:, 0:P], chunk(B_TILE + g, c), chunk(C_TILE + g, c), start=True, stop=True).then_inc(gp, 1)

        def exponents(g, c, hf):
            q = 2 * (TT * g + c) + hf
            pe.wait_ge(rhs_done, q + 1)
            if q >= 2:
                pe.wait_ge(e_x, q - 1)
            out = bank[2 + hf][:, :]
            nc.tensor.matmul(out, M["gt"], erhs[:, hf, 0, :, :].rearrange("p h t -> p (h t)"), start=True, stop=False)
            nc.tensor.matmul(out, M["lt"], erhs[:, hf, 1, :, :].rearrange("p h t -> p (h t)"), start=False, stop=True).then_inc(xp, 1)

        def between(g, c):
            n = TT * g + c
            pe.wait_ge(comb, n) if c else pe.wait_ge(h_ready, g + 1)
            if c > 0:
                mm = nc.tensor.matmul(bank[5][:, :], chunk(C_TILE + g, c), hst[:, 0, c - 1, :], start=True, stop=True)
            if c < TT - 1:
                mm = nc.tensor.matmul(bank[6][:, :], chunk(C_TILE + g, c), hst[:, 1, c, :], start=True, stop=True)
            mm.then_inc(inter, 1)

        def inside(g, c):
            n = TT * g + c
            pe.wait_ge(mlu, 2 * n + 2)
            pe.wait_ge(v_done, n + 1)
            if n:
                pe.wait_ge(ysum, n)
            for h in range(HPG):
                out = bank[4][:, h * HD:(h + 1) * HD]
                nc.tensor.matmul(out, mw[c % 2][:, h // 4, h % 4, :], vfb[:, 0, h * HD:(h + 1) * HD], start=True, stop=False)
                mm = nc.tensor.matmul(out, ew[c % 2][:, h // 4, h % 4, :], vfb[:, 1, h * HD:(h + 1) * HD], start=False, stop=True)
            mm.then_inc(intra, 1)

        def turn_y(g, c):
            n = TT * g + c
            pe.wait_ge(ysum, n + 1)
            if n:
                pe.wait_ge(yev, n)
            for i in range(4):
                mm = nc.tensor.transpose(bank[7][:, i * P:(i + 1) * P], y_one[:, c % 2, i * P:(i + 1) * P], C["ident"])
            mm.then_inc(typ, 1)

        def turn_x(g, c):
            n = TT * g + c
            if c == 0 and g >= 2:
                pe.wait_ge(yn, 4 * (g - 1))
            if c == 1 and g:
                pe.wait_ge(yev, TT * g)
            if c >= 2:
                pe.wait_ge(vt_done, n - 1)
            for i in range(4):
                mm = nc.tensor.transpose(tbank(c)[:, i * P:(i + 1) * P], chunk(4 * g + i, c), C["ident"])
            mm.then_inc(txp, 1)

        def states(g, c):
            n = TT * g + c
            pe.wait_ge(vt_done, n + 1)
            if c == 0 and g:
                pe.wait_ge(comb, n)
            if c:
                pe.wait_ge(hub, n)
            if c == 2:
                pe.wait_ge(hu, 2 * g + 1)
            if c < TT - 1:
                mm = nc.tensor.matmul(bank[5][:, :], btok[:, c, :], vtl[c % 2][:, 0, :], start=True, stop=True)
            if c > 0:
                mm = nc.tensor.matmul(bank[6][:, :], btok[:, c, :], vtl[c % 2][:, 1, :], start=True, stop=True)
            mm.then_inc(stp, 1)

        def norm_sums(g, tiles):
            for i in tiles:
                pe.wait_ge(ysq, 4 * g + i + 1)
                nc.tensor.matmul(nbank(g)[:, :], C["ones"], sq_c[g][i % 2][:, :], start=i == 0, stop=i == 3).then_inc(ysqu, 1)

        def begin(g):
            if g:
                pe.wait_ge(gl_done, TT * g)
            for c in range(TT):
                mm = nc.tensor.transpose(bank[1][:, c * P:(c + 1) * P], chunk(B_TILE + g, c), C["ident"])
            mm.then_inc(tbp, 1)
            turn_x(g, 0)

        begin(0)
        for g in range(SG):
            turn_x(g, 1)
            pairs(g, 0)
            exponents(g, 0, 0)
            for c in range(TT):
                if c + 2 < TT:
                    turn_x(g, c + 2)
                states(g, c)
                if c == 0:
                    exponents(g, 0, 1)
            for c in range(TT):
                if c + 1 < TT:
                    pairs(g, c + 1)
                    exponents(g, c + 1, 0)
                    exponents(g, c + 1, 1)
                between(g, c)
                if c == 1 and g:
                    norm_sums(g - 1, (0, 1))
                inside(g, c)
                if c == 1 and g:
                    norm_sums(g - 1, (2, 3))
                if c:
                    turn_y(g, c - 1)
            if g + 1 < SG:
                begin(g + 1)
            turn_y(g, TT - 1)
        norm_sums(SG - 1, range(4))

    def ssd_act(act):
        def token_major(g, c):
            n = TT * g + c
            act.wait_ge(txp, n + 1)
            if g and c == 0:
                act.wait_ge(v_done, TT * g)
            nc.scalar.activation(xtok[:, c, :], tbank(c)[:, :], ACT.Copy).then_inc(xtc, 1)

        def squares(g):
            for i in range(4):
                k = 4 * g + i
                act.wait_ge(gated, k + 1)
                if i >= 2:
                    act.wait_ge(ysqu, k - 1)
                nc.scalar.activation(sq_c[g][i % 2][:, :], xbc[:, k, :], ACT.Square).then_inc(ysq, 1)

        def roots(g):
            act.wait_ge(ysqu, 4 * (g + 1))
            nc.scalar.activation(nrm_c[g][:, 0, :], nbank(g)[:, :], ACT.Ln, scale=1.0 / GW, bias=eps_col[:, :]).then_inc(yln, 1)
            act.wait_ge(yln, 2 * g + 1)
            nc.scalar.activation(nrm_c[g][:, 1, :], nrm_c[g][:, 0, :], ACT.Exp, scale=-0.5).then_inc(yln, 1)

        def decays(g, c, hf):
            n = TT * g + c
            act.wait_ge(xp, 2 * n + hf + 1)
            if n >= 2 and hf == 0:
                act.wait_ge(intra, n - 1)
            nc.scalar.activation(ew[c % 2][:, hf, :, :].rearrange("p h t -> p (h t)"), bank[2 + hf][:, :], ACT.Exp).then_inc(e_x, 1)

        def high(g):
            act.wait_ge(yn, 4 * (g + 1))
            for i in range(4):
                k = 4 * g + i
                nc.scalar.activation(y_hi[:, k, :], xbc[:, k, :], ACT.Copy).then_inc(yhi, 1)

        for g in range(SG):
            act.wait_ge(tbp, g + 1)
            if g:
                act.wait_ge(stp, TT * g)
            nc.scalar.activation(btok[:, :, :].rearrange("p c n -> p (c n)"), bank[1][:, :], ACT.Copy).then_inc(tbc, 1)
            token_major(g, 0)
            token_major(g, 1)
            for c in range(TT):
                n = TT * g + c
                if c + 2 < TT:
                    token_major(g, c + 2)
                act.wait_ge(stp, n + 1)
                if c == 0:
                    if g:
                        act.wait_ge(inter, n)
                    nc.scalar.activation(hst[:, 0, 0, :], bank[5][:, :], ACT.Copy).then_inc(hub, 1)
                else:
                    nc.scalar.activation(hst[:, 1, c - 1, :], bank[6][:, :], ACT.Copy).then_inc(hub, 1)
                if c < 2:
                    decays(g, 0, c)
            for c in range(TT):
                if c:
                    decays(g, c, 0)
                    decays(g, c, 1)
                if c == 1 and g:
                    squares(g - 1)
                if c == 2 and g:
                    roots(g - 1)
                if c == 3 and g:
                    high(g - 1)
        squares(SG - 1)
        roots(SG - 1)
        high(SG - 1)

    def low(ops, eng, g):
        for i in range(4):
            k = 4 * g + i
            eng.wait_ge(yhi, k + 1)
            ops.tensor_tensor(y_lo[:, k, :], xbc[:, k, :], y_hi[:, k, :].bitcast(F32), ALU.subtract).then_inc(ylo, 1)

    def ssd_pool(pool):
        pool.wait_ge(dt_ok, 1)
        pool.wait_ge(tri_load, 16)
        pool.wait_ge(dt_fin, 1)

        def operands(g, c):
            for hf in range(2):
                q = 2 * (TT * g + c) + hf
                if q >= 2:
                    pool.wait_ge(xp, q - 1)
                for d, m in enumerate(("le", "ge")):
                    h0 = HPG * g + 4 * hf
                    t = nc.gpsimd.tensor_tensor(erhs[:, hf, d, :, :], M[m].unsqueeze(1).to_broadcast([P, 4, P]),
                                                da[:, c, d, h0:h0 + 4].unsqueeze(2).to_broadcast([P, 4, P]), ALU.mult)
                t.then_inc(rhs_done, 1)

        def stepped(g, c):
            n = TT * g + c
            pool.wait_ge(xtc, n + 1)
            if n:
                pool.wait_ge(intra, n)
            for d in range(2):
                t = nc.gpsimd.tensor_tensor(wide(vfb[:, d, :]), wide(xtok[:, c, :]), heads(dtv, c, d, g), ALU.mult)
            t.then_inc(v_done, 1)
        operands(0, 0)
        for g in range(SG):
            for c in range(TT):
                if c + 1 < TT:
                    operands(g, c + 1)
                elif g + 1 < SG:
                    operands(g + 1, 0)
                stepped(g, c)
            if g:
                low(nc.gpsimd, pool, g - 1)
            pool.wait_ge(yev, TT * (g + 1))
            for i in range(4):
                k = 4 * g + i
                nc.gpsimd.tensor_tensor(xbc[:, k, :], xbc[:, k, :], zt[:, k, :], ALU.mult).then_inc(gated, 1)

    def ssd_dve(dve):
        dve.wait_ge(cum_x, 3)
        nc.vector.tensor_tensor(dtt[:, :, :, :].rearrange("p c d h -> p (c d h)"), dtt[:, :, :, :].rearrange("p c d h -> p (c d h)"),
                                dtv[:, :, :, :].rearrange("p c d h -> p (c d h)"), ALU.mult).then_inc(dt_fin, 1)
        dve.wait_ge(dt_fin, 1)

        def grow(state, d, c, g):
            return nc.vector.tensor_tensor(wide(htmp[:, :]), wide(hst[:, d, state, :]), heads(tote, c, d, g), ALU.mult)

        def tailed(g, c):
            n = TT * g + c
            dve.wait_ge(xtc, n + 1)
            if n >= 2:
                dve.wait_ge(stp, n - 1)
            for d in range(2):
                t = nc.vector.tensor_tensor(wide(vtl[c % 2][:, d, :]), wide(tbank(c)[:, :]), heads(dtt, c, d, g), ALU.mult)
            t.then_inc(vt_done, 1)

        def roots(g):
            dve.wait_ge(yln, 2 * g + 2)
            halve(dve, nbank(g)[:, :], 1.0 / GW, nrm_c[g][:, 2, :])
            refine(dve, nrm_c[g][:, 1, :], nrm_c[g][:, 2, :], nrm_c[g][:, 0, :])
            for i in range(4):
                k = 4 * g + i
                nc.vector.scalar_tensor_tensor(out=xbc[:, k, :], in0=xbc[:, k, :], scalar=pcol("ssd_g", k), in1=nrm_c[g][:, 1, :],
                                               op0=ALU.mult, op1=ALU.mult).then_inc(yn, 1)

        def masked(g, c):
            n = TT * g + c
            dve.wait_ge(gp, n + 1)
            gm = gmask[:, c % 2, :, :]
            nc.vector.tensor_tensor(gm[:, 0, :], bank[1][:, 0:P], M["le"], ALU.mult)
            nc.vector.tensor_tensor(gm[:, 1, :], bank[1][:, 0:P], M["gt"], ALU.mult).then_inc(gl_done, 1)
            dve.wait_ge(gl_done, n + 1)
            for hf in range(2):
                dve.wait_ge(e_x, 2 * n + hf + 1)
                link("dve", dve, nc.vector.tensor_tensor(mw[c % 2][:, hf, :, :], ew[c % 2][:, hf, :, :],
                                                         gm[:, 0:1, :].to_broadcast([P, 4, P]), ALU.mult))
                nc.vector.tensor_tensor(ew[c % 2][:, hf, :, :], ew[c % 2][:, hf, :, :],
                                        gm[:, 1:2, :].to_broadcast([P, 4, P]), ALU.mult).then_inc(mlu, 1)

        def evac_y(g, c):
            dve.wait_ge(typ, TT * g + c + 1)
            for i in range(4):
                k = 4 * g + i
                t = nc.vector.scalar_tensor_tensor(out=chunk(k, c), in0=chunk(k, c), scalar=pcol("d_skip", k),
                                                   in1=bank[7][:, i * P:(i + 1) * P], op0=ALU.mult, op1=ALU.add)
            t.then_inc(yev, 1)

        for g in range(SG):
            tailed(g, 0)
            for c in range(TT):
                if c + 1 < TT:
                    tailed(g, c + 1)
                if 0 < c < TT - 1:
                    dve.wait_ge(hub, TT * g + 1)
                    if g:
                        dve.wait_ge(typ, TT * g)
                    link("dve", dve, grow(c - 1, 0, c, g))
                    dve.wait_ge(stp, TT * g + c + 1)
                    nc.vector.tensor_tensor(hst[:, 0, c, :], htmp[:, :], bank[5][:, :], ALU.add).then_inc(hu, 1)
                    dve.wait_ge(hu, 2 * g + c)
                if c == 2:
                    masked(g, 0)
            dve.wait_ge(hub, TT * (g + 1))
            for c in (2, 1):
                link("dve", dve, grow(c, 1, c, g))
                t = nc.vector.tensor_tensor(hst[:, 1, c - 1, :], hst[:, 1, c - 1, :], htmp[:, :], ALU.add)
                if c == 2:
                    link("dve", dve, t)
            t.then_inc(h_ready, 1)
            for c in range(TT):
                n = TT * g + c
                if c + 1 < TT:
                    masked(g, c + 1)
                dve.wait_ge(inter, n + 1)
                if c >= 2:
                    dve.wait_ge(typ, n - 1)
                y1, y2 = y_one[:, c % 2, :], y_two[:, c % 2, :]
                if c > 0:
                    t = nc.vector.tensor_tensor(wide(y1), wide(bank[5][:, :]), heads(cume, c, 0, g), ALU.mult)
                if c < TT - 1:
                    t = nc.vector.tensor_tensor(wide(y2 if c else y1), wide(bank[6][:, :]), heads(cume, c, 1, g), ALU.mult)
                t.then_inc(comb, 1)
                dve.wait_ge(comb, n + 1)
                if 0 < c < TT - 1:
                    link("dve", dve, nc.vector.tensor_tensor(y1, y1, y2, ALU.add))
                dve.wait_ge(intra, n + 1)
                nc.vector.tensor_tensor(y1, y1, bank[4][:, :], ALU.add).then_inc(ysum, 1)
                if c:
                    evac_y(g, c - 1)
                if c == 2 and g:
                    roots(g - 1)
            evac_y(g, TT - 1)
        roots(SG - 1)
        low(nc.vector, dve, SG - 1)

    dt_fin, hub = sem("dt_fin"), sem("hub")

    def tile_of(buf, i, j):
        return buf[:, 4 * i + j, :] if isinstance(i, int) else buf[:, bass.ds(4 * i + j, 1), :].rearrange("p a t -> p (a t)")

    def z_take(i, j, done):
        act_.wait_ge(slot_done, done)
        nc.scalar.activation(tile_of(zt, i, j), bank[j][:, :], ACT.Silu).then_inc(evac[j], 1)

    def xbc_act(i, j, done):
        def silu(jj):
            act_.wait_ge(evac[jj], i + PLAN["xbc"]["tile0"] // 4 + 1)
            nc.scalar.activation(tile_of(xbc, i, jj), cv[:, jj, :], ACT.Silu).then_inc(xsilu, 1)
        act_.wait_ge(slot_done, done)
        nc.scalar.activation(cv[:, j, :], bank[j][:, :], ACT.Identity, scale=col("conv_w", 5, i, j, 2),
                             bias=col("conv_b", 1, i, j)).then_inc(xmid, 1)
        if j:
            silu(j - 1)
        if j == 3:
            silu(3)

    def xbc_dve(i, j, done):
        dve_.wait_ge(xmid, 4 * i + j + 1)
        for n, (tap, by) in enumerate(((0, -2), (1, -1), (3, 1), (4, 2))):
            a, b = max(0, -by), S - max(0, by)
            dst = cv[:, j, a:b]
            if n:
                dve_.wait_ge(xtap, 12 * i + 3 * j + n)
            nc.vector.scalar_tensor_tensor(out=dst, in0=bank[j][:, a + by:b + by], scalar=col("conv_w", 5, i, j, tap), in1=dst,
                                           op0=ALU.mult, op1=ALU.add).then_inc(evac[j] if n == 3 else xtap, 1)

    @block.sync
    def _(sp_):
        sp_.dma_start(memx[:, :, :], dr["memT"]).then_inc(mem_load, 16)
        for name, _, _ in WEIGHTS:
            load_weights(sp_, name)
        for k in range(KT):
            updated(sp_, X_UPDATES - 1, k)
            sp_.dma_start(dr["out"][:, k, :], x[:, k, :]).then_inc(out_done, 16)
        sp_.wait_ge(out_done, 16 * KT)

    @block.gpsimd
    def _(pool):
        nc.gpsimd.memset(eps_col[:, :], EPS).then_inc(eps_done, 1)
        nc.gpsimd.engine_nop().then_inc(prod, 2)
        nc.gpsimd.engine_nop().then_inc(psq_used, 2)
        low_pool(pool, 0, MEM, mem_hi, mem_lo)
        low_pool(pool, 1, S, a_hi, a_lo)
        pool_pool(pool)
        stick_pool(pool)
        sums_pool(pool, 0, sq, nrm[:, 0, :])
        low_pool(pool, 2, S, a_hi, a_lo)
        ret_pool(pool)
        ret_gate_pool(pool)
        na_pool(pool)
        sums_pool(pool, 1, sq, nrm[:, 0, :])
        post_norm_pool(pool, 0, m_mix)
        low_pool(pool, 3, S, a_hi, a_lo)
        up_pool(pool, 0)
        sums_pool(pool, 2, sq_b, nrm_b[:, 0, :])
        post_norm_pool(pool, 1, m_ffn)
        low_pool(pool, 4, S, a_hi, a_lo)
        ssd_pool(pool)
        sums_pool(pool, 3, sq_b, nrm_b[:, 0, :])
        post_norm_pool(pool, 2, m_ssd)
        low_pool(pool, 5, S, a_hi, a_lo)
        up_pool(pool, 1)
        sums_pool(pool, 4, sq_b, nrm_b[:, 0, :])
        post_norm_pool(pool, 3, m_ffn)

    @block.scalar
    def _(act):
        act.dma_start(cst[:, :, :], dr["consts"]).then_inc(cst_load, 16)
        act.dma_start(par[:, :], dr["params"]).then_inc(par_load, 16)
        act.dma_start(x[:, :, :], dr["xT"]).then_inc(x_load, 16)
        act.wait_ge(eps_done, 1)
        for s in range(2):
            act.wait_ge(w_load[s], 16)
            nc.scalar.activation(w_hi[:, s, :], raw[:, s, :], ACT.Copy).then_inc(hi_done, 1)
        nc.scalar.preload_act_table_set(LOGEXP)
        act.wait_ge(mem_load, 16)
        norm_act(act, 0, 0, memx, MEM)
        for q in range(2):
            split_hi(act, "mem_kv", 0, q)
        norm_act(act, 1, 1, x, S, ready=lambda k: act.wait_ge(x_load, 16) if k == 0 else None, nrm=nrm_x, b=5,
                 beside=lambda k: high_act(act, 0, MEM, mem_hi, (k,)))
        high_act(act, 1, S, a_hi)

        def take_kv(i, j, done):
            act.wait_ge(slot_done, done)
            nc.scalar.activation(kv[:, j, :], bank[j][:, 0:MEM], ACT.Copy).then_inc(evac[j], 1)
        product_split(act, "mem_kv", split_hi, take_kv, 2)
        act.wait_ge(slot_done, PLAN["in1"]["slot0"])
        act.dma_start(invc[:, :, :], dr["inv_count"]).then_inc(poolc_load, 16)

        def take_p1(i, j, done):
            if j % 2 == 0:
                act.wait_ge(slot_done, done)
                dst = p1[:, 4 * i + j, :] if isinstance(i, int) else p1[:, bass.ds(4 * i + j, 1), :].rearrange("p a t -> p (a t)")
                nc.scalar.activation(dst, bank[j][:, :], ACT.Copy).then_inc(evac[j], 1)
        product_split(act, "in1", split_hi, take_p1)
        act.wait_ge(evac[1], PLAN["out1"]["tile0"] // 4)
        act.wait_ge(evac[3], PLAN["out1"]["tile0"] // 4)
        act.wait_ge(sem("poolw_zero"), 1)
        for t in range(2):
            for g in range(2):
                act.dma_start(poolw[g * DH:(g + 1) * DH, t, g * DH:(g + 1) * DH], dr["pool_w"][2 * t + g]).then_inc(sem("poolw_load"), 16)
        for n, (src, t, w, g, o) in enumerate(NORMS):
            nc.scalar.activation(msq[:, n, 0:w], src[:, t, :], ACT.Square).then_inc(msq_done, 1)
        for t in (POOL_G, POOL_G + 1, SB_G, SB_G + 1, SB_G + 2, SB_G + 3, MEM_G, MEM_G + 1):
            nc.scalar.activation(p1[:, t, :], p1[:, t, :], ACT.Silu).then_inc(silu_done, 1)
        nc.scalar.preload_act_table_set(LOGEXP)
        mem_norm_act(act)
        stick_act(act)
        mem_act(act)
        split_mix_act(act)

        def square_x(i, j, done):
            act.wait_ge(evac[j], i + (PLAN["out1"]["tile0"] // 4 + 1))
            square_act(0, sq, i, j, tile_of(x, i, j))
        product_split(act, "out1", split_hi, square_x)
        sums_act(act, 2, 0, nrm)
        high_act(act, 2, S, a_hi)
        act.dma_start(rope[:, :, :], dr["rope"]).then_inc(tab_load, 16)
        act.dma_start(dist[:, :], dr["dist"]).then_inc(dist_load, 16)
        product_split(act, "in2", split_hi, copy_tiles(p2, 0))
        for j in (1, 3):
            act.wait_ge(evac[j], PLAN["out2"]["tile0"] // 4)
        for t in range(4):
            nc.scalar.activation(p2[:, RET_G + t, :], p2[:, RET_G + t, :], ACT.Silu).then_inc(silu_done, 1)
        nc.scalar.preload_act_table_set(LOGEXP)
        ret_act(act)
        na_act(act)
        split_mix2_act(act)
        product_split(act, "out2", split_hi, out_act(1, sq))
        sums_act(act, 3, 1, nrm)
        norm_act(act, 4, 2, x, S, lambda k: updated(act, 0, k))
        high_act(act, 3, S, a_hi)
        nc.scalar.preload_act_table(ACT.Gelu_apprx_tanh)
        product_split(act, "up0", split_hi, up_act(0))
        nc.scalar.preload_act_table_set(LOGEXP)
        product_split(act, "down0", split_hi, out_act(2, sq_b))
        sums_act(act, 5, 2, nrm_b)
        norm_act(act, 6, 3, x, S, lambda k: updated(act, 1, k))
        high_act(act, 4, S, a_hi)
        act.dma_start(tri[:, :, :], dr["tri"]).then_inc(tri_load, 16)
        act.dma_start(wdt[:, :, :], dr["w_dt"]).then_inc(dtw_load, 16)
        act.wait_ge(dtw_load, 16)
        nc.scalar.activation(wdt_hi[:, :, :], wdt[:, :, :], ACT.Copy).then_inc(dtw_hi, 1)
        nc.scalar.preload_act_table(ACT.Silu)
        product_split(act, "z", split_hi, z_take)
        nc.scalar.preload_act_table_set(LOGEXP)
        dt_act(act)
        nc.scalar.preload_act_table(ACT.Silu)
        act.wait_ge(dt_ok, 1)
        product_split(act, "xbc", split_hi, xbc_act)
        nc.scalar.preload_act_table_set(LOGEXP)
        cum_act(act)
        ssd_act(act)
        product_split(act, "out3", split_hi, out_act(3, sq_b))
        sums_act(act, 7, 3, nrm_b)
        norm_act(act, 8, 4, x, S, lambda k: updated(act, 2, k))
        high_act(act, 5, S, a_hi)
        nc.scalar.preload_act_table(ACT.Gelu_apprx_tanh)
        product_split(act, "up1", split_hi, up_act(1))
        nc.scalar.preload_act_table_set(LOGEXP)
        product_split(act, "down1", split_hi, out_act(4, sq_b))
        sums_act(act, 9, 4, nrm_b)

    @block.vector
    def _(dve):
        for s in range(2):
            dve.wait_ge(hi_done, s + 1)
            nc.vector.tensor_tensor(w_lo[:, s, :], raw[:, s, :], w_hi[:, s, :].bitcast(F32), ALU.subtract).then_inc(lo_done, 1)
        dve.wait_ge(par_load, 16)
        pre_norm_dve(dve, 0, 0, memx, MEM, "mem_norm_g", mem_hi, mem_lo)
        for q in range(2):
            split_lo(dve, "mem_kv", 0, q)
        pre_norm_dve(dve, 1, 1, x, S, "norm_g", a_hi, a_lo, nrm_x, 5)
        product_split(dve, "mem_kv", split_lo, lambda i, j, done: None, 2)

        def take_p1(i, j, done):
            if j % 2 == 1:
                dve.wait_ge(slot_done, done)
                dst = p1[:, 4 * i + j, :] if isinstance(i, int) else p1[:, bass.ds(4 * i + j, 1), :].rearrange("p a t -> p (a t)")
                nc.vector.tensor_copy(dst, bank[j][:, :]).then_inc(evac[j], 1)
        product_split(dve, "in1", split_lo, take_p1)
        dve.wait_ge(evac[0], PLAN["out1"]["tile0"] // 4)
        dve.wait_ge(evac[2], PLAN["out1"]["tile0"] // 4)
        for t in range(4):
            nc.vector.tensor_scalar(p1[:, SB_Q + t, :], p1[:, SB_Q + t, :], DH ** -0.5, None, ALU.mult).then_inc(q_scaled, 1)
        mem_half_dve(dve)
        pool_dve(dve)
        dve.wait_ge(silu_done, 8)
        stick_dve(dve)
        mem_dve(dve)
        split_mix_dve(dve)

        def add_x(i, j, done):
            dve.wait_ge(slot_done, done)
            nc.vector.tensor_tensor(x[:, 4 * i + j, :], x[:, 4 * i + j, :], bank[j][:, :], ALU.add).then_inc(evac[j], 1)
        product_split(dve, "out1", split_lo, add_x)
        pre_norm_dve(dve, 2, 2, x, S, "mix_pre0", a_hi, a_lo)
        product_split(dve, "in2", split_lo, copy_tiles(p2, 1))
        dve.wait_ge(silu_done, 12)
        ret_dve(dve)
        na_dve(dve)
        split_mix2_dve(dve)
        product_split(dve, "out2", split_lo, out_dve(1, m_mix))
        post_norm_dve(dve, 3, 0, m_mix, "mix_post0")
        pre_norm_dve(dve, 4, 3, x, S, "ffn_pre0", a_hi, a_lo)
        nc.vector.engine_nop().then_inc(glo, 2)
        product_split(dve, "up0", split_lo, up_dve(0))
        product_split(dve, "down0", split_lo, out_dve(2, m_ffn))
        post_norm_dve(dve, 5, 1, m_ffn, "ffn_post0", nrm_b)
        pre_norm_dve(dve, 6, 4, x, S, "mix_pre1", a_hi, a_lo)
        dve.wait_ge(dtw_hi, 1)
        nc.vector.tensor_tensor(wdt_lo[:, :, :], wdt[:, :, :], wdt_hi[:, :, :].bitcast(F32), ALU.subtract).then_inc(dtw_lo, 1)
        product_split(dve, "z", split_lo, lambda i, j, done: None)
        dt_dve(dve)
        product_split(dve, "xbc", split_lo, xbc_dve)
        ssd_dve(dve)
        product_split(dve, "out3", split_lo, out_dve(3, m_ssd))
        post_norm_dve(dve, 7, 2, m_ssd, "mix_post1", nrm_b)
        pre_norm_dve(dve, 8, 5, x, S, "ffn_pre1", a_hi, a_lo)
        product_split(dve, "up1", split_lo, up_dve(1))
        product_split(dve, "down1", split_lo, out_dve(4, m_ffn))
        post_norm_dve(dve, 9, 3, m_ffn, "ffn_post1", nrm_b)

    @block.tensor
    def _(pe):
        pe.wait_ge(cst_load, 16)
        norm_pe(pe, 0, MEM)
        norm_pe(pe, 1, S, 5)
        product_pe(pe, "mem_kv", mem_hi, mem_lo, MEM, ready=lambda k: split_done(pe, 0, k))
        product_pe(pe, "in1", a_hi, a_lo, ready=lambda k: split_done(pe, 1, k))
        for b in range(4):
            pe.wait_ge(evac[b], PLAN["out1"]["tile0"] // 4)
        mem_norm_pe(pe)
        pool_pe(pe)
        pe.wait_ge(pool_y, 2)
        stick_pe(pe)
        mem_pe(pe)
        pe.wait_ge(my_read, MEM_HEADS)
        product_pe(pe, "out1", a_hi, a_lo, ready=lambda k: pe.wait_ge(mixlo, k + 1))
        sums_pe(pe, 0, sq, nrm[:, 0, :])
        product_pe(pe, "in2", a_hi, a_lo, ready=lambda k: split_done(pe, 2, k))
        for b in range(4):
            pe.wait_ge(evac[b], PLAN["out2"]["tile0"] // 4)
        ret_pe(pe)
        na_pe(pe)
        product_pe(pe, "out2", a_hi, a_lo, ready=lambda k: pe.wait_ge(mixlo, KT + k + 1))
        sums_pe(pe, 1, sq, nrm[:, 0, :])
        norm_pe(pe, 2, S)
        product_pe(pe, "up0", a_hi, a_lo, ready=lambda k: split_done(pe, 3, k))
        product_pe(pe, "down0", g_hi, g_lo, ready=lambda k: pe.wait_ge(glo, k + 3))
        sums_pe(pe, 2, sq_b, nrm_b[:, 0, :])
        norm_pe(pe, 3, S)
        product_pe(pe, "z", a_hi, a_lo, ready=lambda k: split_done(pe, 4, k))
        dt_pe(pe)
        product_pe(pe, "xbc", a_hi, a_lo)
        for b in range(4):
            pe.wait_ge(evac[b], PLAN["out3"]["tile0"] // 4)
        cum_pe(pe)
        pe.wait_ge(xsilu, 24)
        ssd_pe(pe)
        product_pe(pe, "out3", y_hi, y_lo, ready=lambda k: pe.wait_ge(ylo, k + 1))
        sums_pe(pe, 3, sq_b, nrm_b[:, 0, :])
        norm_pe(pe, 4, S)
        product_pe(pe, "up1", a_hi, a_lo, ready=lambda k: split_done(pe, 5, k))
        product_pe(pe, "down1", g_hi, g_lo, ready=lambda k: pe.wait_ge(glo, FT + k + 3))
        sums_pe(pe, 4, sq_b, nrm_b[:, 0, :])


def blocks(w):
    k, n = w.shape
    return np.ascontiguousarray(w.reshape(k // P, P, n // P, P).transpose(2, 1, 0, 3).reshape(n // P, P, k))


def features(v):
    return np.ascontiguousarray(v.reshape(-1, P).T)


def rotation_tables():
    half = DH // 2
    inv = (1.0 / (np.float32(10000.0) ** (np.arange(half, dtype=np.float32) / np.float32(half)))).astype(np.float32)
    ang = np.arange(S, dtype=np.float32)[None, :] * inv[np.arange(P) % half][:, None]
    return np.ascontiguousarray(np.stack([np.cos(ang), np.sin(ang)], 1).astype(np.float32))


def swap_matrix():
    m = np.zeros((P, P), np.float32)
    for j in range(P):
        if j % DH < DH // 2:
            m[j + DH // 2, j] = -1
        else:
            m[j - DH // 2, j] = 1
    return m


def distances():
    return (np.arange(STRIP)[None, :] - (S - P) - np.arange(P)[:, None]).astype(np.float32)


def column_mask():
    out = np.full((P, 4, KEYW), NEG, np.float32)
    for c in range(4):
        first = min(max(QB * c - WIN_C // 2, 0), GRID_W - KEYW)
        for p in range(P):
            q = QB * c + p % QB
            a = min(max(q - WIN_C // 2, 0), GRID_W - WIN_C) - first
            out[p, c, a:a + WIN_C] = 0
    return out


def interleave(a):
    k = a.shape[:-1]
    return np.ascontiguousarray(a.reshape(*k, 2, FT, P).swapaxes(-3, -2).reshape(*k, 2 * FFN))


def taps(w):
    return np.ascontiguousarray(w.reshape(w.shape[0], -1, P).transpose(2, 1, 0).reshape(P, -1))


def constants():
    i = np.arange(P)
    c = {
        "ident": np.eye(P), "ones": np.ones((P, P)), "ones64": (i[:, None] // DH == i[None, :] // DH),
        "neg_tri": -(i[:, None] >= i[None, :]).astype(np.float32), "neg_ones": -np.ones((P, P)),
        "swap": swap_matrix(),
    }
    return np.ascontiguousarray(np.stack([c[n].astype(np.float32) for n in CONSTS], 1))


def triangles():
    r, c = np.arange(P)[:, None], np.arange(P)[None, :]
    return np.ascontiguousarray(np.stack([r > c, r < c, r <= c, r >= c], 1).astype(np.float32))


def inv_count():
    out = np.zeros((P, 2, S), np.float32)
    t = np.arange(S)
    for g, w in enumerate((2, 4, 8, 16)):
        out[(g % 2) * DH:(g % 2 + 1) * DH, g // 2] = 1.0 / np.minimum(t + 1, w)
    return out


def kernel(**inp):
    import concourse.bacc as bacc
    from concourse.bass_utils import run_bass_kernel_spmd

    a = {k: np.asarray(v) for k, v in inp.items()}
    par = {
        "norm_g": features(a["norm_g"][0]), "mem_norm_g": features(a["mem_norm_g"][0]),
        "pool_scale": features(a["pool_scale"][0]),
        "q_norm_g": np.concatenate([a["q_norm_g"][0]] * 2)[:, None], "k_norm_g": np.concatenate([a["k_norm_g"][0]] * 2)[:, None],
    }
    for l in range(2):
        for n in ("mix_pre", "mix_post", "ffn_pre", "ffn_post"):
            par[f"{n}{l}"] = features(a[f"norm_{n}_2"][l])
        par[f"ffn_w{l}"] = taps(interleave(a["ffn_conv_w_2"][l]))
        par[f"ffn_b{l}"] = features(interleave(a["ffn_conv_b_2"][l]))
    par["conv_w"], par["conv_b"] = taps(a["c_conv_w_2"][0]), features(a["c_conv_b_2"][0])
    par["d_skip"] = features(np.repeat(a["c_d_skip_2"][0], HD))
    par["ssd_g"] = features(a["c_norm_g_2"][0])
    par["dt_bias"] = np.broadcast_to(a["c_dt_bias_2"][0].reshape(1, -1), (P, 2 * SH))
    par["a_log"] = np.broadcast_to(a["c_a_log_2"][0].reshape(1, -1), (P, 2 * SH))
    w_in3, inner = a["c_w_in_2"][0], SH * HD
    conv = inner + 2 * SG * NS
    par["ret_gn_g"] = features(a["ab_ret_gn_g_2"][0])
    par["decay"] = np.broadcast_to(a["ab_ret_decay_logit_2"][0].reshape(1, 16), (P, 16))
    rpb = np.zeros((NH, 2 * ROWS - 1, RPB_W), np.float32)
    rpb[:, :, WIN_C:WIN_C + 2 * WIN_C - 1] = a["ab_na_rpb_2"][0]
    rpb = np.stack([[rpb[h].reshape(-1)[(ROWS - 1 - r) * RPB_W + QB - 1 - q:][:BIAS_RUN] for r in range(ROWS) for q in range(QB)]
                    for h in range(NH)])
    arrays = {
        "rope": rotation_tables(), "dist": distances(), "col_mask": column_mask(), "rpb": rpb,
        "w_in2": blocks(a["ab_w_in_2"][0]), "w_out2": blocks(a["ab_w_out_2"][0]),
        "w_z": blocks(w_in3[:, :inner]), "w_xbc": blocks(w_in3[:, inner:inner + conv]),
        "w_dt": np.ascontiguousarray(w_in3[:, inner + conv:].reshape(KT, P, 2 * SH).transpose(1, 0, 2)),
        "w_out3": blocks(a["c_w_out_2"][0]), "tri": triangles(),
        "w_up1": blocks(interleave(a["ffn_w_up_2"][1])), "w_down1": blocks(a["ffn_w_down_2"][1]),
        "w_up0": blocks(interleave(a["ffn_w_up_2"][0])), "w_down0": blocks(a["ffn_w_down_2"][0]),
        "xT": np.ascontiguousarray(a["x"][0].reshape(S, KT, P).transpose(2, 1, 0)),
        "memT": np.ascontiguousarray(a["mem"][0].reshape(MEM, KT, P).transpose(2, 1, 0)),
        "consts": constants(), "inv_count": inv_count(),
        "params": np.ascontiguousarray(np.concatenate([par[n] for n, _ in PARAMS], 1)),
        "pool_w": a["pool_w"][0],
        "w_mem_kv": blocks(a["w_mem_kv"][0]), "w_in1": blocks(a["w_in"][0]), "w_out1": blocks(a["w_out"][0]),
    }
    nc = bacc.Bacc("TRN2", target_bir_lowering=False, num_devices=1)
    dr = {k: nc.dram_tensor("in_" + k, v.shape, F32, kind="ExternalInput").ap() for k, v in arrays.items()}
    dr["out"] = nc.dram_tensor("out", (P, KT, S), F32, kind="ExternalOutput").ap()
    program(nc, dr)
    r = run_bass_kernel_spmd(nc, [{"in_" + k: v for k, v in arrays.items()}], core_ids=[0])
    out = r.results[0]["out"]
    return np.ascontiguousarray(out.transpose(2, 1, 0).reshape(1, S, D))
```
